# Optimizing a Trainium2 kernel written in Bass

```python
import math
import jax
import jax.numpy as jnp
from jax import lax
import numpy as np

D_MODEL = 1024
BATCH = 1
SEQ = 256
DEPTH = 2

HEAD_DIM = 64
Q_BLOCK = 128
EPS = 1e-6
NEG = -1e30

NUM_BUCKETS = 32
MAX_DISTANCE = 128
BIAS_HEADS = 16

NSA_HEADS = 8
NSA_KV_HEADS = 2
NSA_GROUP = NSA_HEADS // NSA_KV_HEADS
CMP_BLOCK = 32
CMP_STRIDE = 16
CMP_HIDDEN = 128
SEL_BLOCK = 64
SEL_TOPN = 16
WINDOW = 512
FORCE_BONUS = 1e3

DIFF_HEADS = 4
DIFF_VDIM = 2 * HEAD_DIM

MOBA_HEADS = 16
MOBA_BLOCK = 256
MOBA_TOPK = 3
MOBA_QCHUNK = 32

D_FF = 4 * D_MODEL

NSA_Q = NSA_HEADS * HEAD_DIM
NSA_KV = NSA_KV_HEADS * HEAD_DIM
NSA_GATES = 3 * NSA_HEADS
DIFF_QK = DIFF_HEADS * 2 * HEAD_DIM
DIFF_V = DIFF_HEADS * DIFF_VDIM
D_MIX = NSA_Q + DIFF_V
EVEN_SIZES = (NSA_Q,) + (NSA_KV,) * 6 + (NSA_GATES, DIFF_QK, DIFF_QK, DIFF_V)
EVEN_PROJ = sum(EVEN_SIZES)
ODD_PROJ = 3 * MOBA_HEADS * HEAD_DIM
ODD_MIX = MOBA_HEADS * HEAD_DIM


def rms_norm(x, g):
    xf = x.astype(jnp.float32)
    y = xf * lax.rsqrt(jnp.mean(xf * xf, axis=-1, keepdims=True) + EPS)
    return (y * g.astype(jnp.float32)).astype(x.dtype)

def t5_bucket(rel):
    n = jnp.maximum(rel, 0)
    max_exact = NUM_BUCKETS // 2
    large = max_exact + (jnp.log(jnp.maximum(n, 1).astype(jnp.float32) / max_exact)
                         / math.log(MAX_DISTANCE / max_exact)
                         * (NUM_BUCKETS - max_exact)).astype(jnp.int32)
    large = jnp.minimum(large, NUM_BUCKETS - 1)
    return jnp.where(n < max_exact, n, large)

def masked_softmax(logits, mask):
    l = jnp.where(mask, logits.astype(jnp.float32), NEG)
    m = jnp.max(l, axis=-1, keepdims=True)
    p = jnp.where(mask, jnp.exp(l - m), 0.0)
    return p / jnp.maximum(jnp.sum(p, axis=-1, keepdims=True), 1e-30)

def to_heads(t, n):
    b, s, _ = t.shape
    return t.reshape(b, s, n, -1).transpose(0, 2, 1, 3)

def compress_kv(kv, pos, w1, w2):
    b, g, s, d = kv.shape
    nc = (s - CMP_BLOCK) // CMP_STRIDE + 1
    tok = jnp.arange(nc)[:, None] * CMP_STRIDE + jnp.arange(CMP_BLOCK)[None, :]
    blk = kv[:, :, tok] + pos
    hid = jax.nn.gelu(blk.reshape(b, g, nc, CMP_BLOCK * d) @ w1)
    return hid @ w2

def nsa_attention(q, kc, vc, ks, vs, kw, vw, gates, tbl_h):
    b, g, r, s, d = q.shape
    nc = kc.shape[2]
    ns = s // SEL_BLOCK
    n_sel = min(SEL_TOPN, ns)
    scale = d ** -0.5
    tbl_gr = tbl_h.reshape(g, r, NUM_BUCKETS)
    cmp_end = jnp.arange(nc) * CMP_STRIDE + CMP_BLOCK - 1
    tok = jnp.arange(nc)[:, None] * CMP_STRIDE + jnp.arange(CMP_BLOCK)[None, :]
    overlap = jax.nn.one_hot(tok // SEL_BLOCK, ns, dtype=jnp.float32).sum(axis=1) / CMP_BLOCK
    ks_blk = ks.reshape(b, g, ns, SEL_BLOCK, d)
    vs_blk = vs.reshape(b, g, ns, SEL_BLOCK, d)
    kw_pad = jnp.pad(kw, ((0, 0), (0, 0), (WINDOW, 0), (0, 0)))
    vw_pad = jnp.pad(vw, ((0, 0), (0, 0), (WINDOW, 0), (0, 0)))
    span = WINDOW + Q_BLOCK
    bi = jnp.arange(b)[:, None, None, None]
    gi = jnp.arange(g)[None, :, None, None]
    gi6 = jnp.arange(g)[None, :, None, None, None, None]
    ri6 = jnp.arange(r)[None, None, :, None, None, None]
    blk_ids = jnp.arange(ns)

    def block(j):
        q0 = j * Q_BLOCK
        t = q0 + jnp.arange(Q_BLOCK)
        qb = lax.dynamic_slice_in_dim(q, q0, Q_BLOCK, axis=3)
        gb = lax.dynamic_slice_in_dim(gates, q0, Q_BLOCK, axis=4)
        rel_c = t[:, None] - cmp_end[None, :]
        lc = jnp.einsum('bgrqd,bgcd->bgrqc', qb, kc) * scale + tbl_gr[:, :, t5_bucket(rel_c)]
        pc = masked_softmax(lc, rel_c >= 0)
        oc = jnp.einsum('bgrqc,bgcd->bgrqd', pc.astype(vc.dtype), vc)
        imp = jnp.einsum('bgrqc,cn->bgqn', pc, overlap)
        cur = t // SEL_BLOCK
        eligible = blk_ids[None, :] <= cur[:, None]
        forced = ((blk_ids[None, :] == 0) | (blk_ids[None, :] == cur[:, None])
                  | (blk_ids[None, :] == cur[:, None] - 1))
        score = jnp.where(eligible, imp + jnp.where(forced, FORCE_BONUS, 0.0), -1.0)
        _, sel = lax.top_k(score, n_sel)
        k_sel = ks_blk[bi, gi, sel]
        v_sel = vs_blk[bi, gi, sel]
        pos_s = sel[..., None] * SEL_BLOCK + jnp.arange(SEL_BLOCK)
        rel_s = t[None, None, :, None, None] - pos_s
        bias_s = tbl_gr[gi6, ri6, t5_bucket(rel_s)[:, :, None]]
        ls = jnp.einsum('bgrqd,bgqnkd->bgrqnk', qb, k_sel) * scale + bias_s
        ms = jnp.broadcast_to((rel_s >= 0)[:, :, None], ls.shape)
        ps = masked_softmax(ls.reshape(b, g, r, Q_BLOCK, -1),
                            ms.reshape(b, g, r, Q_BLOCK, -1)).reshape(ls.shape)
        o_s = jnp.einsum('bgrqnk,bgqnkd->bgrqd', ps.astype(v_sel.dtype), v_sel)
        kwb = lax.dynamic_slice_in_dim(kw_pad, q0, span, axis=2)
        vwb = lax.dynamic_slice_in_dim(vw_pad, q0, span, axis=2)
        pos_w = q0 - WINDOW + jnp.arange(span)
        rel_w = t[:, None] - pos_w[None, :]
        mask_w = (rel_w >= 0) & (rel_w < WINDOW) & (pos_w[None, :] >= 0)
        lw = jnp.einsum('bgrqd,bgkd->bgrqk', qb, kwb) * scale + tbl_gr[:, :, t5_bucket(rel_w)]
        pw = masked_softmax(lw, mask_w)
        ow = jnp.einsum('bgrqk,bgkd->bgrqd', pw.astype(vwb.dtype), vwb)
        return (gb[:, 0][..., None] * oc + gb[:, 1][..., None] * o_s
                + gb[:, 2][..., None] * ow)

    out = lax.map(block, jnp.arange(s // Q_BLOCK))
    return out.transpose(1, 0, 4, 2, 3, 5).reshape(b, s, g * r * d)

def diff_attention(q, k, v, lam, lam_init, subln_g, tbl_h):
    b, s = q.shape[:2]
    q = q.transpose(0, 3, 2, 1, 4)
    k = k.transpose(0, 3, 2, 1, 4)
    v = v.transpose(0, 2, 1, 3)
    kpos = jnp.arange(s)
    scale = HEAD_DIM ** -0.5

    def block(j):
        q0 = j * Q_BLOCK
        t = q0 + jnp.arange(Q_BLOCK)
        qb = lax.dynamic_slice_in_dim(q, q0, Q_BLOCK, axis=3)
        rel = t[:, None] - kpos[None, :]
        logits = jnp.einsum('bmhqd,bmhkd->bmhqk', qb, k) * scale + tbl_h[:, t5_bucket(rel)]
        p = masked_softmax(logits, rel >= 0)
        a = p[:, 0] - lam * p[:, 1]
        return jnp.einsum('bhqk,bhkv->bhqv', a.astype(v.dtype), v)

    out = lax.map(block, jnp.arange(s // Q_BLOCK))
    out = out.transpose(1, 0, 3, 2, 4).reshape(b, s, DIFF_HEADS, DIFF_VDIM)
    out = rms_norm(out, subln_g) * (1.0 - lam_init)
    return out.reshape(b, s, DIFF_HEADS * DIFF_VDIM)

def moba_attention(q, k, v, tbl_h):
    b, h, s, d = q.shape
    nb = -(-s // MOBA_BLOCK)
    pad = nb * MOBA_BLOCK - s
    k_pad = jnp.pad(k, ((0, 0), (0, 0), (0, pad), (0, 0)))
    v_pad = jnp.pad(v, ((0, 0), (0, 0), (0, pad), (0, 0)))
    kb = k_pad.reshape(b, h, nb, MOBA_BLOCK, d)
    vb = v_pad.reshape(b, h, nb, MOBA_BLOCK, d)
    k_mean = jnp.mean(kb.astype(jnp.float32), axis=3).astype(k.dtype)
    n_sel = min(MOBA_TOPK, nb)
    scale = d ** -0.5
    bi = jnp.arange(b)[:, None, None, None]
    hi = jnp.arange(h)[None, :, None, None]
    hi5 = jnp.arange(h)[None, :, None, None, None]
    blk_ids = jnp.arange(nb)

    def block(j):
        q0 = j * MOBA_QCHUNK
        t = q0 + jnp.arange(MOBA_QCHUNK)
        c = q0 // MOBA_BLOCK
        qb = lax.dynamic_slice_in_dim(q, q0, MOBA_QCHUNK, axis=2)
        gate = jnp.einsum('bhqd,bhnd->bhqn', qb, k_mean).astype(jnp.float32)
        past = blk_ids < c
        _, sel = lax.top_k(jnp.where(past, gate, NEG), n_sel)
        valid = sel < c
        k_sel = kb[bi, hi, sel]
        v_sel = vb[bi, hi, sel]
        pos_s = sel[..., None] * MOBA_BLOCK + jnp.arange(MOBA_BLOCK)
        bias_s = tbl_h[hi5, t5_bucket(t[None, None, :, None, None] - pos_s)]
        ls = jnp.einsum('bhqd,bhqnkd->bhqnk', qb, k_sel) * scale + bias_s
        ms = jnp.broadcast_to(valid[..., None], ls.shape)
        k_own = lax.dynamic_slice_in_dim(k_pad, c * MOBA_BLOCK, MOBA_BLOCK, axis=2)
        v_own = lax.dynamic_slice_in_dim(v_pad, c * MOBA_BLOCK, MOBA_BLOCK, axis=2)
        rel_o = t[:, None] - (c * MOBA_BLOCK + jnp.arange(MOBA_BLOCK))[None, :]
        lo = jnp.einsum('bhqd,bhkd->bhqk', qb, k_own) * scale + tbl_h[:, t5_bucket(rel_o)]
        mo = jnp.broadcast_to(rel_o >= 0, lo.shape)
        n_g = n_sel * MOBA_BLOCK
        logits = jnp.concatenate([ls.reshape(b, h, MOBA_QCHUNK, n_g), lo], axis=-1)
        mask = jnp.concatenate([ms.reshape(b, h, MOBA_QCHUNK, n_g), mo], axis=-1)
        p = masked_softmax(logits, mask)
        ps = p[..., :n_g].reshape(ls.shape).astype(v.dtype)
        po = p[..., n_g:].astype(v.dtype)
        return (jnp.einsum('bhqnk,bhqnkd->bhqd', ps, v_sel)
                + jnp.einsum('bhqk,bhkd->bhqd', po, v_own))

    out = lax.map(block, jnp.arange(s // MOBA_QCHUNK))
    return out.transpose(1, 0, 3, 2, 4).reshape(b, s, h * d)

def even_mixer(hn, w_in, w_out, pos_k, w1_k, w2_k, pos_v, w1_v, w2_v,
               lam_q1, lam_k1, lam_q2, lam_k2, subln_g, bias_table, lam_init):
    b, s, _ = hn.shape
    parts = jnp.split(hn @ w_in, np.cumsum(EVEN_SIZES)[:-1].tolist(), axis=-1)
    q, kc, vc, ks, vs, kw, vw, g, dq, dk, dv = parts
    qn = to_heads(q, NSA_HEADS).reshape(b, NSA_KV_HEADS, NSA_GROUP, s, HEAD_DIM)
    kc = compress_kv(to_heads(kc, NSA_KV_HEADS), pos_k, w1_k, w2_k)
    vc = compress_kv(to_heads(vc, NSA_KV_HEADS), pos_v, w1_v, w2_v)
    gates = jax.nn.sigmoid(g.astype(jnp.float32)).astype(hn.dtype)
    gates = gates.reshape(b, s, 3, NSA_KV_HEADS, NSA_GROUP).transpose(0, 2, 3, 4, 1)
    o_a = nsa_attention(qn, kc, vc, to_heads(ks, NSA_KV_HEADS), to_heads(vs, NSA_KV_HEADS),
                        to_heads(kw, NSA_KV_HEADS), to_heads(vw, NSA_KV_HEADS), gates,
                        bias_table[:, :NSA_HEADS].T)
    lam = (jnp.exp(jnp.sum((lam_q1 * lam_k1).astype(jnp.float32)))
           - jnp.exp(jnp.sum((lam_q2 * lam_k2).astype(jnp.float32))) + lam_init)
    o_b = diff_attention(dq.reshape(b, s, DIFF_HEADS, 2, HEAD_DIM),
                         dk.reshape(b, s, DIFF_HEADS, 2, HEAD_DIM),
                         dv.reshape(b, s, DIFF_HEADS, DIFF_VDIM), lam, lam_init, subln_g,
                         bias_table[:, NSA_HEADS:NSA_HEADS + DIFF_HEADS].T)
    return jnp.concatenate([o_a, o_b], axis=-1) @ w_out

def odd_mixer(hn, w_in, w_out, bias_table):
    q, k, v = jnp.split(hn @ w_in, 3, axis=-1)
    o = moba_attention(to_heads(q, MOBA_HEADS), to_heads(k, MOBA_HEADS),
                       to_heads(v, MOBA_HEADS), bias_table[:, :MOBA_HEADS].T)
    return o @ w_out

def sqrelu_mlp(hn, w1, w2):
    return jnp.square(jax.nn.relu(hn @ w1)) @ w2

def first_inputs(seed: int = 0) -> dict:
    key = jax.random.key(seed)
    k = jax.random.split(key, 22)
    ne = (DEPTH + 1) // 2
    no = DEPTH // 2
    f32 = jnp.float32

    def nrm(i, shape, scale):
        return jax.random.normal(k[i], shape, f32) * scale

    return {
        'x': nrm(0, (BATCH, SEQ, D_MODEL), 1.0),
        'bias_table': nrm(1, (NUM_BUCKETS, BIAS_HEADS), 0.5),
        'norm_mix': 1.0 + nrm(2, (DEPTH, D_MODEL), 0.1),
        'norm_mlp': 1.0 + nrm(3, (DEPTH, D_MODEL), 0.1),
        'norm_final': 1.0 + nrm(4, (D_MODEL,), 0.1),
        'mlp_w1': nrm(5, (DEPTH, D_MODEL, D_FF), D_MODEL ** -0.5),
        'mlp_w2': nrm(6, (DEPTH, D_FF, D_MODEL), D_FF ** -0.5),
        'ev_w_in': nrm(7, (ne, D_MODEL, EVEN_PROJ), D_MODEL ** -0.5),
        'ev_w_out': nrm(8, (ne, D_MIX, D_MODEL), D_MIX ** -0.5),
        'ev_cmp_pos_k': nrm(9, (ne, CMP_BLOCK, HEAD_DIM), 0.1),
        'ev_cmp_w1_k': nrm(10, (ne, CMP_BLOCK * HEAD_DIM, CMP_HIDDEN), (CMP_BLOCK * HEAD_DIM) ** -0.5),
        'ev_cmp_w2_k': nrm(11, (ne, CMP_HIDDEN, HEAD_DIM), CMP_HIDDEN ** -0.5),
        'ev_cmp_pos_v': nrm(12, (ne, CMP_BLOCK, HEAD_DIM), 0.1),
        'ev_cmp_w1_v': nrm(13, (ne, CMP_BLOCK * HEAD_DIM, CMP_HIDDEN), (CMP_BLOCK * HEAD_DIM) ** -0.5),
        'ev_cmp_w2_v': nrm(14, (ne, CMP_HIDDEN, HEAD_DIM), CMP_HIDDEN ** -0.5),
        'ev_lam_q1': nrm(15, (ne, HEAD_DIM), 0.1),
        'ev_lam_k1': nrm(16, (ne, HEAD_DIM), 0.1),
        'ev_lam_q2': nrm(17, (ne, HEAD_DIM), 0.1),
        'ev_lam_k2': nrm(18, (ne, HEAD_DIM), 0.1),
        'ev_subln': 1.0 + nrm(19, (ne, DIFF_VDIM), 0.1),
        'od_w_in': nrm(20, (no, D_MODEL, ODD_PROJ), D_MODEL ** -0.5),
        'od_w_out': nrm(21, (no, ODD_MIX, D_MODEL), ODD_MIX ** -0.5),
    }

def first_block(x, bias_table, norm_mix, norm_mlp, norm_final, mlp_w1, mlp_w2,
              ev_w_in, ev_w_out, ev_cmp_pos_k, ev_cmp_w1_k, ev_cmp_w2_k,
              ev_cmp_pos_v, ev_cmp_w1_v, ev_cmp_w2_v, ev_lam_q1, ev_lam_k1,
              ev_lam_q2, ev_lam_k2, ev_subln, od_w_in, od_w_out):
    for i in range(DEPTH):
        hn = rms_norm(x, norm_mix[i])
        if i % 2 == 0:
            e = i // 2
            lam_init = 0.8 - 0.6 * math.exp(-0.3 * i)
            mix = even_mixer(hn, ev_w_in[e], ev_w_out[e], ev_cmp_pos_k[e], ev_cmp_w1_k[e],
                             ev_cmp_w2_k[e], ev_cmp_pos_v[e], ev_cmp_w1_v[e], ev_cmp_w2_v[e],
                             ev_lam_q1[e], ev_lam_k1[e], ev_lam_q2[e], ev_lam_k2[e],
                             ev_subln[e], bias_table, lam_init)
        else:
            o = i // 2
            mix = odd_mixer(hn, od_w_in[o], od_w_out[o], bias_table)
        x = x + mix
        x = x + sqrelu_mlp(rms_norm(x, norm_mlp[i]), mlp_w1[i], mlp_w2[i])
    return rms_norm(x, norm_final)


F32 = jnp.float32

GDN_HEADS = 6
GDN_DK = 64
GDN_DV = 64
GDN_CONV = 5
GDN_CHUNK = 64
GDN_QK_W = GDN_HEADS * GDN_DK
GDN_W = GDN_HEADS * GDN_DV
GDN_QKV_W = 2 * GDN_QK_W + GDN_W

MLA_HEADS = 6
MLA_NOPE = 64
MLA_ROPE = 32
MLA_V = 64
MLA_Q_RANK = 192
MLA_KV_RANK = 128
MLA_QBLOCK = 128
ROPE_THETA = 10000.0
MLA_W = MLA_HEADS * MLA_V

RWKV_HEADS = 4
RWKV_HD = 64
RWKV_DECAY_LORA = 64
RWKV_ICLR_LORA = 64
RWKV_W = RWKV_HEADS * RWKV_HD
RWKV_SHIFT_W = 3 * RWKV_W + RWKV_DECAY_LORA + RWKV_ICLR_LORA
RWKV_LN_EPS = 64e-5

D_MIX_2 = GDN_W + MLA_W + RWKV_W
NORM_EPS = 1e-6

IN_LAYOUT = (
    ('gate', D_MIX_2),
    ('gdn_q', GDN_QK_W), ('gdn_k', GDN_QK_W), ('gdn_v', GDN_W),
    ('gdn_a', 2 * GDN_HEADS), ('gdn_b', 2 * GDN_HEADS),
    ('mla_cq', MLA_Q_RANK), ('mla_ckv', MLA_KV_RANK), ('mla_kr', MLA_ROPE),
    ('rw_r', RWKV_W), ('rw_k', RWKV_W), ('rw_v', RWKV_W),
    ('rw_wd', RWKV_DECAY_LORA), ('rw_ad', RWKV_ICLR_LORA),
)
N_IN = sum(width for _, width in IN_LAYOUT)


def split_columns(p):
    cols = {}
    off = 0
    for name, width in IN_LAYOUT:
        cols[name] = p[..., off:off + width]
        off += width
    return cols

def rms_norm_2(x, g, eps=NORM_EPS):
    xf = x.astype(F32)
    y = xf * lax.rsqrt(jnp.mean(xf * xf, axis=-1, keepdims=True) + eps)
    return (y * g.astype(F32)).astype(x.dtype)

def l2_normalize(x, eps=1e-6):
    xf = x.astype(F32)
    return xf * lax.rsqrt(jnp.sum(xf * xf, axis=-1, keepdims=True) + eps)

def centred_depthwise_conv(x, w):
    pad = w.shape[0] // 2
    return lax.conv_general_dilated(
        x, w[:, None, :].astype(x.dtype), window_strides=(1,), padding=[(pad, pad)],
        dimension_numbers=('NWC', 'WIO', 'NWC'), feature_group_count=x.shape[-1])

def centred_token_shift(x, mu):
    zeros = jnp.zeros_like(x[:, :1])
    x_prev = jnp.concatenate([zeros, x[:, :-1]], axis=1)
    x_next = jnp.concatenate([x[:, 1:], zeros], axis=1)
    return x + mu[0] * (x_prev - x) + mu[1] * (x_next - x)

def bidir_stack(t_fwd, t_bwd):
    return jnp.concatenate([t_fwd, jnp.flip(t_bwd, axis=1)], axis=0)

def bidir_merge(y):
    b = y.shape[0] // 2
    return y[:b] + jnp.flip(y[b:], axis=1)

def gated_delta_chunked(q, k, v, g, beta):
    n, l, h, dk = q.shape
    dv = v.shape[-1]
    c = GDN_CHUNK
    nc = l // c

    def chunks(t):
        return jnp.moveaxis(t.reshape((n, nc, c, h) + t.shape[3:]), 3, 1)

    q, k, v, g, beta = chunks(q), chunks(k), chunks(v), chunks(g), chunks(beta)
    cum = jnp.cumsum(g, axis=-1)
    diff = cum[..., :, None] - cum[..., None, :]
    idx = jnp.arange(c)
    incl = idx[:, None] >= idx[None, :]
    strict = idx[:, None] > idx[None, :]
    d_incl = jnp.exp(jnp.where(incl, diff, -jnp.inf))
    d_strict = jnp.where(strict, d_incl, 0.0)
    a_mat = beta[..., :, None] * jnp.einsum('nhcid,nhcjd->nhcij', k, k) * d_strict
    gam = jnp.exp(cum)
    rhs = jnp.concatenate([beta[..., None] * v, (beta * gam)[..., None] * k], axis=-1)
    sol = lax.linalg.triangular_solve(a_mat, rhs, left_side=True, lower=True, unit_diagonal=True)
    u0, w = sol[..., :dv], sol[..., dv:]
    p_intra = jnp.einsum('nhcid,nhcjd->nhcij', q, k) * d_incl
    q_g = q * gam[..., None]
    k_d = k * jnp.exp(cum[..., -1:] - cum)[..., None]
    g_end = jnp.exp(cum[..., -1])
    xs = tuple(jnp.moveaxis(t, 2, 0) for t in (w, u0, p_intra, q_g, k_d, g_end))

    def step(s, inp):
        w_c, u0_c, p_c, qg_c, kd_c, ge_c = inp
        u = u0_c - jnp.einsum('nhcd,nhde->nhce', w_c, s)
        o = jnp.einsum('nhcd,nhde->nhce', qg_c, s) + jnp.einsum('nhij,nhje->nhie', p_c, u)
        s = ge_c[..., None, None] * s + jnp.einsum('nhcd,nhce->nhde', kd_c, u)
        return s, o

    s0 = jnp.zeros((n, h, dk, dv), F32)
    _, o = lax.scan(step, s0, xs)
    return jnp.transpose(o, (1, 0, 3, 2, 4)).reshape(n, l, h, dv)

def gdn_branch(cols, conv_w, a_log, dt_bias, norm_g):
    b, l = cols['gdn_q'].shape[:2]
    qkv = jnp.concatenate([cols['gdn_q'], cols['gdn_k'], cols['gdn_v']], axis=-1)
    qkv = jax.nn.silu(centred_depthwise_conv(qkv, conv_w))
    q, k, v = jnp.split(qkv, [GDN_QK_W, 2 * GDN_QK_W], axis=-1)
    q = l2_normalize(q.reshape(b, l, GDN_HEADS, GDN_DK)) * (GDN_DK ** -0.5)
    k = l2_normalize(k.reshape(b, l, GDN_HEADS, GDN_DK))
    v = v.reshape(b, l, GDN_HEADS, GDN_DV).astype(F32)
    a = cols['gdn_a'].astype(F32).reshape(b, l, 2, GDN_HEADS)
    bt = cols['gdn_b'].astype(F32).reshape(b, l, 2, GDN_HEADS)
    g = -jnp.exp(a_log.astype(F32)) * jax.nn.softplus(a + dt_bias.astype(F32))
    beta = jax.nn.sigmoid(bt)
    o = gated_delta_chunked(
        bidir_stack(q, q), bidir_stack(k, k), bidir_stack(v, v),
        bidir_stack(g[:, :, 0], g[:, :, 1]), bidir_stack(beta[:, :, 0], beta[:, :, 1]))
    o = rms_norm_2(bidir_merge(o), norm_g)
    return o.reshape(b, l, GDN_W)

def apply_rope(x, cos, sin):
    xf = x.astype(F32)
    x1, x2 = jnp.split(xf, 2, axis=-1)
    return jnp.concatenate([x1 * cos - x2 * sin, x2 * cos + x1 * sin], axis=-1)

def mla_branch(cols, positions, q_norm_g, w_uq, kv_norm_g, w_ukv):
    b, l = cols['mla_cq'].shape[:2]
    q = (rms_norm_2(cols['mla_cq'], q_norm_g) @ w_uq).reshape(b, l, MLA_HEADS, MLA_NOPE + MLA_ROPE)
    kv = (rms_norm_2(cols['mla_ckv'], kv_norm_g) @ w_ukv).reshape(b, l, MLA_HEADS, MLA_NOPE + MLA_V)
    q_nope, q_rot = q[..., :MLA_NOPE], q[..., MLA_NOPE:]
    k_nope, v = kv[..., :MLA_NOPE], kv[..., MLA_NOPE:]
    half = MLA_ROPE // 2
    inv_freq = ROPE_THETA ** (-jnp.arange(half, dtype=F32) / half)
    ang = positions.astype(F32)[..., None] * inv_freq
    cos, sin = jnp.cos(ang), jnp.sin(ang)
    q_rot = apply_rope(q_rot, cos[:, :, None], sin[:, :, None])
    k_rot = apply_rope(cols['mla_kr'], cos, sin)
    scale = (MLA_NOPE + MLA_ROPE) ** -0.5
    q = jnp.concatenate([q_nope.astype(F32), q_rot], axis=-1) * scale
    k = jnp.concatenate([k_nope.astype(F32),
                         jnp.broadcast_to(k_rot[:, :, None], (b, l, MLA_HEADS, MLA_ROPE))], axis=-1)
    v = v.astype(F32)
    nb = l // MLA_QBLOCK
    q_blocks = jnp.moveaxis(q.reshape(b, nb, MLA_QBLOCK, MLA_HEADS, MLA_NOPE + MLA_ROPE), 1, 0)

    def attend(q_blk):
        s = jnp.einsum('bqhd,bkhd->bhqk', q_blk, k)
        p = jax.nn.softmax(s, axis=-1)
        return jnp.einsum('bhqk,bkhd->bqhd', p, v)

    o = lax.map(attend, q_blocks)
    return jnp.moveaxis(o, 0, 1).reshape(b, l, MLA_W)

def to_heads_2(t):
    return t.reshape(t.shape[:-1] + (RWKV_HEADS, RWKV_HD))

def rwkv7_branch(cols, mu, w0, w2, a0, a2, k_k, k_a, r_k, ln_g, ln_b):
    b, l = cols['rw_r'].shape[:2]
    feats = jnp.concatenate([cols['rw_r'], cols['rw_k'], cols['rw_v'], cols['rw_wd'], cols['rw_ad']],
                            axis=-1).astype(F32)
    feats = centred_token_shift(feats, mu.astype(F32))
    r, k, v, wd, ad = jnp.split(feats, [RWKV_W, 2 * RWKV_W, 3 * RWKV_W, 3 * RWKV_W + RWKV_DECAY_LORA], axis=-1)
    w_log = -jax.nn.softplus(-(w0.astype(F32)[:, None, None]
                               + jnp.einsum('bld,edc->eblc', jnp.tanh(wd), w2.astype(F32)))) - 0.5
    decay = jnp.exp(-jnp.exp(w_log))
    a = jax.nn.sigmoid(a0.astype(F32)[:, None, None] + jnp.einsum('bld,edc->eblc', ad, a2.astype(F32)))
    kk = l2_normalize(to_heads_2(k * k_k.astype(F32)))
    k_mod = k[None] * (1.0 + (a - 1.0) * k_a.astype(F32))
    r_h, v_h = to_heads_2(r), to_heads_2(v)
    a_h = to_heads_2(a)
    xs = (
        bidir_stack(r_h, r_h),
        bidir_stack(to_heads_2(decay[0]), to_heads_2(decay[1])),
        bidir_stack(to_heads_2(k_mod[0]), to_heads_2(k_mod[1])),
        bidir_stack(v_h, v_h),
        bidir_stack(kk, kk),
        bidir_stack(a_h[0] * kk, a_h[1] * kk),
    )
    xs = tuple(jnp.moveaxis(t, 1, 0) for t in xs)

    def step(s, inp):
        r_t, w_t, k_t, v_t, kk_t, b_t = inp
        sa = jnp.einsum('nhij,nhj->nhi', s, -kk_t)
        s = s * w_t[:, :, None, :] + sa[..., None] * b_t[:, :, None, :] + v_t[..., None] * k_t[:, :, None, :]
        y = jnp.einsum('nhij,nhj->nhi', s, r_t)
        return s, y

    s0 = jnp.zeros((2 * b, RWKV_HEADS, RWKV_HD, RWKV_HD), F32)
    _, y = lax.scan(step, s0, xs)
    y = bidir_merge(jnp.moveaxis(y, 0, 1))
    mean = jnp.mean(y, axis=-1, keepdims=True)
    var = jnp.mean(jnp.square(y - mean), axis=-1, keepdims=True)
    y = ((y - mean) * lax.rsqrt(var + RWKV_LN_EPS)).reshape(b, l, RWKV_W) * ln_g.astype(F32) + ln_b.astype(F32)
    k_bonus = to_heads_2(0.5 * (k_mod[0] + k_mod[1]))
    bonus = jnp.sum(r_h * k_bonus * r_k.astype(F32), axis=-1, keepdims=True) * v_h
    return y + bonus.reshape(b, l, RWKV_W)

def second_inputs(seed: int = 0) -> dict:
    key = jax.random.key(seed)
    ks = jax.random.split(key, 24)

    def nrm(k, shape, scale):
        return jax.random.normal(k, shape, F32) * scale

    x = nrm(ks[0], (BATCH, SEQ, D_MODEL), 1.0)
    positions = (jnp.arange(SEQ, dtype=jnp.int32)[None, :]
                 + jax.random.randint(ks[1], (BATCH, 1), 0, 512, dtype=jnp.int32))
    norm_g = 1.0 + nrm(ks[2], (DEPTH, D_MODEL), 0.02)
    w_in = nrm(ks[3], (DEPTH, D_MODEL, N_IN), D_MODEL ** -0.5)
    gdn_conv = nrm(ks[4], (DEPTH, GDN_CONV, GDN_QKV_W), GDN_CONV ** -0.5)
    gdn_a_log = jnp.log(jax.random.uniform(ks[5], (DEPTH, 2, GDN_HEADS), F32, 1.0, 16.0))
    dt = jnp.exp(jax.random.uniform(ks[6], (DEPTH, 2, GDN_HEADS), F32, math.log(1e-3), math.log(1e-1)))
    gdn_dt_bias = dt + jnp.log(-jnp.expm1(-dt))
    gdn_norm_g = 1.0 + nrm(ks[7], (DEPTH, GDN_DV), 0.02)
    mla_q_norm_g = 1.0 + nrm(ks[8], (DEPTH, MLA_Q_RANK), 0.02)
    mla_w_uq = nrm(ks[9], (DEPTH, MLA_Q_RANK, MLA_HEADS * (MLA_NOPE + MLA_ROPE)), MLA_Q_RANK ** -0.5)
    mla_kv_norm_g = 1.0 + nrm(ks[10], (DEPTH, MLA_KV_RANK), 0.02)
    mla_w_ukv = nrm(ks[11], (DEPTH, MLA_KV_RANK, MLA_HEADS * (MLA_NOPE + MLA_V)), MLA_KV_RANK ** -0.5)
    rwkv_mu = jax.random.uniform(ks[12], (DEPTH, 2, RWKV_SHIFT_W), F32, 0.0, 0.5)
    rwkv_w0 = jax.random.uniform(ks[13], (DEPTH, 2, RWKV_W), F32, -6.0, -1.0)
    rwkv_w2 = nrm(ks[14], (DEPTH, 2, RWKV_DECAY_LORA, RWKV_W), 0.1)
    rwkv_a0 = nrm(ks[15], (DEPTH, 2, RWKV_W), 0.1)
    rwkv_a2 = nrm(ks[16], (DEPTH, 2, RWKV_ICLR_LORA, RWKV_W), 0.1)
    rwkv_k_k = 0.85 + nrm(ks[17], (DEPTH, RWKV_W), 0.02)
    rwkv_k_a = 1.0 + nrm(ks[18], (DEPTH, RWKV_W), 0.02)
    rwkv_r_k = nrm(ks[19], (DEPTH, RWKV_HEADS, RWKV_HD), 0.1)
    rwkv_ln_g = 1.0 + nrm(ks[20], (DEPTH, RWKV_W), 0.02)
    rwkv_ln_b = nrm(ks[21], (DEPTH, RWKV_W), 0.02)
    w_out = nrm(ks[22], (DEPTH, D_MIX_2, D_MODEL), D_MIX_2 ** -0.5)
    final_norm_g = 1.0 + nrm(ks[23], (D_MODEL,), 0.02)
    return {
        'x': x, 'positions': positions, 'norm_g': norm_g, 'w_in': w_in,
        'gdn_conv': gdn_conv, 'gdn_a_log': gdn_a_log, 'gdn_dt_bias': gdn_dt_bias, 'gdn_norm_g': gdn_norm_g,
        'mla_q_norm_g': mla_q_norm_g, 'mla_w_uq': mla_w_uq, 'mla_kv_norm_g': mla_kv_norm_g, 'mla_w_ukv': mla_w_ukv,
        'rwkv_mu': rwkv_mu, 'rwkv_w0': rwkv_w0, 'rwkv_w2': rwkv_w2, 'rwkv_a0': rwkv_a0, 'rwkv_a2': rwkv_a2,
        'rwkv_k_k': rwkv_k_k, 'rwkv_k_a': rwkv_k_a, 'rwkv_r_k': rwkv_r_k,
        'rwkv_ln_g': rwkv_ln_g, 'rwkv_ln_b': rwkv_ln_b,
        'w_out': w_out, 'final_norm_g': final_norm_g,
    }

def second_block(x, positions, norm_g, w_in, gdn_conv, gdn_a_log, gdn_dt_bias, gdn_norm_g,
              mla_q_norm_g, mla_w_uq, mla_kv_norm_g, mla_w_ukv,
              rwkv_mu, rwkv_w0, rwkv_w2, rwkv_a0, rwkv_a2, rwkv_k_k, rwkv_k_a, rwkv_r_k,
              rwkv_ln_g, rwkv_ln_b, w_out, final_norm_g):
    for layer in range(DEPTH):
        h = rms_norm_2(x, norm_g[layer])
        cols = split_columns(h @ w_in[layer])
        y_gdn = gdn_branch(cols, gdn_conv[layer], gdn_a_log[layer], gdn_dt_bias[layer], gdn_norm_g[layer])
        y_mla = mla_branch(cols, positions, mla_q_norm_g[layer], mla_w_uq[layer],
                           mla_kv_norm_g[layer], mla_w_ukv[layer])
        y_rwkv = rwkv7_branch(cols, rwkv_mu[layer], rwkv_w0[layer], rwkv_w2[layer], rwkv_a0[layer],
                              rwkv_a2[layer], rwkv_k_k[layer], rwkv_k_a[layer], rwkv_r_k[layer],
                              rwkv_ln_g[layer], rwkv_ln_b[layer])
        mix = jnp.concatenate([y_gdn.astype(F32), y_mla.astype(F32), y_rwkv.astype(F32)], axis=-1)
        mix = mix * jax.nn.silu(cols['gate'].astype(F32))
        x = x + mix.astype(x.dtype) @ w_out[layer]
    return rms_norm_2(x, final_norm_g)


def setup_inputs(seed=0):
    out = dict(first_inputs(seed))
    for name, value in second_inputs(seed + 1).items():
        if name != "x":
            out[name + "_2"] = value
    return out


def reference(
    x, bias_table, norm_mix, norm_mlp, norm_final, mlp_w1, mlp_w2, ev_w_in, ev_w_out,
    ev_cmp_pos_k, ev_cmp_w1_k, ev_cmp_w2_k, ev_cmp_pos_v, ev_cmp_w1_v, ev_cmp_w2_v, ev_lam_q1,
    ev_lam_k1, ev_lam_q2, ev_lam_k2, ev_subln, od_w_in, od_w_out, positions_2, norm_g_2, w_in_2,
    gdn_conv_2, gdn_a_log_2, gdn_dt_bias_2, gdn_norm_g_2, mla_q_norm_g_2, mla_w_uq_2,
    mla_kv_norm_g_2, mla_w_ukv_2, rwkv_mu_2, rwkv_w0_2, rwkv_w2_2, rwkv_a0_2, rwkv_a2_2,
    rwkv_k_k_2, rwkv_k_a_2, rwkv_r_k_2, rwkv_ln_g_2, rwkv_ln_b_2, w_out_2, final_norm_g_2,
):
    x = first_block(
        x, bias_table, norm_mix, norm_mlp, norm_final, mlp_w1, mlp_w2, ev_w_in, ev_w_out,
        ev_cmp_pos_k, ev_cmp_w1_k, ev_cmp_w2_k, ev_cmp_pos_v, ev_cmp_w1_v, ev_cmp_w2_v,
        ev_lam_q1, ev_lam_k1, ev_lam_q2, ev_lam_k2, ev_subln, od_w_in, od_w_out,
    )
    return second_block(
        x, positions_2, norm_g_2, w_in_2, gdn_conv_2, gdn_a_log_2, gdn_dt_bias_2, gdn_norm_g_2,
        mla_q_norm_g_2, mla_w_uq_2, mla_kv_norm_g_2, mla_w_ukv_2, rwkv_mu_2, rwkv_w0_2,
        rwkv_w2_2, rwkv_a0_2, rwkv_a2_2, rwkv_k_k_2, rwkv_k_a_2, rwkv_r_k_2, rwkv_ln_g_2,
        rwkv_ln_b_2, w_out_2, final_norm_g_2,
    )


_drawn_inputs = setup_inputs


def setup_inputs(seed=0):
    import zlib

    import numpy as np

    out = dict(_drawn_inputs(seed))
    spreads = {}
    factors = {'ev_cmp_pos_k': 8.0,
     'gdn_norm_g_2': 5.764,
     'mla_q_norm_g_2': 8.0,
     'mla_kv_norm_g_2': 8.0,
     'rwkv_a0_2': 3.675,
     'rwkv_ln_g_2': 6.671,
     'rwkv_ln_b_2': 7.28,
     'final_norm_g_2': 2.832}
    for name, (base, spread) in spreads.items():
        noise = np.random.default_rng([zlib.crc32(name.encode()), seed]).standard_normal(out[name].shape)
        drawn = base * np.exp(spread * noise) if base else spread * noise
        out[name] = jnp.asarray(drawn.astype(out[name].dtype))
    for name, factor in factors.items():
        out[name] = (out[name] * factor).astype(out[name].dtype)
    return out
```

```python
import math
from contextlib import ExitStack

import numpy as np
import concourse.bass as bass
from concourse import mybir

F32 = mybir.dt.float32
I32 = mybir.dt.int32
ALU = mybir.AluOpType
ACT = mybir.ActivationFunctionType
AX = mybir.AxisListType
ADD, SUB, MUL, MAX, MIN = ALU.add, ALU.subtract, ALU.mult, ALU.max, ALU.min

P = 128
S = 256
T = S // P
D = 1024
KC = D // P
HD = 64
NEG = -1e30
LAM_INIT = 0.8 - 0.6 * math.exp(0.0)
SLAB = 4096
SLOTS = 4
LEVELS = (2, 4, 8, 16, 32, 64)
NC_CMP = (S - 32) // 16 + 1

C_ID, C_ONE, C_BLK, C_TRI, C_NEG = 0, 128, 256, 384, 640
C_SI = 896
C_M1 = 1408
C_LV = 1664
C_FRQ = C_LV + 2 * len(LEVELS) * P
C_ROWOK = C_FRQ + 16
C_EPS = C_ROWOK + 2
C_N = C_EPS + 3


def shape_constants():
    c = np.zeros((P, C_N), np.float32)
    j = np.arange(P)[:, None]
    i = np.arange(P)[None, :]
    c[:, C_ID:C_ID + P] = j == i
    c[:, C_ONE:C_ONE + P] = 1
    c[:, C_BLK:C_BLK + P] = (j // 64) == (i // 64)
    for d, (inc, strict) in enumerate(((j <= i, j < i), (j >= i, j > i))):
        c[:, C_TRI + d * P:C_TRI + (d + 1) * P] = inc
        c[:, C_NEG + d * P:C_NEG + (d + 1) * P] = np.where(inc, 0, NEG)
        c[:, C_SI + 2 * d * P:C_SI + (2 * d + 1) * P] = strict
        c[:, C_SI + (2 * d + 1) * P:C_SI + (2 * d + 2) * P] = inc
        lo, hi = (j, i) if d == 0 else (i, j)
        c[:, C_M1 + d * P:C_M1 + (d + 1) * P] = (lo // 2 == hi // 2) & (lo < hi)
        for n, m in enumerate(LEVELS):
            same = (j // (2 * m)) == (i // (2 * m))
            late, early = (j % (2 * m) >= m), (i % (2 * m) < m)
            if d == 1:
                late, early = ~late, ~early
            o = C_LV + (d * len(LEVELS) + n) * P
            c[:, o:o + P] = same & late & early
    c[:, C_FRQ:C_FRQ + 16] = np.float32(10000.0) ** (-np.arange(16, dtype=np.float32) / np.float32(16))
    for t in range(T):
        c[:, C_ROWOK + t] = (t * P + np.arange(P)) >= 31
    c[:, C_EPS] = 1e-6
    c[:, C_EPS + 1] = 64e-5
    c[:, C_EPS + 2] = 1.0
    rel = 255 - np.arange(384)
    n = np.maximum(rel, 0)
    large = 16 + (np.log(np.maximum(n, 1).astype(np.float32) / 16) / np.float32(math.log(8.0)) * 16).astype(np.int32)
    bucket = np.where(n < 16, n, np.minimum(large, 31))
    oh = np.zeros((32, 768), np.float32)
    oh[bucket, np.arange(384)] = rel >= 0
    oh[:, 384:] = np.where(rel >= 0, 0, 8 * NEG)
    return c, oh


BT = 0
_b1 = 4096
QT, KCVC, KST, KD = _b1, _b1 + 1024, _b1 + 1536, _b1 + 2048
VS, VW, GT = _b1 + 3072, _b1 + 3328, _b1 + 3584
DQ, DK, DV = _b1 + 3632, _b1 + 4656, _b1 + 5680
BLK, HID, GE = _b1 + 6704, _b1 + 7664, _b1 + 7724
KCT, VCN, VBD, PC, PCT = _b1 + 7844, _b1 + 7874, _b1 + 8002, _b1 + 8514, _b1 + 8770
_mix0 = _b1 + 9026
_pb = _mix0 + 2048
TBL, OH, FR, STG = _pb, _pb + 16, _pb + 784, _pb + 1168
MQ, MV = _b1, _b1 + 4096
HT = _b1
GATE, MIXB, RP = 0, 2048, 4096
_r = 5904
GP, GC = _r, _r + 2340
LOW = _r + 4644
_m = LOW + 752
CQN, CT = _m, _m + 640
QN, KN, KV = _m + 1408, _m + 2560, _m + 3712
QKT = _m + 5248
RTM = GC
GN = _m
KQ = GN + 2304
XTG, YYG = KQ + 1536, KQ + 3072
GKD = YYG + 1536
GR, GU = GKD + 384, GKD + 768
GS, RT0 = 0, 384
GLT, GPT, XXG = _r, _r + 1536, _r + 3072
GO = LOW - 28
RF = _r
RKX, RKK2, RVN = RF + 1792, RF + 2304, RF + 2816
RPR = RKK2
RSW, RSA, RKM, RCM, REP, RCL = (RF + 3328 + 1024 * i for i in range(6))
RAR, RBK = RF + 9472, RF + 11520
RM4, RXX, RXT = RSW, REP, RCL
RYY, RBN, RY = RF, RF + 1024, RF + 1536
RU, RRH = RF + 2048, RF + 2432
R_N = 19640

SS, SB, LM, CM, TRG, TRK, PF, NB, MU = 0, 24, 32, 40, 64, 128, 144, 150, 160
RMD, REN, RE, BN, YM, MXB = 168, 176, 184, 192, 200, 212
GAB, GBT, GSP, GAL, GG, GCU, GGA, GKF = 500, 524, 548, 572, 584, 608, 656, 680
SUMS = {"sel": 300, "win": 320, "moba": 340, "diff": 380, "mla": 400}


def XT(st):
    return XTG if st == "g" else RXT


def XX(st):
    return XXG if st == "g" else RXX


def YY(st):
    return YYG if st == "g" else RYY


def GE_(g):
    return YYG + 512 * g


def RT(m):
    return HT + 8192 + 512 * m


def MIX(L):
    return _mix0 if L < 2 else MIXB


def PB(h, name=""):
    return (GC if isinstance(name, tuple) else _pb) + (h % 3) * 768


def PTB(h, name=""):
    return (QN if isinstance(name, tuple) else _pb + 2304) + (h % 2) * 512


def MX(h, mp):
    return MXB + (h % 4) * 4 + 2 * mp


def SU(name, h, mp):
    return SUMS[name[0] if isinstance(name, tuple) else name] + (4 * h + 2 * mp if name == "diff" else 2 * h)


_INS = ["x", "bias_table", "norm_mix", "norm_mlp", "norm_final", "mlp_w1", "mlp_w2", "ev_w_in", "ev_w_out",
        "ev_cmp_pos_k", "ev_cmp_w1_k", "ev_cmp_w2_k", "ev_cmp_pos_v", "ev_cmp_w1_v", "ev_cmp_w2_v", "ev_lam_q1",
        "ev_lam_k1", "ev_lam_q2", "ev_lam_k2", "ev_subln", "od_w_in", "od_w_out", "positions_2", "norm_g_2", "w_in_2",
        "gdn_conv_2", "gdn_a_log_2", "gdn_dt_bias_2", "gdn_norm_g_2", "mla_q_norm_g_2", "mla_w_uq_2",
        "mla_kv_norm_g_2", "mla_w_ukv_2", "rwkv_mu_2", "rwkv_w0_2", "rwkv_w2_2", "rwkv_a0_2", "rwkv_a2_2",
        "rwkv_k_k_2", "rwkv_k_a_2", "rwkv_r_k_2", "rwkv_ln_g_2", "rwkv_ln_b_2", "w_out_2", "final_norm_g_2"]


class Counts:

    def __init__(self, nc, ctx, known):
        self.nc, self.ctx, self.known = nc, ctx, known
        self.sems, self.value, self.table = {}, {}, {}

    def sem(self, name):
        if name not in self.sems:
            self.sems[name] = self.ctx.enter_context(self.nc.semaphore(name))
            self.value[name] = 0
        return self.sems[name]

    def up(self, name, *key, by=1):
        s = self.sem(name)
        self.value[name] += by
        assert (name,) + key not in self.table, (name, key)
        self.table[(name,) + key] = self.last = self.value[name]
        return s, by

    def at(self, name, *key):
        s = self.sem(name)
        return s, (self.known[(name,) + key] if self.known else 1)


def view(t, off, *dims, p0=0, np_=P):
    w = t.shape[1]
    return bass.AP(t, p0 * w + off, [[w, np_]] + [list(x) for x in dims])


def program(nc, a, out, known=None):
    ctx = ExitStack()
    with ctx:
        C = Counts(nc, ctx, known)
        up, at = C.up, C.at

        def sb(name, n, dt=F32):
            return ctx.enter_context(nc.sbuf_tensor(name, [P, n], dt))

        scratch = nc.dram_tensor("bias_by_distance" + ("" if known else "_dry"), [16, P * 384], F32, kind="Internal")
        ps = ctx.enter_context(nc.psum_tensor("banks", [P, 8 * 512], F32))
        slabs = sb("weight_slabs", SLOTS * SLAB)
        x = sb("x_res", T * D)
        hn = sb("hn", T * D)
        hnT = sb("hnT", KC * S)
        cst = sb("consts", C_N)
        cols = sb("columns", 2 * P)
        rows = sb("row_params", 2680)
        mlaw = sb("mla_weights", 1920)
        rww = sb("rwkv_lora", 512)
        cmpw = sb("cmp_w2", 128)
        sm = sb("small", 1024)
        R = sb("region", R_N)
        posi = sb("positions", T, I32)

        CN_MIX, CN_MLP, CN_G2 = 0, 16, 32
        CL = 48
        K_MU, K_W0, K_A0, K_KK, K_KA, K_RK, K_QN, K_KVN = 0, 14, 18, 22, 24, 26, 28, 30
        CB_CONV, CB_POS = P, P + 90
        R_SUB, R_GN, R_LNG, R_LNB, R_FIN, R_AL, R_DT, R_LAM = 0, 128, 256, 768, 1280, 2304, 2328, 2352

        def cc(c, n=1):
            return cst[:, c:c + n]

        IDENT = cst[:, C_ID:C_ID + P]

        plan = []

        def cols_slab(key, w, c0, n):
            plan.append((key, [(view(slabs, 0, (n, KC), (1, n)), w[:, c0:c0 + n].rearrange("(k p) n -> p k n", p=P))]))

        def rows_slab(key, w, r0):
            plan.append((key, [(view(slabs, 0, (D, 4), (1, D)), w[r0:r0 + 512, :].rearrange("(k p) n -> p k n", p=P))]))

        for n, (c0, w) in enumerate(((0, 512), (512, 512), (1024, 280), (1304, 512), (1816, 512), (2328, 512))):
            cols_slab(("in", 0, n), a["ev_w_in"][0], c0, w)
        plan.append((("cmp",), [(view(slabs, 2048 * i, (P, 16), (1, P)),
                                 a[nm][0].rearrange("(k p) n -> p k n", p=P)) for i, nm in enumerate(("ev_cmp_w1_k", "ev_cmp_w1_v"))]))
        for L in range(4):
            if L == 1:
                for n in range(6):
                    cols_slab(("in", 1, n), a["od_w_in"][0], 512 * n, 512)
            if L >= 2:
                for n, (c0, w) in enumerate(((0, 512), (512, 512), (1024, 512), (1536, 512), (2048, 504), (2552, 512), (3064, 384))):
                    cols_slab(("in", L, n), a["w_in_2"][L - 2], c0, w)
            wo = (a["ev_w_out"][0], a["od_w_out"][0], a["w_out_2"][0], a["w_out_2"][1])[L]
            for n in range(2):
                cols_slab(("out", L, n), wo, 512 * n, 512)
            if L < 2:
                for n in range(8):
                    cols_slab(("w1", L, n), a["mlp_w1"][L], 512 * n, 512)
                for n in range(8):
                    rows_slab(("w2", L, n), a["mlp_w2"][L], 512 * n)
        slot_of = {key: n % SLOTS for n, (key, _) in enumerate(plan)}

        jobs = {"short": [], "long": []}
        bank_of = known.get("bank_of", {}) if known else {}
        reader = known.get("reader", {}) if known else {}
        freed_by = known.get("freed_by", {}) if known else {}
        new_bank, new_reader, new_freed = {}, {}, {}

        def bank(key):
            return bank_of.get(key, 0) * 512

        block = ctx.enter_context(nc.Block())

        @block.sync
        def _(sp):
            for n, (key, parts) in enumerate(plan):
                slot = n % SLOTS
                if n >= SLOTS:
                    sp.wait_ge(*at(*freed_by.get(plan[n - SLOTS][0], ("bank_full",))))
                for i, (dst, src) in enumerate(parts):
                    dst = bass.AP(slabs, dst.offset + slot * SLAB, dst.ap)
                    sp.dma_start(dst, src).then_inc(*up(f"slab_in_slot{slot}", *key, i, by=16))
            for t in range(T):
                sp.wait_ge(*at("result_ready", t))
                sp.dma_start(out[0, t * P:(t + 1) * P, :], view(hn, t * D, (1, D))).then_inc(*up("result_stored", t, by=16))
            for t in range(T):
                sp.wait_ge(*at("result_stored", t))

        @block.tensor
        def _(pe):
            closed = []

            def open_(key, ring="short"):
                size, base = (6, 0) if ring == "short" else (2, 6)
                lst = jobs[ring]
                n = len(lst)
                lst.append(key)
                if n >= size:
                    old = lst[n - size]
                    pe.wait_ge(*at(reader.get(old, "bank_read_by_vector"), *old))
                new_bank[key] = base + n % size
                return (base + n % size) * 512

            def close(ins, key):
                ins.then_inc(*up("bank_full", *key))
                closed.append(key)

            def slab(key, i=0):
                pe.wait_ge(*at(f"slab_in_slot{slot_of[key]}", *key, i))
                return slot_of[key] * SLAB

            def used(key):
                new_freed[key] = ("bank_full",) + closed[-1]

            mm = nc.tensor.matmul

            def transposes(key, srcs, rd, evs=()):
                for e in evs:
                    pe.wait_ge(*e)
                b = open_(key)
                for i, s in enumerate(srcs):
                    k, m = s.shape[0], s.shape[1]
                    ins = nc.tensor.transpose(view(ps, b + i * P, (1, k), np_=m), s, cst[0:k, C_ID:C_ID + k])
                close(ins, key)

            def proj_T(skey, key, c0s, width, wait=()):
                o = slab(skey)
                for e in wait:
                    pe.wait_ge(*e)
                b = open_(key)
                for i, c0 in enumerate(c0s):
                    for k in range(KC):
                        ins = mm(view(ps, b + i * S, (1, S)), view(slabs, o + k * width + c0, (1, P)),
                                 view(hnT, k * S, (1, S)), start=k == 0, stop=k == KC - 1)
                close(ins, key)

            def proj_N(skey, key, c0, n, width, t):
                o = slab(skey)
                b = open_(key)
                for k in range(KC):
                    ins = mm(view(ps, b, (1, n)), view(hnT, k * S + t * P, (1, P)),
                             view(slabs, o + k * width + c0, (1, n)), start=k == 0, stop=k == KC - 1)
                close(ins, key)

            def normed_T(L, which):
                for t in range(T):
                    for q in range(2):
                        transposes(("hnT", which, L, t, q),
                                   [view(hn, t * D + (4 * q + i) * P, (1, P)) for i in range(4)], "v",
                                   [at("hn_ready", which, L, t)])
                pe.wait_ge(*at("bank_read_by_vector", "hnT", which, L, T - 1, 1))

            def mlp(L):
                normed_T(L, "mlp")
                for n in range(8):
                    for m in range(2):
                        proj_T(("w1", L, n), ("h", L, n, m), (256 * m, 256 * m + P), 512)
                    used(("w1", L, n))
                bs = [open_(("y", L, i)) for i in range(4)]
                for n in range(8):
                    o = slab(("w2", L, n))
                    pe.wait_ge(*at("hidden_ready", L, n, 1))
                    for k in range(4):
                        for i in range(4):
                            t, half = i // 2, i % 2
                            kk = 4 * n + k
                            ins = mm(view(ps, bs[i], (1, 512)), view(R, HT + kk * S + t * P, (1, P)),
                                     view(slabs, o + k * D + half * 512, (1, 512)), start=kk == 0, stop=kk == 31)
                            if n == 7 and k == 3:
                                close(ins, ("y", L, i))
                    if n < 7:
                        ins.then_inc(*up("w2_slab_used", L, n))
                        new_freed[("w2", L, n)] = ("w2_slab_used", L, n)
                    else:
                        used(("w2", L, n))

            def out_proj(L):
                for t in range(T):
                    for q in range(2):
                        transposes(("mixT", L, t, q),
                                   [view(R, MIX(L) + t * D + (4 * q + i) * P, (1, P)) for i in range(4)], "v",
                                   [at("mix_ready", L, t)])
                pe.wait_ge(*at("bank_read_by_scalar", "mixT", L, T - 1, 1))
                for n in range(2):
                    for t in range(T):
                        proj_N(("out", L, n), ("o", L, n, t), 0, 512, 512, t)
                    used(("out", L, n))

            def attention(name, H, scores, values, nblk, vw):
                per = 512 // vw
                for i in range(H + 2):
                    if i < H:
                        scores(i)
                    if 0 <= i - 1 < H:
                        h = i - 1
                        key = ("PT", name, h)
                        pe.wait_ge(*at("diff_probs_ready" if name == "diff" else "probs_ready", name, h))
                        b = open_(key)
                        for j in range(nblk):
                            ins = nc.tensor.transpose(view(ps, b + j * P, (1, P)), view(R, PB(h, name) + j * P, (1, P)), IDENT)
                        close(ins, key)
                    if 0 <= i - 2 < H:
                        h = i - 2
                        if h % per == 0:
                            ob = [open_(("O", name, h // per, t), "long") for t in range(T)]
                        pe.wait_ge(*at("bank_read_by_scalar", "PT", name, h))
                        c = (h % per) * vw
                        blocks = ((0, 0, 0), (1, 1, 0), (2, 1, 1)) if nblk == 3 else ((0, 0, 0), (1, 0, 1), (2, 1, 0), (3, 1, 1))
                        for j, t, k in blocks:
                            last_k = k == (t if nblk == 3 else 1)
                            ins = mm(view(ps, ob[t] + c, (1, vw)), view(R, PTB(h, name) + j * P, (1, P)), values(h, k),
                                     start=k == 0, stop=last_k)
                            if last_k and (h % per == per - 1 or h == H - 1):
                                close(ins, ("O", name, h // per, t))

            def causal_scores(name, q_of, k_of):
                def f(h, key=None):
                    key = key or ("S", name, h)
                    b = open_(key)
                    q, k = q_of(h), k_of(h)
                    mm(view(ps, b, (1, P)), q(0, P), k(0, P), start=True, stop=True)
                    close(mm(view(ps, b + P, (1, S)), q(P, P), k(0, S), start=True, stop=True), key)
                return f

            def tview(base, tile, half):
                return lambda o, n: view(R, base + tile * S + o, (1, n), p0=64 * half, np_=64)

            pe.wait_ge(*at("row_params_in", 0))
            pe.wait_ge(*at("constants_in", "o"))
            transposes(("cols",), [view(R, STG, (1, P)), view(R, STG + P, (1, P))], "v")
            b = open_(("bias",))
            close(mm(view(ps, b, (1, 384), np_=16), view(R, TBL, (1, 16), np_=32), view(R, OH, (1, 384), np_=32),
                     start=True, stop=True), ("bias",))

            normed_T(0, "mix")
            for m in range(2):
                proj_T(("in", 0, 0), ("q", m), (256 * m, 256 * m + P), 512)
            used(("in", 0, 0))
            proj_T(("in", 0, 1), ("kcvc",), (0, P), 512)
            proj_T(("in", 0, 1), ("ks",), (256,), 512)
            for t in range(T):
                proj_N(("in", 0, 1), ("vs", t), 384, P, 512, t)
            used(("in", 0, 1))
            proj_T(("in", 0, 2), ("kw",), (0,), 280)
            for t in range(T):
                proj_N(("in", 0, 2), ("vwg", t), 128, 152, 280, t)
            used(("in", 0, 2))
            for m in range(2):
                proj_T(("in", 0, 3), ("dq", m), (256 * m, 256 * m + P), 512)
            used(("in", 0, 3))
            for m in range(2):
                proj_T(("in", 0, 4), ("dk", m), (256 * m, 256 * m + P), 512)
            used(("in", 0, 4))
            for t in range(T):
                proj_N(("in", 0, 5), ("dv", t), 0, 512, 512, t)
            used(("in", 0, 5))
            pe.wait_ge(*at("cmp_blocks_ready", 1))
            for i in range(2):
                o = slab(("cmp",), 1)
                b = open_(("hid", i))
                for jj in range(16):
                    ins = mm(view(ps, b, (1, 30)), view(slabs, o + 2048 * i + jj * P, (1, P)),
                             view(R, BLK + i * 480 + jj * 15, (240, 2), (1, 15)), start=jj == 0, stop=jj == 15)
                close(ins, ("hid", i))
            used(("cmp",))
            pe.wait_ge(*at("cmp_hidden_ready", 1))
            b = open_(("cmpkv",))
            mm(view(ps, b, (1, 30), np_=64), view(cmpw, 0, (1, 64)), view(R, HID, (1, 30)), start=True, stop=True)
            for g in range(2):
                ins = mm(view(ps, b + 64 + 64 * g, (1, 64), np_=15), view(R, HID + 30 + 15 * g, (1, 15)),
                         view(cmpw, 64, (1, 64)), start=True, stop=True)
            close(ins, ("cmpkv",))
            pe.wait_ge(*at("kdup_ready", 0))
            for nm, kb, vb in (("sel", KD, VS), ("win", KD + 512, VW)):
                attention(nm, 8, causal_scores(nm, lambda h: tview(QT, h // 2, h % 2),
                                               lambda h, kb=kb: tview(kb, h // 4, h % 2)),
                          lambda h, k, vb=vb: view(R, vb + k * P + (h // 4) * 64, (1, 64)), 3, 64)
            pe.wait_ge(*at("cmp_kv_ready", 0))
            for par in range(2):
                b = open_(("Sc", par))
                for t in range(T):
                    for hh in range(4):
                        h = 2 * hh + par
                        ins = mm(view(ps, b + (t * 4 + hh) * 16, (1, 15)),
                                 view(R, QT + (h // 2) * S + t * P, (1, P), p0=64 * par, np_=64),
                                 view(R, KCT + (h // 4) * 15, (1, 15), p0=64 * par, np_=64), start=True, stop=True)
                close(ins, ("Sc", par))
            pe.wait_ge(*at("cmp_probs_ready", 0))
            transposes(("PTc",), [view(R, PC + t * P, (1, P)) for t in range(T)], "a")
            pe.wait_ge(*at("bank_read_by_scalar", "PTc"))
            pe.wait_ge(*at("vbd_ready", 0, 7))
            for t in range(T):
                b = open_(("Oc", t))
                close(mm(view(ps, b, (1, 512)), view(R, PCT + t * P, (1, P)), view(R, VBD, (1, 512)), start=True, stop=True),
                      ("Oc", t))
            dsc = causal_scores("diff", lambda c: tview(DQ, c // 2, c % 2), lambda c: tview(DK, c // 2, c % 2))

            def diff_scores(h):
                dsc(2 * h, ("S", "diff", h, 0))
                dsc(2 * h + 1, ("S", "diff", h, 1))
            attention("diff", 4, diff_scores, lambda h, k: view(R, DV + k * 512 + h * P, (1, P)), 3, P)
            out_proj(0)
            mlp(0)

            normed_T(1, "mix")
            for n in range(4):
                for m in range(2):
                    proj_T(("in", 1, n), ("mqk", n, m), (256 * m, 256 * m + P), 512)
                used(("in", 1, n))
            for n in range(2):
                for t in range(T):
                    proj_N(("in", 1, 4 + n), ("mv", n, t), 0, 512, 512, t)
                used(("in", 1, 4 + n))
            pe.wait_ge(*at("bank_read_by_scalar", "mv", 1, 1))
            attention("moba", 16, causal_scores("moba", lambda h: tview(MQ, h // 2, h % 2),
                                                lambda h: tview(MQ, 8 + h // 2, h % 2)),
                      lambda h, k: view(R, MV + k * D + h * 64, (1, 64)), 3, 64)
            out_proj(1)
            mlp(1)

            def invert(tag, d, ngroups, LTv, st):
                for g in range(ngroups):
                    key = ("X0", tag, g)
                    transposes(key, [view(R, XT(st) + (4 * g + i) * P, (1, P)) for i in range(4)], "a",
                               [at("inverse_seed_ready", tag, g)])
                for n, m in enumerate(LEVELS):
                    e = 0 if d == 0 else m
                    l = m - e
                    np2 = P // (2 * m)
                    for g in range(ngroups):
                        if n == 0:
                            pe.wait_ge(*at("bank_read_by_scalar", "X0", tag, g))
                        else:
                            pe.wait_ge(*at("bank_read_by_vector", "Z", tag, n - 1, g))
                        b = open_(("Y", tag, n, g))
                        for i in range(4):
                            ins = mm(view(ps, b + i * P, (1, P)), LTv(4 * g + i), view(R, XX(st) + (4 * g + i) * P, (1, P)),
                                     start=True, stop=True)
                        close(ins, ("Y", tag, n, g))
                    for g in range(ngroups):
                        pe.wait_ge(*at("bank_read_by_vector", "Y", tag, n, g))
                        b = open_(("Z", tag, n, g))
                        for i in range(4):
                            s = (4 * g + i) * P
                            if m < 64:
                                mm(view(ps, b + i * 64, (1, 64)), view(R, XT(st) + s, (1, P)),
                                   view(R, YY(st) + s + e, (2 * m, np2), (1, m)), start=True, stop=True)
                            ins = mm(view(ps, b + 256 + i * 64, (1, 64)), view(R, YY(st) + s, (1, P)),
                                     view(R, XT(st) + s + l, (2 * m, np2), (1, m)), start=True, stop=True)
                        close(ins, ("Z", tag, n, g))
                for g in range(ngroups):
                    pe.wait_ge(*at("bank_read_by_vector", "Z", tag, len(LEVELS) - 1, g))

            for L in (2, 3):
                normed_T(L, "mix")
                for n in range(2):
                    for t in range(T):
                        proj_N(("in", L, n), ("gate", L, n, t), 0, 512, 512, t)
                    used(("in", L, n))
                for n in range(2):
                    for m in range(2):
                        proj_T(("in", L, 2 + n), ("gqkv", L, n, m), (256 * m, 256 * m + P), 512)
                    used(("in", L, 2 + n))
                proj_T(("in", L, 4), ("gqkv", L, 2, 0), (0,), 504)
                for t in range(T):
                    proj_N(("in", L, 4), ("low", L, t), 128, 376, 504, t)
                used(("in", L, 4))
                for m in range(2):
                    proj_T(("in", L, 5), ("rw", L, m), (256 * m, 256 * m + P), 512)
                used(("in", L, 5))
                proj_T(("in", L, 6), ("rw", L, 2), (0, P), 384)
                proj_T(("in", L, 6), ("rw", L, 3), (256,), 384)
                used(("in", L, 6))

                for t in range(T):
                    transposes(("cT", L, t), [view(R, CQN + t * 320, (1, P)), view(R, CQN + t * 320 + P, (1, 64)),
                                              view(R, CQN + t * 320 + 192, (1, P))], "v", [at("latents_ready", L)])
                pe.wait_ge(*at("latents_T_ready", L, 1))
                pe.wait_ge(*at("mla_weights_in", L))
                for t in range(T):
                    for hf in range(2):
                        b = open_(("uq", L, t, hf))
                        mm(view(ps, b, (1, 288)), view(R, CT + t * P, (1, P)), view(mlaw, hf * 288, (1, 288)), start=True, stop=False)
                        close(mm(view(ps, b, (1, 288)), view(R, CT + 256 + t * P, (1, P), np_=64),
                                 view(mlaw, 576 + hf * 288, (1, 288), np_=64), start=False, stop=True), ("uq", L, t, hf))
                    for hf in range(2):
                        b = open_(("ukv", L, t, hf))
                        close(mm(view(ps, b, (1, 384)), view(R, CT + 512 + t * P, (1, P)), view(mlaw, 1152 + hf * 384, (1, 384)),
                                 start=True, stop=True), ("ukv", L, t, hf))
                for h in range(6):
                    transposes(("qkT", L, h), [view(R, QN + t * 576 + h * 96, (1, 96)) for t in range(T)]
                               + [view(R, KN + t * 576 + h * 96, (1, 96)) for t in range(T)], "a", [at("rope_ready", L)])
                pe.wait_ge(*at("bank_read_by_scalar", "qkT", L, 5))

                def mla_scores(h, L=L):
                    b = open_(("S", "mla", L, h))
                    for t in range(T):
                        ins = mm(view(ps, b + t * S, (1, S)), view(R, QKT + h * 512 + t * P, (1, P), np_=96),
                                 view(R, QKT + h * 512 + S, (1, S), np_=96), start=True, stop=True)
                    close(ins, ("S", "mla", L, h))
                attention(("mla", L), 6, mla_scores, lambda h, k: view(R, KV + k * 768 + h * P + 64, (1, 64)), 4, 64)

                for t in range(T):
                    for w in range(3):
                        transposes(("gn", L, t, w), [view(R, GC + (3 * w + i) * S + t * P, (1, P)) for i in range(3)], "a",
                                   [at("conv_ready", L)])
                for m in range(3):
                    transposes(("kq", L, m), [view(R, GN + t * 1152 + w * 384 + m * P, (1, P)) for w in (1, 0) for t in range(T)],
                               "a", [at("qk_normed", L)])
                pe.wait_ge(*at("decay_ready", L))
                b = open_(("cum", L))
                for t in range(T):
                    for d in range(2):
                        mm(view(ps, b + t * 24 + d * 6, (1, 6)), cc(C_TRI + d * P, P), view(sm, GG + t * 12 + d * 6, (1, 6)),
                           start=True, stop=True)
                    ins = mm(view(ps, b + t * 24 + 12, (1, 12)), cc(C_ONE, P), view(sm, GG + t * 12, (1, 12)), start=True, stop=True)
                close(ins, ("cum", L))
                pe.wait_ge(*at("bank_read_by_scalar", "kq", L, 2))
                for d in range(2):
                    tag = ("g", L, d)
                    for g in range(3):
                        b = open_(("E", tag, g))
                        for i in range(4):
                            c, h = divmod(4 * g + i, 6)
                            ins = mm(view(ps, b + i * P, (1, P)), view(sm, GG + c * 12 + d * 6 + h, (0, P)), cc(C_TRI + d * P, P),
                                     start=True, stop=True)
                        close(ins, ("E", tag, g))
                        for i2 in range(2):
                            b = open_(("G", tag, g, i2))
                            for i in range(2):
                                c, h = divmod(4 * g + 2 * i + i2, 6)
                                m, hf = h // 2, h % 2
                                ins = mm(view(ps, b + i * 256, (1, 256)),
                                         view(R, KQ + m * 512 + c * P, (1, P), p0=64 * hf, np_=64),
                                         view(R, KQ + m * 512 + c * P, (256, 2), (1, P), p0=64 * hf, np_=64), start=True, stop=True)
                            close(ins, ("G", tag, g, i2))
                    invert(tag, d, 3, lambda s: view(R, GLT + s * P, (1, P)), "g")
                    for n, c in enumerate((0, 1) if d == 0 else (1, 0)):
                        if n == 1:
                            for w in range(2):
                                b = open_(("KS", tag, w))
                                for m in range(3):
                                    ins = mm(view(ps, b + m * P, (1, P)), view(R, KQ + m * 512 + w * 256 + c * P, (1, P)),
                                             view(hnT, GS + m * P, (1, P)), start=True, stop=True)
                                close(ins, ("KS", tag, w))
                            pe.wait_ge(*at("delta_rhs_ready", tag))
                        b = open_(("U", tag, n))
                        for h in range(6):
                            rhs = view(R, GN + c * 1152 + 768 + h * 64, (1, 64)) if n == 0 else view(R, GR + h * 64, (1, 64))
                            ins = mm(view(ps, b + h * 64, (1, 64)), view(R, XT("g") + (c * 6 + h) * P, (1, P)), rhs, start=True, stop=True)
                        close(ins, ("U", tag, n))
                        pe.wait_ge(*at("bank_read_by_vector", "U", tag, n))
                        b = open_(("PU", tag, n))
                        for h in range(6):
                            ins = mm(view(ps, b + h * 64, (1, 64)), view(R, GPT + (c * 6 + h) * P, (1, P)), view(R, GU + h * 64, (1, 64)),
                                     start=True, stop=True)
                        close(ins, ("PU", tag, n))
                        if n == 0:
                            pe.wait_ge(*at("kd_ready", tag))
                            b = open_(("GS", tag))
                            for h in range(6):
                                ins = mm(view(ps, b + (h // 2) * 64, (1, 64), p0=64 * (h % 2), np_=64),
                                         view(R, GKD + h * 64, (1, 64)), view(R, GU + h * 64, (1, 64)), start=True, stop=True)
                            close(ins, ("GS", tag))
                            pe.wait_ge(*at("bank_read_by_scalar", "GS", tag))

                pe.wait_ge(*at("shifted_ready", L))
                pe.wait_ge(*at("lora_weights_in", L))
                for e in range(2):
                    for w in range(2):
                        b = open_(("lora", L, e, w))
                        for ct in range(2):
                            ins = mm(view(ps, b + ct * S, (1, S)), view(rww, e * 256 + ct * P, (1, P), p0=64 * w, np_=64),
                                     view(R, RF + 6 * S, (1, S), p0=64 * w, np_=64), start=True, stop=True)
                        close(ins, ("lora", L, e, w))
                pe.wait_ge(*at("kk_squares_ready", L))
                b = open_(("kkss", L))
                close(mm(view(ps, b, (1, 512)), cc(C_BLK, P), view(R, RKK2, (1, 512)), start=True, stop=True), ("kkss", L))
                transposes(("vn", L), [view(R, RF + (4 + ct) * S + c * P, (1, P)) for c in range(2) for ct in range(2)], "a")
                pe.wait_ge(*at("bonus_terms_ready", L))
                b = open_(("bonus", L))
                for t in range(T):
                    for ct in range(2):
                        ins = mm(view(ps, b + t * 4 + ct * 2, (1, 2)), view(R, RPR + ct * S + t * P, (1, P)),
                                 view(cst, C_BLK, (64, 2)), start=True, stop=True)
                close(ins, ("bonus", L))
                for d in range(2):
                    tag = ("r", L, d)
                    c1 = d
                    pe.wait_ge(*at("rwkv_factors_ready", L, d))
                    transposes(("BKn", tag), [view(R, RBK + d * 1024 + ct * 512 + w * 256 + c1 * P, (1, P)) for w in range(2) for ct in range(2)], "a")
                    for s in range(8):
                        c, h = divmod(s, 4)
                        ct, hf = h // 2, h % 2
                        b = open_(("M4", tag, s))
                        for w in range(2):
                            ins = mm(view(ps, b + w * 256, (1, 256)),
                                     view(R, RBK + d * 1024 + ct * 512 + w * 256 + c * P, (1, P), p0=64 * hf, np_=64),
                                     view(R, RAR + d * 1024 + ct * 512 + c * P, (256, 2), (1, P), p0=64 * hf, np_=64), start=True, stop=True)
                        close(ins, ("M4", tag, s))
                    invert(tag, d, 2, lambda s: view(R, RM4 + s * 512, (1, P)), "r")
                    for n, c in enumerate((0, 1) if d == 0 else (1, 0)):
                        def from_state(b, h, w):
                            mm(view(ps, b + h * 64, (1, P)), view(R, RAR + d * 1024 + (h // 2) * 512 + w * 256 + c * P, (1, P)),
                               view(hnT, RT0 + (h // 2) * P, (1, P)), start=True, stop=False)

                        def m4(h, w):
                            return view(R, RM4 + (c * 4 + h) * 512 + w * P, (1, P))

                        def vn(h):
                            return view(R, RVN + c * 256 + h * 64, (1, 64))
                        if n == 0:
                            pe.wait_ge(*at("bank_read_by_scalar", "vn", L))
                            pe.wait_ge(*at("bank_read_by_scalar", "BKn", tag))
                        b = open_(("r", tag, n))
                        for h in range(4):
                            o = view(ps, b + h * 64, (1, 64))
                            if n == 1 and h % 2 == 0:
                                from_state(b, h, 0)
                            ins = mm(o, m4(h, 2), vn(h), start=n == 0, stop=n == 0 or h % 2 == 1)
                        close(ins, ("r", tag, n))
                        pe.wait_ge(*at("bank_read_by_scalar", "r", tag, n))
                        b = open_(("Ur", tag, n))
                        for h in range(4):
                            ins = mm(view(ps, b + h * 64, (1, 64)), view(R, XT("r") + (c * 4 + h) * P, (1, P)),
                                     view(R, RRH + h * 64, (1, 64)), start=True, stop=True)
                        close(ins, ("Ur", tag, n))
                        pe.wait_ge(*at("bank_read_by_scalar", "Ur", tag, n))
                        b = open_(("Yr", tag, n))
                        for h in range(4):
                            o = view(ps, b + h * 64, (1, 64))
                            if n == 1 and h % 2 == 0:
                                from_state(b, h, 1)
                            mm(o, m4(h, 1), view(R, RU + h * 64, (1, 64)), start=n == 0, stop=False)
                            ins = mm(o, m4(h, 3), vn(h), start=False, stop=n == 0 or h % 2 == 1)
                        close(ins, ("Yr", tag, n))
                        if n == 0:
                            b = open_(("T0", tag))
                            for h in range(4):
                                o = view(ps, b + (h // 2) * 64, (1, 64), p0=64 * (h % 2), np_=64)
                                mm(o, view(R, RBN + h * 64, (1, 64)), view(R, RU + h * 64, (1, 64)), start=True, stop=False)
                                ins = mm(o, view(R, RBN + 256 + h * 64, (1, 64)), vn(h), start=False, stop=True)
                            close(ins, ("T0", tag))
                            pe.wait_ge(*at("bank_read_by_vector", "T0", tag))
                out_proj(L)

        def full(eng, *key):
            eng.wait_ge(*at("bank_full", *key))
            return bank(key)

        def read(engname, *key):
            new_reader[key] = "bank_read_by_" + engname
            return up("bank_read_by_" + engname, *key)

        @block.scalar
        def _(act):
            def step(ins):
                s, _ = up("scalar_step", C.value.get("scalar_step", 0))
                ins.then_inc(s, 1)
                act.wait_ge(s, C.value["scalar_step"])

            def say(ins, ev):
                ins.then_inc(*ev)
                act.wait_ge(ev[0], C.last)

            A = nc.scalar.activation

            def copy_out(dst, *key, dims=None, n=512, np_=P, scale=1.0):
                b = full(act, *key)
                say(A(dst, view(ps, b, *(dims or ((1, n),)), np_=np_), ACT.Copy, scale=scale), read("scalar", *key))

            def rstd(o, n, scale, eps):
                v = view(sm, o, (1, n))
                step(A(v, v, ACT.Ln, scale=scale, bias=cc(C_EPS + eps)))
                step(A(v, v, ACT.Exp, scale=-0.5))

            def norm(L, which):
                for t in range(T):
                    if which != "mix" or L > 0:
                        act.wait_ge(*at("x_updated", which, L, t, 1))
                    step(A(view(hn, t * D, (1, D)), view(x, t * D, (1, D)), ACT.Square, accum_out=view(sm, SS + t, (1, 1))))
                    rstd(SS + t, 1, 1.0 / D, 0)
                    say(A(view(hn, t * D, (1, D)), view(x, t * D, (1, D)), ACT.Copy, scale=view(sm, SS + t, (1, 1))),
                        up("hn_ready", which, L, t))

            def mlp(L):
                norm(L, "mlp")
                for n in range(8):
                    for m in range(2):
                        act.wait_ge(*at("relu_ready", L, n, m))
                        say(A(view(R, HT + (4 * n + 2 * m) * S, (1, 512)), view(R, RT(m), (1, 512)), ACT.Square),
                            up("hidden_ready", L, n, m))

            def mix_T(L):
                for t in range(T):
                    for q in range(2):
                        copy_out(view(hnT, 4 * q * S + t * P, (S, 4), (1, P)), "mixT", L, t, q, dims=((P, 4), (1, P)))

            def softmax_exp(name, H, shape, width=384, maps=1):
                for i in range(H + 1):
                    if i < H:
                        for mp in range(maps):
                            act.wait_ge(*at("logits_ready", name, i, mp))
                            b = bank(("S", "mla", name[1], i)) if isinstance(name, tuple) else 0
                            for j, (o, n, t) in enumerate(shape):
                                dst = view(R, PB(i, name) + mp * 384 + o, (1, n))
                                src = view(ps, b + o, (1, n)) if isinstance(name, tuple) else dst
                                ins = A(dst, src, ACT.Exp, bias=view(sm, MX(i, mp) + t, (1, 1)), accum_out=view(sm, SU(name, i, mp) + t, (1, 1)))
                                if j == len(shape) - 1:
                                    if name[0] == "mla":
                                        say(ins, read("scalar", "S", "mla", name[1], i))
                                    elif maps == 2:
                                        say(ins, up("diff_exp_ready", i, mp))
                                if not (j == len(shape) - 1) or (maps == 1 and name[0] != "mla"):
                                    if j == len(shape) - 1:
                                        say(ins, up("probs_ready", name, i))
                                    else:
                                        step(ins)
                            if name[0] == "mla":
                                act.sem_inc(up("probs_ready", name, i)[0], 1)
                    if i >= 1:
                        h = i - 1
                        copy_out(view(R, PTB(h, name), (1, width)), "PT", name, h, n=width)

            CAUSAL = ((0, P, 0), (P, S, 1))

            def load(dst, src, *key, slow=False):
                act.dma_start(dst, src, allow_slow_non_contiguous=slow).then_inc(*up(*key, by=16))
            load(cst[:, :], a["const_masks"], "constants_in", "c")
            load(view(x, 0, (D, T), (1, D)), a["x"][0].rearrange("(t p) d -> p t d", p=P), "constants_in", 0)
            load(view(R, TBL, (1, 16), np_=32), a["bias_table"], "constants_in", "t")
            load(view(R, OH, (1, 768), np_=32), a["const_buckets"], "constants_in", "o")
            act.wait_ge(*at("stage_cleared", 0))
            n_loads = 0

            def rload(r0, src, tile=0, w=P):
                load(view(R, STG + tile * P, (1, w), p0=r0, np_=src.shape[0]), src, "row_params_in", "s", tile, r0)
            for nm, r0 in (("norm_mix", CN_MIX), ("norm_mlp", CN_MLP), ("norm_g_2", CN_G2)):
                rload(r0, a[nm].rearrange("l (k p) -> (l k) p", p=P))
            for l in range(2):
                b0 = CL + 31 * l
                rload(b0 + K_MU, a["rwkv_mu_2"][l].rearrange("e (k p) -> (e k) p", p=P))
                rload(b0 + K_W0, a["rwkv_w0_2"][l].rearrange("e (k p) -> (e k) p", p=P))
                rload(b0 + K_A0, a["rwkv_a0_2"][l].rearrange("e (k p) -> (e k) p", p=P))
                rload(b0 + K_KK, a["rwkv_k_k_2"][l].rearrange("(k p) -> k p", p=P))
                rload(b0 + K_KA, a["rwkv_k_a_2"][l].rearrange("(k p) -> k p", p=P))
                rload(b0 + K_RK, a["rwkv_r_k_2"][l].rearrange("(k a) d -> k (a d)", a=2))
                rload(b0 + K_QN, a["mla_q_norm_g_2"][l, 0:P].rearrange("(k p) -> k p", p=P))
                rload(b0 + K_QN + 1, a["mla_q_norm_g_2"][l, P:192].rearrange("(k p) -> k p", p=64), w=64)
                rload(b0 + K_KVN, a["mla_kv_norm_g_2"][l].rearrange("(k p) -> k p", p=P))
                rload(45 * l, a["gdn_conv_2"][l].rearrange("j (m p) -> (j m) p", p=P), tile=1)
            for i, nm in enumerate(("ev_cmp_pos_k", "ev_cmp_pos_v")):
                rload(90 + 16 * i, a[nm][0].rearrange("(j e) d -> j (e d)", e=2), tile=1)

            def brow(o, src, name="row_params_in"):
                n = 1
                for s_ in src.shape:
                    n *= s_
                load(view(rows, o, (1, n)), bass.AP(src.tensor, src.offset, [[0, P], [1, n]]), name, "b", o)
            brow(R_SUB, a["ev_subln"])
            brow(R_GN, a["gdn_norm_g_2"])
            brow(R_LNG, a["rwkv_ln_g_2"])
            brow(R_LNB, a["rwkv_ln_b_2"])
            brow(R_FIN, a["norm_final"])
            brow(R_AL, a["gdn_a_log_2"])
            brow(R_DT, a["gdn_dt_bias_2"])
            for i, nm in enumerate(("ev_lam_q1", "ev_lam_k1", "ev_lam_q2", "ev_lam_k2")):
                brow(R_LAM + 64 * i, a[nm])
            load(view(cmpw, 0, (1, 64)), a["ev_cmp_w2_k"][0], "row_params_in", "w2k")
            load(view(cmpw, 64, (1, 64)), a["ev_cmp_w2_v"][0], "row_params_in", "w2v")
            load(bass.AP(posi, 0, [[T, P], [1, T]]), a["positions_2"].rearrange("b (t p) -> p (b t)", p=P), "row_params_in", 0, slow=True)

            def layer_weights(l):
                load(view(mlaw, 0, (1, 576)), a["mla_w_uq_2"][l, 0:P, :], "mla_weights_in", "a", l)
                load(view(mlaw, 576, (1, 576), np_=64), a["mla_w_uq_2"][l, P:192, :], "mla_weights_in", "b", l)
                load(view(mlaw, 1152, (1, 768)), a["mla_w_ukv_2"][l], "mla_weights_in", l + 2)
                load(view(rww, 0, (256, 2), (1, 256), np_=64), a["rwkv_w2_2"][l].rearrange("e d c -> d e c"), "lora_weights_in", "a", l)
                load(view(rww, 0, (256, 2), (1, 256), p0=64, np_=64), a["rwkv_a2_2"][l].rearrange("e d c -> d e c"), "lora_weights_in", l + 2)
            layer_weights(0)
            act.wait_ge(*at("constants_in", "o"))
            act.wait_ge(*at("bias_rows_ready", 0))
            act.dma_start(scratch.ap().rearrange("h (q x) -> h q x", q=P), view(R, FR, (0, P), (1, 384), np_=16))\
                .then_inc(*up("bias_rows_stored", 0, by=16))
            act.wait_ge(*at("bias_rows_stored", 0))
            for h in range(16):
                act.dma_start(view(R, BT + h * S, (1, S)), bass.AP(scratch, h * P * 384 + 127, [[383, P], [1, S]]))\
                    .then_inc(*up("bias_tiles_in", h, by=16))

            norm(0, "mix")
            for m in range(2):
                copy_out(view(R, QT + m * 512, (1, 512)), "q", m)
            copy_out(view(R, KCVC, (1, 512)), "kcvc")
            copy_out(view(R, KST, (1, S)), "ks", n=S)
            for t in range(T):
                copy_out(view(R, VS + t * P, (1, P)), "vs", t, n=P)
            copy_out(view(R, KST + S, (1, S)), "kw", n=S)
            for kind in range(2):
                for g in range(2):
                    for half in range(2):
                        ins = A(view(R, KD + kind * 512 + g * S, (1, S), p0=64 * half, np_=64),
                                view(R, KST + kind * S, (1, S), p0=64 * g, np_=64), ACT.Copy)
                        if (kind, g, half) == (1, 1, 1):
                            say(ins, up("kdup_ready", 0))
                        else:
                            step(ins)
            for t in range(T):
                b = full(act, "vwg", t)
                step(A(view(R, VW + t * P, (1, P)), view(ps, b, (1, P)), ACT.Copy))
                say(A(view(R, GT + t * 24, (1, 24)), view(ps, b + P, (1, 24)), ACT.Exp, scale=-1.0), read("scalar", "vwg", t))
            for nm, base in (("dq", DQ), ("dk", DK)):
                for m in range(2):
                    copy_out(view(R, base + m * 512, (1, 512)), nm, m)
            for t in range(T):
                copy_out(view(R, DV + t * 512, (1, 512)), "dv", t)
            for i in range(2):
                act.wait_ge(*at("gelu_arg_ready", i))
                say(A(view(R, GE + 60 + 30 * i, (1, 30)), view(R, GE + 60 + 30 * i, (1, 30)), ACT.Exp, scale=2 * math.sqrt(2 / math.pi)),
                    up("gelu_exp_ready", i))
            act.wait_ge(*at("lam_sums_ready", 0))
            say(A(view(sm, LM, (1, 2)), view(sm, LM, (1, 2)), ACT.Exp), up("lam_exp_ready", 0))
            b = full(act, "cmpkv")
            for half in range(2):
                step(A(view(R, KCT, (1, 30), p0=64 * half, np_=64), view(ps, b, (1, 30), np_=64), ACT.Copy))
            say(A(view(R, VCN, (1, 128), np_=15), view(ps, b + 64, (1, 128), np_=15), ACT.Copy), read("scalar", "cmpkv"))
            act.sem_inc(up("cmp_kv_ready", 0)[0], 1)
            act.wait_ge(*at("vbd_cleared", 0))
            for h in range(8):
                act.dma_start(view(R, VBD + h * 64, (1, 64), p0=16 * h, np_=15), view(R, VCN + (h // 4) * 64, (1, 64), np_=15))\
                    .then_inc(*up("vbd_ready", 0, h, by=16))
            softmax_exp("sel", 8, CAUSAL)
            softmax_exp("win", 8, CAUSAL)
            act.wait_ge(*at("cmp_logits_ready", 0))
            say(A(view(R, PC, (1, 256)), view(R, PC, (1, 256)), ACT.Exp), up("cmp_exp_ready", 0))
            copy_out(view(R, PCT, (1, 256)), "PTc", n=256)
            for h in range(5):
                if h < 4:
                    for mp in range(2):
                        act.wait_ge(*at("logits_ready", "diff", h, mp))
                        for o, n, t in CAUSAL:
                            v = view(R, PB(h) + mp * 384 + o, (1, n))
                            ins = A(v, v, ACT.Exp, bias=view(sm, MX(h, mp) + t, (1, 1)), accum_out=view(sm, SU("diff", h, mp) + t, (1, 1)))
                            if t == 0:
                                step(ins)
                            else:
                                say(ins, up("diff_exp_ready", h, mp))
                if h >= 1:
                    copy_out(view(R, PTB(h - 1), (1, 384)), "PT", "diff", h - 1, n=384)
            act.wait_ge(*at("subln_ss_ready", 0))
            rstd(SB, 8, 1.0 / 128, 0)
            act.sem_inc(up("subln_rstd_ready", 0)[0], 1)
            mix_T(0)
            mlp(0)

            norm(1, "mix")
            for n in range(4):
                for m in range(2):
                    copy_out(view(R, MQ + (4 * n + 2 * m) * S, (1, 512)), "mqk", n, m)
            for n in range(2):
                for t in range(T):
                    copy_out(view(R, MV + t * D + 512 * n, (1, 512)), "mv", n, t)
            softmax_exp("moba", 16, CAUSAL)
            mix_T(1)
            mlp(1)

            norm(2, "end")

            for L in (2, 3):
                norm(L, "mix")
                if L == 2:
                    brow(R_FIN, a["final_norm_g_2"], "final_gain_in")
                for n in range(2):
                    for t in range(T):
                        b = full(act, "gate", L, n, t)
                        o = GATE + t * D + 512 * n
                        step(A(view(R, MIXB + t * D + 512 * n, (1, 512)), view(ps, b, (1, 512)), ACT.Exp, scale=-1.0))
                        say(A(view(R, o, (1, 512)), view(ps, b, (1, 512)), ACT.Copy), read("scalar", "gate", L, n, t))
                for n, m in ((0, 0), (0, 1), (1, 0), (1, 1), (2, 0)):
                    k = 1 if n == 2 else 2
                    copy_out(view(R, GP + (4 * n + 2 * m) * 260 + 2, (260, k), (1, S)), "gqkv", L, n, m, dims=((S, k), (1, S)))
                for t in range(T):
                    copy_out(view(R, LOW + t * 376, (1, 376)), "low", L, t, n=376)
                for m in range(4):
                    k = 1 if m == 3 else 2
                    copy_out(view(R, RP + 2 * m * 258 + 1, (258, k), (1, S)), "rw", L, m, dims=((S, k), (1, S)))
                act.sem_inc(up("low_ready", L)[0], 1)
                for t in range(T):
                    for w, (o, n) in enumerate(((24, 192), (216, 128))):
                        step(A(view(R, CQN + t * 320, (1, n)), view(R, LOW + t * 376 + o, (1, n)), ACT.Square,
                               accum_out=view(sm, SS + 2 * w + t, (1, 1))))
                rstd(SS, 2, 1.0 / 192, 0)
                rstd(SS + 2, 2, 1.0 / 128, 0)
                for t in range(T):
                    for w, (o, n, q) in enumerate(((24, 192, 0), (216, 128, 192))):
                        ins = A(view(R, CQN + t * 320 + q, (1, n)), view(R, LOW + t * 376 + o, (1, n)), ACT.Copy,
                                scale=view(sm, SS + 2 * w + t, (1, 1)))
                        if t == 1 and w == 1:
                            say(ins, up("latents_ready", L))
                        else:
                            step(ins)
                if L == 2:
                    act.wait_ge(*at("angles_ready", 0))
                    say(A(view(sm, TRG, (1, 64)), view(sm, TRG, (1, 64)), ACT.Sin), up("trig_ready", 0))
                for t in range(T):
                    for hf in range(2):
                        copy_out(view(R, QN + t * 576 + hf * 288, (1, 288)), "uq", L, t, hf, n=288, scale=96 ** -0.5)
                    for hf in range(2):
                        copy_out(view(R, KV + t * 768 + hf * 384, (1, 384)), "ukv", L, t, hf, n=384)
                for t in range(T):
                    ins = A(view(R, KN + t * 576, (96, 6), (1, 64)), view(R, KV + t * 768, (P, 6), (1, 64)), ACT.Copy)
                    if t == 0:
                        step(ins)
                    else:
                        say(ins, up("uprojected", L))
                for h in range(6):
                    copy_out(view(R, QKT + h * 512, (1, 512), np_=96), "qkT", L, h, np_=96)
                softmax_exp(("mla", L), 6, ((0, S, 0), (S, S, 1)), width=512)

                act.wait_ge(*at("conv_sum_ready", L))
                say(A(view(R, GP, (1, 2304)), view(R, GC, (1, 2304)), ACT.Exp, scale=-1.0), up("silu_exp_ready", L))
                for t in range(T):
                    for w in range(3):
                        copy_out(view(R, GN + t * 1152 + w * 384, (1, 384)), "gn", L, t, w, n=384)
                step(A(view(R, GP, (768, 2), (1, 768)), view(R, GN, (1152, 2), (1, 768)), ACT.Square))
                act.sem_inc(up("qk_squares_ready", L)[0], 1)
                act.wait_ge(*at("dt_ready", L))
                step(A(view(sm, GAB, (1, 24)), view(sm, GAB, (1, 24)), ACT.Exp))
                step(A(view(sm, GAB, (1, 24)), view(sm, GAB, (1, 24)), ACT.Ln, bias=cc(C_EPS + 2)))
                step(A(view(sm, GBT, (12, 2), (1, 12)), view(R, LOW + 12, (376, 2), (1, 12)), ACT.Exp, scale=-1.0))
                say(A(view(sm, GAL, (1, 12)), view(rows, R_AL + 12 * (L - 2), (1, 12)), ACT.Exp), up("softplus_ready", L))
                act.wait_ge(*at("qk_ss_ready", L))
                rstd(SS, 24, 1.0, 0)
                act.sem_inc(up("qk_rstd_ready", L)[0], 1)
                for m in range(3):
                    copy_out(view(R, KQ + m * 512, (1, 512)), "kq", L, m)
                act.wait_ge(*at("cum_ready", L))
                step(A(view(sm, GGA, (12, 2), (1, 12)), view(sm, GCU, (24, 2), (1, 12)), ACT.Exp))
                say(A(view(sm, GKF, (12, 2), (1, 12)), view(sm, GKF, (12, 2), (1, 12)), ACT.Exp), up("decay_exp_ready", L))
                for d in range(2):
                    tag = ("g", L, d)
                    for g in range(3):
                        act.wait_ge(*at("exponent_ready", tag, g))
                        say(A(view(R, GE_(g), (1, 512)), view(R, GE_(g), (1, 512)), ACT.Exp), up("decay_matrix_ready", tag, g))
                    for g in range(3):
                        copy_out(view(R, XX("g") + g * 512, (1, 512)), "X0", tag, g)
                    b = full(act, "GS", tag)
                    step(A(view(hnT, GS, (P, 3), (1, 64), np_=64), view(ps, b, (64, 3), (1, 64), np_=64), ACT.Copy))
                    say(A(view(hnT, GS + 64, (P, 3), (1, 64), p0=64, np_=64), view(ps, b, (64, 3), (1, 64), p0=64, np_=64), ACT.Copy),
                        read("scalar", "GS", tag))
                act.wait_ge(*at("gdn_ss_ready", L))
                rstd(SS, 12, 1.0 / 64, 0)
                act.sem_inc(up("gdn_rstd_ready", L)[0], 1)

                act.wait_ge(*at("tanh_arg_ready", L))
                say(A(view(R, RF + 6 * S, (1, S), np_=64), view(R, RF + 6 * S, (1, S), np_=64), ACT.Exp, scale=2.0), up("tanh_exp_ready", L))
                for e in range(2):
                    for w, (dst, k) in enumerate(((RSW, K_W0), (RSA, K_A0))):
                        b = full(act, "lora", L, e, w)
                        for ct in range(2):
                            ins = A(view(R, dst + e * 512 + ct * S, (1, S)), view(ps, b + ct * S, (1, S)), ACT.Exp, scale=-1.0,
                                    bias=view(sm, NB + (0 if w == 0 else 4) + 2 * e + ct, (1, 1)))
                            if ct == 0:
                                step(ins)
                            else:
                                say(ins, read("scalar", "lora", L, e, w))
                b = full(act, "kkss", L)
                step(A(view(R, RKK2, (1, 512)), view(ps, b, (1, 512)), ACT.Ln, bias=cc(C_EPS)))
                say(A(view(R, RKK2, (1, 512)), view(R, RKK2, (1, 512)), ACT.Exp, scale=-0.5), read("scalar", "kkss", L))
                copy_out(view(R, RVN, (1, 512)), "vn", L)
                act.wait_ge(*at("rwkv_cum_ready", L))
                step(A(view(R, REP, (1, 1024)), view(R, RCM, (1, 1024)), ACT.Exp))
                step(A(view(R, RCL, (1, 1024)), view(R, RCL, (1, 1024)), ACT.Exp))
                step(A(view(sm, RE, (1, 4)), view(sm, RE, (1, 4)), ACT.Exp))
                say(A(view(R, RCM, (1, 1024)), view(R, RCM, (1, 1024)), ACT.Exp, scale=-1.0), up("rwkv_exp_ready", L))
                for d in range(2):
                    tag = ("r", L, d)
                    copy_out(view(R, RBN, (1, 512)), "BKn", tag)
                    for g in range(2):
                        copy_out(view(R, XX("r") + g * 512, (1, 512)), "X0", tag, g)
                    for n in range(2):
                        copy_out(view(R, RRH, (1, 256)), "r", tag, n, n=256, scale=-1.0)
                        copy_out(view(R, RU, (1, 256)), "Ur", tag, n, n=256)
                act.wait_ge(*at("rwkv_var_ready", L))
                rstd(SS, 8, 1.0 / 64, 1)
                act.sem_inc(up("rwkv_rstd_ready", L)[0], 1)
                if L == 2:
                    layer_weights(1)
                mix_T(L)
            norm(4, "fin")

        @block.vector
        def _(dve):
            V = nc.vector

            def step(ins):
                s, _ = up("vector_step", C.value.get("vector_step", 0))
                ins.then_inc(s, 1)
                dve.wait_ge(s, C.value["vector_step"])

            def say(ins, ev):
                ins.then_inc(*ev)
                dve.wait_ge(ev[0], C.last)

            def tt(o, p_, q, op):
                step(V.tensor_tensor(o, p_, q, op))

            def ts(o, i, s1, s2, op0, op1=None):
                step(V.tensor_scalar(o, i, s1, s2, op0, op1) if op1 is not None else V.tensor_scalar(o, i, s1, None, op0))

            def recip(o, i):
                step(V.reciprocal(o, i))

            def signal(*key):
                dve.sem_inc(up(*key)[0], 1)

            def normed_T(L, which):
                base = {"mix": (CN_MIX, CN_MIX + 8, CN_G2, CN_G2 + 8)[L] if L < 4 else 0, "mlp": CN_MLP + 8 * L}[which]
                for t in range(T):
                    for q in range(2):
                        key = ("hnT", which, L, t, q)
                        b = full(dve, *key)
                        say(V.tensor_tensor(view(hnT, 4 * q * S + t * P, (S, 4), (1, P)), view(ps, b, (P, 4), (1, P)),
                                            view(cols, base + 4 * q, (1, 4), (0, P)), MUL), read("vector", *key))

            def residual(kind, L, nxt, nL):
                for t in range(T):
                    for half in range(2):
                        key = (kind, L, half, t) if kind == "o" else (kind, L, 2 * t + half)
                        b = full(dve, *key)
                        v = view(x, t * D + 512 * half, (1, 512))
                        say(V.tensor_tensor(v, view(ps, b, (1, 512)), v, ADD), read("vector", *key))
                        signal("x_updated", nxt, nL, t, half)

            def mlp(L):
                normed_T(L, "mlp")
                for n in range(8):
                    for m in range(2):
                        b = full(dve, "h", L, n, m)
                        if n > 0:
                            dve.wait_ge(*at("hidden_ready", L, n - 1, m))
                        say(V.tensor_scalar(view(R, RT(m), (1, 512)), view(ps, b, (1, 512)), 0.0, None, MAX), read("vector", "h", L, n, m))
                        signal("relu_ready", L, n, m)
                residual("y", L, "mix" if L == 0 else "end", L + 1)

            def logits(name, h, mp, key, bh):
                b = full(dve, *key)
                for o, n, t, k0 in ((0, P, 0, P), (P, S, 1, 0)):
                    v = view(R, PB(h) + mp * 384 + o, (1, n))
                    step(V.tensor_tensor(v, view(ps, b + o, (1, n)), view(R, BT + bh * S + k0, (1, n)), ADD))
                    step(V.tensor_reduce(view(sm, MX(h, mp) + t, (1, 1)), v, AX.X, MAX))
                    if t == 0:
                        step(V.tensor_scalar(v, v, 0.125, None, MUL))
                    else:
                        say(V.tensor_scalar(v, v, 0.125, None, MUL), read("vector", *key))
                ts(view(sm, MX(h, mp), (1, 2)), view(sm, MX(h, mp), (1, 2)), -0.125, None, MUL)
                signal("logits_ready", name, h, mp)

            def head_out(name, H, dst, coef, first, per=8, vw=64, groups=None):
                for gq in groups or range((H + per - 1) // per):
                    n = min(per, H - gq * per)
                    for t in range(T):
                        b = full(dve, "O", name, gq, t)
                        o = dst(t) + gq * per * vw
                        src = view(ps, b, (vw, n), (1, vw))
                        cf = coef(t, gq * per, n)
                        if first:
                            say(V.tensor_tensor(view(R, o, (vw, n), (1, vw)), src, cf, MUL), read("vector", "O", name, gq, t))
                        else:
                            say(V.tensor_tensor(view(hn, 0, (vw, n), (1, vw)), src, cf, MUL), read("vector", "O", name, gq, t))
                            tt(view(R, o, (vw, n), (1, vw)), view(R, o, (vw, n), (1, vw)), view(hn, 0, (vw, n), (1, vw)), ADD)

            step(V.memset(view(R, STG, (1, 2 * P)), 0.0))
            signal("stage_cleared", 0)
            dve.wait_ge(*at("constants_in", "o"))
            b = full(dve, "cols")
            say(V.tensor_copy(cols[:, :], view(ps, b, (1, 2 * P))), read("vector", "cols"))
            b = full(dve, "bias")
            say(V.scalar_tensor_tensor(view(R, FR, (1, 384), np_=16), view(ps, b, (1, 384), np_=16), 8.0,
                                       view(R, OH + 384, (1, 384), np_=16), MUL, ADD), read("vector", "bias"))
            signal("bias_rows_ready", 0)
            dve.wait_ge(*at("row_params_in", 0))
            for i in range(2):
                tt(view(R, GE, (1, 64)), view(rows, R_LAM + 128 * i, (1, 64)), view(rows, R_LAM + 128 * i + 64, (1, 64)), MUL)
                step(V.tensor_reduce(view(sm, LM + i, (1, 1)), view(R, GE, (1, 64)), AX.X, ADD))
            signal("lam_sums_ready", 0)
            normed_T(0, "mix")
            dve.wait_ge(*at("bank_read_by_scalar", "kcvc"))
            for i in range(2):
                for g in range(2):
                    for par in range(2):
                        tt(view(R, BLK + i * 480 + g * 240, (15, 16), (1, 15), p0=64 * par, np_=64),
                           view(R, KCVC + i * S + par, (2, 16), (16, 15), p0=64 * g, np_=64),
                           view(cols, CB_POS + 16 * i, (1, 16), (0, 15), p0=64 * par, np_=64), ADD)
            signal("cmp_blocks_ready", 1)
            dve.wait_ge(*at("bank_read_by_scalar", "vwg", 1))
            ts(view(R, GT, (1, 48)), view(R, GT, (1, 48)), 1.0, None, ADD)
            recip(view(R, GT, (1, 48)), view(R, GT, (1, 48)))
            for i in range(2):
                h_, u_ = view(R, GE + 30 * i, (1, 30)), view(R, GE + 60 + 30 * i, (1, 30))
                b = full(dve, "hid", i)
                say(V.tensor_copy(h_, view(ps, b, (1, 30))), read("vector", "hid", i))
                tt(u_, h_, h_, MUL)
                ts(u_, u_, 0.044715, 1.0, MUL, ADD)
                tt(u_, u_, h_, MUL)
                ts(u_, u_, 20.0, None, MIN)
                signal("gelu_arg_ready", i)
            for i in range(2):
                h_, u_ = view(R, GE + 30 * i, (1, 30)), view(R, GE + 60 + 30 * i, (1, 30))
                dve.wait_ge(*at("gelu_exp_ready", i))
                ts(u_, u_, 1.0, None, ADD)
                recip(u_, u_)
                ts(u_, u_, -1.0, 1.0, MUL, ADD)
                tt(view(R, HID + 30 * i, (1, 30)), u_, h_, MUL)
            signal("cmp_hidden_ready", 1)
            dve.wait_ge(*at("lam_exp_ready", 0))
            tt(view(sm, LM, (1, 1)), view(sm, LM + 1, (1, 1)), view(sm, LM, (1, 1)), SUB)
            ts(view(sm, LM, (1, 1)), view(sm, LM, (1, 1)), -LAM_INIT, None, ADD)
            step(V.memset(view(R, VBD, (1, 512)), 0.0))
            signal("vbd_cleared", 0)
            dve.wait_ge(*at("bias_tiles_in", 15))

            def softmax(name, H, bh, between=None):
                for h in range(H):
                    if between and h == 11:
                        between()
                    if h >= 3:
                        dve.wait_ge(*at("bank_full", "PT", name, h - 3))
                    logits(name, h, 0, ("S", name, h), bh(h))

            for gi, nm in ((1, "sel"), (2, "win")):
                softmax(nm, 8, lambda h: h)
                dve.wait_ge(*at("probs_ready", nm, 7))
                su = view(sm, SU(nm, 0, 0), (2, 8), (1, 2))
                recip(su, su)
                tt(su, su, view(R, GT + gi * 8, (1, 8), (24, 2)), MUL)
                head_out(nm, 8, lambda t: MIX(0) + t * D,
                         lambda t, h0, n, nm=nm: view(sm, SU(nm, 0, 0) + t, (2, n), (0, 64)), nm == "sel")
            for par in range(2):
                b = full(dve, "Sc", par)
                for t in range(T):
                    nv, k0 = (15, 31) if t == 1 else (7, 159)
                    pc = PC + t * P + par * 16
                    if par == 0:
                        step(V.memset(view(R, PC + t * P, (1, P)), 8 * NEG))
                    ins = V.tensor_tensor(view(R, pc, (32, 4), (1, nv)), view(ps, b + t * 64, (16, 4), (1, nv)),
                                          view(R, BT + par * S + k0, (2 * S, 4), (16, nv)), ADD)
                    if t == 0:
                        step(ins)
                    else:
                        say(ins, read("vector", "Sc", par))
            allp = view(R, PC, (16, 16), (1, 16))
            mx = view(sm, CM, (1, 16))
            step(V.tensor_reduce(mx, allp, AX.X, MAX))
            tt(allp, allp, view(sm, CM, (1, 16), (0, 16)), SUB)
            ts(view(R, PC, (1, 256)), view(R, PC, (1, 256)), 0.125, None, MUL)
            signal("cmp_logits_ready", 0)
            dve.wait_ge(*at("cmp_exp_ready", 0))
            step(V.memset(view(R, PC + 15, (16, 16)), 0.0))
            signal("cmp_probs_ready", 0)
            step(V.tensor_reduce(mx, allp, AX.X, ADD))
            recip(mx, mx)
            for t in range(T):
                tt(view(sm, CM + 8 * t, (1, 8)), view(sm, CM + 8 * t, (1, 8)), view(R, GT + 24 * t, (1, 8)), MUL)
                ts(view(sm, CM + 8 * t, (1, 8)), view(sm, CM + 8 * t, (1, 8)), cc(C_ROWOK + t), None, MUL)
                b = full(dve, "Oc", t)
                say(V.tensor_tensor(view(hn, 0, (64, 8), (1, 64)), view(ps, b, (64, 8), (1, 64)),
                                    view(sm, CM + 8 * t, (1, 8), (0, 64)), MUL), read("vector", "Oc", t))
                tt(view(R, MIX(0) + t * D, (1, 512)), view(R, MIX(0) + t * D, (1, 512)), view(hn, 0, (1, 512)), ADD)
            for i in range(5):
                if i < 4:
                    if i >= 3:
                        dve.wait_ge(*at("bank_full", "PT", "diff", i - 3))
                    for mp in range(2):
                        logits("diff", i, mp, ("S", "diff", i, mp), 8 + i)
                if i >= 1:
                    h = i - 1
                    dve.wait_ge(*at("diff_exp_ready", h, 1))
                    c0, c1 = SU("diff", h, 0), SU("diff", h, 1)
                    recip(view(sm, c0, (1, 2)), view(sm, c0, (1, 2)))
                    recip(view(sm, c1, (1, 2)), view(sm, c1, (1, 2)))
                    ts(view(sm, c1, (1, 2)), view(sm, c1, (1, 2)), view(sm, LM, (1, 1)), None, MUL)
                    for o, n, t in ((0, P, 0), (P, S, 1)):
                        p0_, p1_ = view(R, PB(h) + o, (1, n)), view(R, PB(h) + 384 + o, (1, n))
                        ts(p1_, p1_, view(sm, c1 + t, (1, 1)), None, MUL)
                        step(V.scalar_tensor_tensor(p0_, p0_, view(sm, c0 + t, (1, 1)), p1_, MUL, ADD))
                    signal("diff_probs_ready", "diff", h)
            for t in range(T):
                b = full(dve, "O", "diff", 0, t)
                say(V.tensor_copy(view(R, MIX(0) + t * D + 512, (1, 512)), view(ps, b, (1, 512))), read("vector", "O", "diff", 0, t))
                v = view(R, MIX(0) + t * D + 512, (1, 512))
                tt(view(hn, 0, (1, 512)), v, v, MUL)
                step(V.tensor_reduce(view(sm, SB + 4 * t, (1, 4)), view(hn, 0, (P, 4), (1, P)), AX.X, ADD))
            signal("subln_ss_ready", 0)
            dve.wait_ge(*at("subln_rstd_ready", 0))
            for t in range(T):
                v = view(R, MIX(0) + t * D + 512, (P, 4), (1, P))
                tt(v, v, view(sm, SB + 4 * t, (1, 4), (0, P)), MUL)
                ts(v, v, 1.0 - LAM_INIT, None, MUL)
                tt(v, v, view(rows, R_SUB, (0, 4), (1, P)), MUL)
                signal("mix_ready", 0, t)
            residual("o", 0, "mlp", 0)
            mlp(0)

            normed_T(1, "mix")
            def moba_out(g):
                dve.wait_ge(*at("probs_ready", "moba", 8 * g + 7))
                su = view(sm, SU("moba", 8 * g, 0), (1, 16))
                recip(su, su)
                head_out("moba", 16, lambda t: MIX(1) + t * D,
                         lambda t, h0, n: view(sm, SU("moba", 0, 0) + 2 * h0 + t, (2, n), (0, 64)), True, groups=(g,))
            softmax("moba", 16, lambda h: h, lambda: moba_out(0))
            moba_out(1)
            for t in range(T):
                signal("mix_ready", 1, t)
            residual("o", 1, "mlp", 1)
            mlp(1)
            for t in range(T):
                dve.wait_ge(*at("hn_ready", "end", 2, t))
                tt(view(x, t * D, (1, D)), view(hn, t * D, (1, D)), view(rows, R_FIN, (1, D)), MUL)
                signal("x_updated", "mix", 2, t, 1)

            step(V.tensor_copy(view(sm, PF, (1, 2)), bass.AP(posi, 0, [[T, P], [1, T]])))
            for t in range(T):
                for w, ph in enumerate((0.25, 0.0)):
                    v = view(sm, TRG + w * 32 + t * 16, (1, 16))
                    k_ = view(sm, TRK, (1, 16))
                    ts(v, cc(C_FRQ, 16), view(sm, PF + t, (1, 1)), None, MUL)
                    ts(k_, v, 1.0 / (2 * math.pi), ph, MUL, ADD)
                    ts(k_, k_, 12582912.0, None, ADD)
                    ts(k_, k_, -12582912.0, None, ADD)
                    step(V.scalar_tensor_tensor(v, k_, -6.28125, v, MUL, ADD))
                    step(V.scalar_tensor_tensor(v, k_, -(2 * math.pi - 6.28125), v, MUL, ADD))
                    ts(v, v, ph * 2 * math.pi, 3.1415925, ADD, MIN)
                    ts(v, v, -3.1415925, None, MAX)
            signal("angles_ready", 0)

            def invert(tag, d, ngroups, LTs, st):
                lt, stp = LTs
                for g in range(ngroups):
                    v = view(R, XT(st) + g * 512, (P, 4), (1, P))
                    tt(v, view(R, lt + 4 * g * stp, (stp, 4), (1, P)), view(cst, C_M1 + d * P, (0, 4), (1, P)), MUL)
                    tt(v, view(cst, C_ID, (0, 4), (1, P)), v, SUB)
                    signal("inverse_seed_ready", tag, g)
                for n, m in enumerate(LEVELS):
                    e = 0 if d == 0 else m
                    l = m - e
                    np2 = P // (2 * m)
                    for g in range(ngroups):
                        key = ("Y", tag, n, g)
                        b = full(dve, *key)
                        say(V.tensor_tensor(view(R, YY(st) + g * 512, (P, 4), (1, P)), view(ps, b, (P, 4), (1, P)),
                                            view(cst, C_LV + (d * len(LEVELS) + n) * P, (0, 4), (1, P)), MUL), read("vector", *key))
                    for g in range(ngroups):
                        key = ("Z", tag, n, g)
                        b = full(dve, *key)
                        if m < 64:
                            v = view(R, XX(st) + g * 512 + e, (2 * m, 4 * np2), (1, m))
                            tt(v, v, view(ps, b, (m, 4 * np2), (1, m)), SUB)
                        v = view(R, XT(st) + g * 512 + l, (2 * m, 4 * np2), (1, m))
                        say(V.tensor_tensor(v, v, view(ps, b + 256, (m, 4 * np2), (1, m)), SUB), read("vector", *key))

            for L in (2, 3):
                lc = CL + 31 * (L - 2)

                def col(k, n=1, p0=0, np_=P):
                    return view(cols, lc + k, (1, n), p0=p0, np_=np_)
                if L == 3:
                    dve.wait_ge(*at("x_updated", "mix", L, 1, 1))
                step(V.memset(view(R, GP, (260, 9), (1, 2)), 0.0))
                step(V.memset(view(R, GP + 258, (260, 9), (1, 2)), 0.0))
                step(V.memset(view(R, RP, (257, 2), (258, 7)), 0.0))
                normed_T(L, "mix")
                dve.wait_ge(*at("bank_read_by_scalar", "gate", L, 1, 1))
                e_ = view(R, MIXB, (1, 2048))
                ts(e_, e_, 1.0, None, ADD)
                recip(e_, e_)
                tt(view(R, GATE, (1, 2048)), view(R, GATE, (1, 2048)), e_, MUL)
                for t in range(T):
                    b = full(dve, "cT", L, t)
                    ts(view(R, CT + t * P, (1, P)), view(ps, b, (1, P)), col(K_QN), None, MUL)
                    ts(view(R, CT + 256 + t * P, (1, P), np_=64), view(ps, b + P, (1, P), np_=64), col(K_QN + 1, np_=64), None, MUL)
                    say(V.tensor_scalar(view(R, CT + 512 + t * P, (1, P)), view(ps, b + 2 * P, (1, P)), col(K_KVN), None, MUL),
                        read("vector", "cT", L, t))
                    signal("latents_T_ready", L, t)
                dve.wait_ge(*at("uprojected", L))
                dve.wait_ge(*at("trig_ready", 0))
                for t in range(T):
                    cs, sn = TRG + t * 16, TRG + 32 + t * 16
                    for o, hs, H_ in ((QN + t * 576 + 64, 96, 6), (LOW + t * 376 + 344, 96, 1)):
                        x1, x2 = view(R, o, (hs, H_), (1, 16)), view(R, o + 16, (hs, H_), (1, 16))
                        tc = [view(R, RTM + 96 * i, (16, H_), (1, 16)) for i in range(4)]
                        c_, s_ = view(sm, cs, (0, H_), (1, 16)), view(sm, sn, (0, H_), (1, 16))
                        tt(tc[0], x1, c_, MUL)
                        tt(tc[1], x2, s_, MUL)
                        tt(tc[2], x2, c_, MUL)
                        tt(tc[3], x1, s_, MUL)
                        tt(x1, tc[0], tc[1], SUB)
                        tt(x2, tc[2], tc[3], ADD)
                    step(V.tensor_copy(view(R, KN + t * 576 + 64, (96, 6), (1, 32)), view(R, LOW + t * 376 + 344, (0, 6), (1, 32))))
                signal("rope_ready", L)
                name = ("mla", L)
                for h in range(6):
                    b = full(dve, "S", "mla", L, h)
                    step(V.tensor_reduce(view(sm, MX(h, 0), (1, 2)), view(ps, b, (S, 2), (1, S)), AX.X, MAX))
                    ts(view(sm, MX(h, 0), (1, 2)), view(sm, MX(h, 0), (1, 2)), -1.0, None, MUL)
                    if h >= 3:
                        dve.wait_ge(*at("bank_full", "PT", name, h - 3))
                    signal("logits_ready", name, h, 0)
                dve.wait_ge(*at("probs_ready", name, 5))
                su = view(sm, SU(name, 0, 0), (1, 12))
                recip(su, su)
                head_out(name, 6, lambda t: MIXB + t * D + 384, lambda t, h0, n: view(sm, SU(name, 0, 0) + t, (2, n), (0, 64)), True)

                for m in range(9):
                    wcol = [view(cols, CB_CONV + 45 * (L - 2) + 9 * j + m, (1, 1)) for j in range(5)]
                    o = view(R, GC + m * S, (1, S))
                    ts(o, view(R, GP + m * 260, (1, S)), wcol[0], None, MUL)
                    for j in range(1, 5):
                        step(V.scalar_tensor_tensor(o, view(R, GP + m * 260 + j, (1, S)), wcol[j], o, MUL, ADD))
                signal("conv_sum_ready", L)
                dve.wait_ge(*at("silu_exp_ready", L))
                e_ = view(R, GP, (1, 2304))
                ts(e_, e_, 1.0, None, ADD)
                recip(e_, e_)
                tt(view(R, GC, (1, 2304)), view(R, GC, (1, 2304)), e_, MUL)
                signal("conv_ready", L)
                dtv = view(sm, GSP, (12, 2), (1, 12))
                tt(dtv, view(R, LOW, (376, 2), (1, 12)), view(rows, R_DT + 12 * (L - 2), (0, 2), (1, 12)), ADD)
                neg = view(sm, GAB, (1, 24))
                ts(neg, view(sm, GSP, (1, 24)), -1.0, None, MUL)
                tt(neg, neg, view(sm, GSP, (1, 24)), MIN)
                ts(view(sm, GSP, (1, 24)), view(sm, GSP, (1, 24)), 0.0, None, MAX)
                signal("dt_ready", L)
                dve.wait_ge(*at("softplus_ready", L))
                tt(view(sm, GSP, (1, 24)), view(sm, GSP, (1, 24)), neg, ADD)
                ts(view(sm, GBT, (1, 24)), view(sm, GBT, (1, 24)), 1.0, None, ADD)
                recip(view(sm, GBT, (1, 24)), view(sm, GBT, (1, 24)))
                tt(view(sm, GG, (12, 2), (1, 12)), dtv, view(sm, GAL, (0, 2), (1, 12)), MUL)
                ts(view(sm, GG, (1, 24)), view(sm, GG, (1, 24)), -1.0, None, MUL)
                signal("decay_ready", L)
                dve.wait_ge(*at("qk_squares_ready", L))
                step(V.tensor_reduce(view(sm, SS, (1, 24)), view(R, GP, (64, 24), (1, 64)), AX.X, ADD))
                signal("qk_ss_ready", L)
                dve.wait_ge(*at("qk_rstd_ready", L))
                ts(view(sm, SS, (12, 2), (1, 6)), view(sm, SS, (12, 2), (1, 6)), 0.125, None, MUL)
                for t in range(T):
                    v = view(R, GN + t * 1152, (64, 12), (1, 64))
                    tt(v, v, view(sm, SS + 12 * t, (1, 12), (0, 64)), MUL)
                signal("qk_normed", L)
                b = full(dve, "cum", L)
                say(V.tensor_copy(view(sm, GCU, (1, 48)), view(ps, b, (1, 48))), read("vector", "cum", L))
                tt(view(sm, GKF, (12, 2), (1, 12)), view(sm, GCU + 12, (24, 2), (1, 12)), view(sm, GCU, (24, 2), (1, 12)), SUB)
                signal("cum_ready", L)
                dve.wait_ge(*at("decay_exp_ready", L))
                for d in range(2):
                    tag = ("g", L, d)
                    for g in range(3):
                        b = full(dve, "E", tag, g)
                        for i in range(4):
                            c, h = divmod(4 * g + i, 6)
                            ins = V.scalar_tensor_tensor(view(R, GE_(g) + i * P, (1, P)), view(ps, b + i * P, (1, P)),
                                                         view(sm, GCU + c * 24 + d * 6 + h, (1, 1)), cc(C_NEG + d * P, P), SUB, ADD)
                            if i < 3:
                                step(ins)
                            else:
                                say(ins, read("vector", "E", tag, g))
                        signal("exponent_ready", tag, g)
                        dve.wait_ge(*at("decay_matrix_ready", tag, g))
                        for i2 in range(2):
                            b = full(dve, "G", tag, g, i2)
                            for i in range(2):
                                s = 4 * g + 2 * i + i2
                                c, h = divmod(s, 6)
                                ev = view(R, GE_(g) + (2 * i + i2) * P, (1, P))
                                step(V.scalar_tensor_tensor(view(R, GLT + s * P, (1, P)), view(ps, b + i * 256, (1, P)),
                                                            view(sm, GBT + c * 12 + d * 6 + h, (1, 1)), ev, MUL, MUL))
                                ins = V.tensor_tensor(view(R, GPT + s * P, (1, P)), view(ps, b + i * 256 + P, (1, P)), ev, MUL)
                                if i == 0:
                                    step(ins)
                                else:
                                    say(ins, read("vector", "G", tag, g, i2))
                    c1 = d
                    kd = view(R, GKD, (64, 6), (1, 64))
                    tt(kd, view(R, GN + c1 * 1152 + 384, (64, 6), (1, 64)), view(sm, GKF + c1 * 12 + d * 6, (1, 6), (0, 64)), MUL)
                    if d == 0:
                        step(V.memset(view(hnT, GS, (1, 640)), 0.0))
                    signal("kd_ready", tag)
                    invert(tag, d, 3, (GLT, P), "g")
                    for n, c in enumerate((0, 1) if d == 0 else (1, 0)):
                        gam = view(sm, GGA + c * 12 + d * 6, (1, 6), (0, 64))
                        tmp = view(R, GR, (64, 6), (1, 64))
                        if n == 1:
                            b = full(dve, "KS", tag, 0)
                            say(V.tensor_tensor(tmp, view(ps, b, (64, 6), (1, 64)), gam, MUL), read("vector", "KS", tag, 0))
                            tt(view(R, GR, (1, 384)), view(R, GN + c * 1152 + 768, (1, 384)), view(R, GR, (1, 384)), SUB)
                            signal("delta_rhs_ready", tag)
                        b = full(dve, "U", tag, n)
                        say(V.tensor_tensor(view(R, GU, (64, 6), (1, 64)), view(ps, b, (64, 6), (1, 64)),
                                            view(sm, GBT + c * 12 + d * 6, (1, 6), (0, 64)), MUL), read("vector", "U", tag, n))
                        o = view(R, GO + c * 384, (1, 384))
                        if n == 1:
                            b = full(dve, "KS", tag, 1)
                            say(V.tensor_tensor(tmp, view(ps, b, (64, 6), (1, 64)), gam, MUL), read("vector", "KS", tag, 1))
                            if d == 0:
                                step(V.tensor_copy(o, view(R, GR, (1, 384))))
                            else:
                                tt(o, o, view(R, GR, (1, 384)), ADD)
                        b = full(dve, "PU", tag, n)
                        if d == 0 and n == 0:
                            say(V.tensor_copy(o, view(ps, b, (1, 384))), read("vector", "PU", tag, n))
                        else:
                            say(V.tensor_tensor(o, view(ps, b, (1, 384)), o, ADD), read("vector", "PU", tag, n))
                v = view(R, GO, (1, 768))
                tt(view(hn, 0, (1, 768)), v, v, MUL)
                step(V.tensor_reduce(view(sm, SS, (1, 12)), view(hn, 0, (64, 12), (1, 64)), AX.X, ADD))
                signal("gdn_ss_ready", L)
                dve.wait_ge(*at("gdn_rstd_ready", L))
                tt(view(R, GO, (64, 12), (1, 64)), view(R, GO, (64, 12), (1, 64)), view(sm, SS, (1, 12), (0, 64)), MUL)
                for t in range(T):
                    tt(view(R, MIXB + t * D, (64, 6), (1, 64)), view(R, GO + t * 384, (64, 6), (1, 64)),
                       view(rows, R_GN + 64 * (L - 2), (0, 6), (1, 64)), MUL)

                step(V.tensor_tensor(view(sm, MU, (1, 7)), col(K_MU, 7), col(K_MU + 7, 7), ADD))
                ts(view(sm, MU, (1, 7)), view(sm, MU, (1, 7)), -1.0, 1.0, MUL, ADD)
                for m in range(7):
                    o = view(R, RF + m * S, (1, S))
                    ts(o, view(R, RP + m * 258 + 1, (1, S)), view(sm, MU + m, (1, 1)), None, MUL)
                    step(V.scalar_tensor_tensor(o, view(R, RP + m * 258, (1, S)), col(K_MU + m), o, MUL, ADD))
                    step(V.scalar_tensor_tensor(o, view(R, RP + m * 258 + 2, (1, S)), col(K_MU + 7 + m), o, MUL, ADD))
                w6 = view(R, RF + 6 * S, (1, S), np_=64)
                ts(w6, w6, 20.0, None, MIN)
                signal("tanh_arg_ready", L)
                ts(view(sm, NB, (1, 8)), col(K_W0, 8), -1.0, None, MUL)
                dve.wait_ge(*at("tanh_exp_ready", L))
                ts(w6, w6, 1.0, None, ADD)
                recip(w6, w6)
                ts(w6, w6, -2.0, 1.0, MUL, ADD)
                signal("shifted_ready", L)
                kx = view(R, RKX, (1, 512))
                for ct in range(2):
                    ts(view(R, RKX + ct * S, (1, S)), view(R, RF + (2 + ct) * S, (1, S)), col(K_KK + ct), None, MUL)
                tt(view(R, RKK2, (1, 512)), kx, kx, MUL)
                signal("kk_squares_ready", L)
                dve.wait_ge(*at("bank_read_by_scalar", "kkss", L))
                tt(kx, kx, view(R, RKK2, (1, 512)), MUL)
                for base in (RSW, RSA):
                    v = view(R, base, (1, 1024))
                    ts(v, v, 1.0, None, ADD)
                    recip(v, v)
                v = view(R, RSW, (1, 1024))
                ts(v, v, -math.exp(-0.5), None, MUL)
                ts(view(sm, NB + 8, (1, 2)), col(K_KA, 2), -1.0, 1.0, MUL, ADD)
                for d in range(2):
                    for ct in range(2):
                        o = view(R, RKM + d * 512 + ct * S, (1, S))
                        ts(o, view(R, RSA + d * 512 + ct * S, (1, S)), col(K_KA + ct), view(sm, NB + 8 + ct, (1, 1)), MUL, ADD)
                    tt(view(R, RKM + d * 512, (1, 512)), view(R, RKM + d * 512, (1, 512)), view(R, RF + 2 * S, (1, 512)), MUL)
                pr = view(R, RPR, (1, 512))
                tt(pr, view(R, RKM, (1, 512)), view(R, RKM + 512, (1, 512)), ADD)
                tt(pr, pr, view(R, RF, (1, 512)), MUL)
                for ct in range(2):
                    v = view(R, RPR + ct * S, (1, S))
                    ts(v, v, col(K_RK + ct), 0.5, MUL, MUL)
                signal("bonus_terms_ready", L)
                for d in range(2):
                    for ct in range(2):
                        for c in range(2):
                            q0 = d * 512 + ct * S + c * P
                            first, stp = (0, 1) if d == 0 else (P - 1, -1)
                            step(V.tensor_tensor_scan(view(R, RCM + q0 + first, (stp, P)), view(cst, C_ONE, (1, P)),
                                                      view(R, RSW + q0 + first, (stp, P)), 0.0, MUL, ADD))
                            q = d * 4 + ct * 2 + c
                            mid, end = (63, P - 1) if d == 0 else (64, 0)
                            ts(view(sm, RMD + q, (1, 1)), view(R, RCM + q0 + mid, (1, 1)), 1.0, None, MUL)
                            ts(view(sm, REN + q, (1, 1)), view(R, RCM + q0 + end, (1, 1)), 1.0, None, MUL)
                            ts(view(R, RCM + q0, (1, P)), view(R, RCM + q0, (1, P)), view(sm, RMD + q, (1, 1)), None, SUB)
                        q = d * 4 + ct * 2
                        tt(view(sm, RE + d * 2 + ct, (1, 1)), view(sm, REN + q + d, (1, 1)), view(sm, RMD + q + d, (1, 1)), SUB)
                        tt(view(sm, RE + d * 2 + ct, (1, 1)), view(sm, RE + d * 2 + ct, (1, 1)), view(sm, RMD + q + 1 - d, (1, 1)), ADD)
                tt(view(R, RCL, (1, 1024)), view(R, RCM, (1, 1024)), view(R, RSW, (1, 1024)), SUB)
                signal("rwkv_cum_ready", L)
                dve.wait_ge(*at("rwkv_exp_ready", L))
                for d in range(2):
                    for ct in range(2):
                        o = d * 512 + ct * S
                        q = d * 1024 + ct * 512
                        kk = view(R, RKX + ct * S, (1, S))
                        tt(view(R, RAR + q, (1, S)), kk, view(R, RCL + o, (1, S)), MUL)
                        tt(view(R, RAR + q + 256, (1, S)), view(R, RF + ct * S, (1, S)), view(R, REP + o, (1, S)), MUL)
                        tt(view(R, RBK + q, (1, S)), kk, view(R, RSA + o, (1, S)), MUL)
                        tt(view(R, RBK + q, (1, S)), view(R, RBK + q, (1, S)), view(R, RCM + o, (1, S)), MUL)
                        tt(view(R, RBK + q + 256, (1, S)), view(R, RKM + o, (1, S)), view(R, RCM + o, (1, S)), MUL)
                    signal("rwkv_factors_ready", L, d)
                b = full(dve, "bonus", L)
                say(V.tensor_copy(view(sm, BN, (1, 8)), view(ps, b, (1, 8))), read("vector", "bonus", L))
                for d in range(2):
                    tag = ("r", L, d)
                    for s in range(8):
                        b = full(dve, "M4", tag, s)
                        say(V.tensor_tensor(view(R, RM4 + s * 512, (256, 2), (1, 256)), view(ps, b, (256, 2), (1, 256)),
                                            view(cst, C_SI + 2 * d * P, (0, 2), (1, 256)), MUL), read("vector", "M4", tag, s))
                    invert(tag, d, 2, (RM4, 512), "r")
                    for n, c in enumerate((0, 1) if d == 0 else (1, 0)):
                        o = view(R, RY + c * 256, (1, 256))
                        b = full(dve, "Yr", tag, n)
                        if d == 0:
                            say(V.tensor_copy(o, view(ps, b, (1, 256))), read("vector", "Yr", tag, n))
                        else:
                            say(V.tensor_tensor(o, view(ps, b, (1, 256)), o, ADD), read("vector", "Yr", tag, n))
                        if n == 0:
                            b = full(dve, "T0", tag)
                            for hf in range(2):
                                half = dict(p0=64 * hf, np_=64)
                                ins = V.tensor_tensor(view(hnT, RT0 + 64 * hf, (P, 2), (1, 64), **half), view(ps, b, (64, 2), (1, 64), **half),
                                                      view(sm, RE + 2 * d, (1, 2), (0, 64), **half), MUL)
                                if hf == 0:
                                    step(ins)
                                else:
                                    say(ins, read("vector", "T0", tag))
                y8 = view(R, RY, (64, 8), (1, 64))
                step(V.tensor_reduce(view(sm, YM, (1, 8)), y8, AX.X, ADD))
                ts(view(sm, YM, (1, 8)), view(sm, YM, (1, 8)), 1.0 / 64, None, MUL)
                tt(y8, y8, view(sm, YM, (1, 8), (0, 64)), SUB)
                tt(view(hn, 0, (1, 512)), view(R, RY, (1, 512)), view(R, RY, (1, 512)), MUL)
                step(V.tensor_reduce(view(sm, SS, (1, 8)), view(hn, 0, (64, 8), (1, 64)), AX.X, ADD))
                signal("rwkv_var_ready", L)
                dve.wait_ge(*at("rwkv_rstd_ready", L))
                tt(y8, y8, view(sm, SS, (1, 8), (0, 64)), MUL)
                for t in range(T):
                    yv = view(R, RY + t * 256, (1, 256))
                    tt(yv, yv, view(rows, R_LNG + 256 * (L - 2), (1, 256)), MUL)
                    tt(yv, yv, view(rows, R_LNB + 256 * (L - 2), (1, 256)), ADD)
                tt(view(R, RVN, (64, 8), (1, 64)), view(R, RVN, (64, 8), (1, 64)), view(sm, BN, (1, 8), (0, 64)), MUL)
                tt(view(R, MIXB + 768, (D, 2), (1, 256)), view(R, RY, (256, 2), (1, 256)), view(R, RVN, (256, 2), (1, 256)), ADD)
                for t in range(T):
                    v = view(R, MIXB + t * D, (1, D))
                    tt(v, v, view(R, GATE + t * D, (1, D)), MUL)
                    signal("mix_ready", L, t)
                residual("o", L, "mix" if L == 2 else "fin", L + 1)
            for t in range(T):
                dve.wait_ge(*at("hn_ready", "fin", 4, t))
                dve.wait_ge(*at("final_gain_in", "b", R_FIN))
                v = view(hn, t * D, (1, D))
                tt(v, v, view(rows, R_FIN, (1, D)), MUL)
                signal("result_ready", t)

    return dict(C.table, bank_of=new_bank, reader=new_reader, freed_by=new_freed)


def kernel(**inputs):
    import concourse.bacc as _bacc
    from concourse.bass_utils import run_bass_kernel_spmd as _run

    masks, buckets = shape_constants()
    arrays = {}
    for name in _INS:
        arrays[f"in_{name}"] = np.ascontiguousarray(inputs[name])
    arrays["in_const_masks"] = masks
    arrays["in_const_buckets"] = buckets

    def build(known):
        nc = _bacc.Bacc("TRN2", target_bir_lowering=False, num_devices=1)
        a = {n[3:]: nc.dram_tensor(n, v.shape, mybir.dt.from_np(v.dtype), kind="ExternalInput").ap() for n, v in arrays.items()}
        out = nc.dram_tensor("out", (1, S, D), F32, kind="ExternalOutput").ap()
        return nc, program(nc, a, out, known)

    _, known = build(None)
    nc, _ = build(known)
    r = _run(nc, [arrays], core_ids=[0])
    return r.results[0]["out"]
```

```python
import math
from contextlib import ExitStack

import numpy as np
import concourse.bass as bass
from concourse import mybir

F32 = mybir.dt.float32
I32 = mybir.dt.int32
ALU = mybir.AluOpType
ACT = mybir.ActivationFunctionType
AX = mybir.AxisListType
ADD, SUB, MUL, MAX, MIN = ALU.add, ALU.subtract, ALU.mult, ALU.max, ALU.min

P = 128
S = 256
T = S // P
D = 1024
KC = D // P
HD = 64
NEG = -1e30
LAM_INIT = 0.8 - 0.6 * math.exp(0.0)
SLAB = 4096
SLOTS = 3
LEVELS = (2, 4, 8, 16, 32, 64)
NC_CMP = (S - 32) // 16 + 1

C_ID, C_ONE, C_BLK, C_TRI, C_NEG = 0, 128, 256, 384, 640
C_SI = 896
C_M1 = 1408
C_LV = 1664
C_FRQ = C_LV + 2 * len(LEVELS) * P
C_ROWOK = C_FRQ + 16
C_EPS = C_ROWOK + 2
C_N = C_EPS + 3


def shape_constants():
    c = np.zeros((P, C_N), np.float32)
    j = np.arange(P)[:, None]
    i = np.arange(P)[None, :]
    c[:, C_ID:C_ID + P] = j == i
    c[:, C_ONE:C_ONE + P] = 1
    c[:, C_BLK:C_BLK + P] = (j // 64) == (i // 64)
    for d, (inc, strict) in enumerate(((j <= i, j < i), (j >= i, j > i))):
        c[:, C_TRI + d * P:C_TRI + (d + 1) * P] = inc
        c[:, C_NEG + d * P:C_NEG + (d + 1) * P] = np.where(inc, 0, NEG)
        c[:, C_SI + 2 * d * P:C_SI + (2 * d + 1) * P] = strict
        c[:, C_SI + (2 * d + 1) * P:C_SI + (2 * d + 2) * P] = inc
        lo, hi = (j, i) if d == 0 else (i, j)
        c[:, C_M1 + d * P:C_M1 + (d + 1) * P] = (lo // 2 == hi // 2) & (lo < hi)
        for n, m in enumerate(LEVELS):
            same = (j // (2 * m)) == (i // (2 * m))
            late, early = (j % (2 * m) >= m), (i % (2 * m) < m)
            if d == 1:
                late, early = ~late, ~early
            o = C_LV + (d * len(LEVELS) + n) * P
            c[:, o:o + P] = same & late & early
    c[:, C_FRQ:C_FRQ + 16] = np.float32(10000.0) ** (-np.arange(16, dtype=np.float32) / np.float32(16))
    for t in range(T):
        c[:, C_ROWOK + t] = (t * P + np.arange(P)) >= 31
    c[:, C_EPS] = 1e-6
    c[:, C_EPS + 1] = 64e-5
    c[:, C_EPS + 2] = 1.0
    rel = 255 - np.arange(384)
    n = np.maximum(rel, 0)
    large = 16 + (np.log(np.maximum(n, 1).astype(np.float32) / 16) / np.float32(math.log(8.0)) * 16).astype(np.int32)
    bucket = np.where(n < 16, n, np.minimum(large, 31))
    oh = np.zeros((32, 768), np.float32)
    oh[bucket, np.arange(384)] = rel >= 0
    oh[:, 384:] = np.where(rel >= 0, 0, 8 * NEG)
    return c, oh


BT = 0
_b1 = 4096
QT, KCVC, KST, KD = _b1, _b1 + 1024, _b1 + 1536, _b1 + 2048
VS, VW, GT = _b1 + 3072, _b1 + 3328, _b1 + 3584
DQ, DK, DV = _b1 + 3632, _b1 + 4656, _b1 + 5680
BLK, HID, GE = _b1 + 6704, _b1 + 7664, _b1 + 7724
KCT, VCN, VBD, PC, PCT = _b1 + 7844, _b1 + 7874, _b1 + 8002, _b1 + 8514, _b1 + 8770
_mix0 = _b1 + 9026
_pb = _mix0 + 2048
TBL, OH, FR, STG = _pb, _pb + 16, _pb + 784, _pb + 1168
MQ, MV = _b1, _b1 + 4096
HT = _b1
GATE, MIXB, RP = 0, 2048, 4096
_r = 5904
GP, GC = _r, _r + 2340
LOW = _r + 4644
_m = LOW + 752
CQN, CT = _m, _m + 640
QN, KN, KV = _m + 1408, _m + 2560, _m + 3712
QKT = _m + 5248
RTM = GP
GN = _m
KQ = GN + 2304
XTG, YYG = KQ + 1536, KQ + 3072
GKD = YYG + 1536
GR, GU = GKD + 384, GKD + 768
GS, RT0 = 0, 384
GLT, GPT, XXG = _r, _r + 1536, _r + 3072
GO = LOW - 28
RF = 0
RKX, RKK2, RVN = RP, RP + 512, RP + 1024
RPR = RKK2
RSW, RSA, RKM, RCM = (19640 + 1024 * i for i in range(4))
REP, RAR, RBK = _r, _r + 2048, _r + 4096
RCL = RSW
RM4 = _r + 6144
RXX, RXT, RYY, RBN = RM4 + 4096, RM4 + 5120, RM4 + 6144, RM4 + 6656
RY, RU, RRH = _r, _r + 512, _r + 768
R_N = 23736

SS, SB, LM, CM, TRG, TRK, PF, NB, MU = 0, 24, 32, 40, 64, 128, 144, 150, 160
RMD, REN, RE, BN, YM, MXB = 168, 176, 184, 192, 200, 212
GAB, GBT, GSP, GAL, GG, GCU, GGA, GKF = 500, 524, 548, 572, 584, 608, 656, 680
SUMS = {"sel": 300, "win": 320, "moba": 340, "diff": 380, "mla": 400}


def XT(st):
    return XTG if st == "g" else RXT


def XX(st):
    return XXG if st == "g" else RXX


def YY(st):
    return YYG if st == "g" else RYY


def GE_(g):
    return YYG + 512 * g


def RT(m):
    return HT + 8192 + 512 * m


def MIX(L):
    return _mix0 if L < 2 else MIXB


def PB(h, name=""):
    return (GP if isinstance(name, tuple) else _pb) + (h % 3) * 768


def PTB(h, name=""):
    return (QN if isinstance(name, tuple) else _pb + 2304) + (h % 2) * 512


def MX(h, mp):
    return MXB + (h % 4) * 4 + 2 * mp


def SU(name, h, mp):
    return SUMS[name[0] if isinstance(name, tuple) else name] + (4 * h + 2 * mp if name == "diff" else 2 * h)


_INS = ["x", "bias_table", "norm_mix", "norm_mlp", "norm_final", "mlp_w1", "mlp_w2", "ev_w_in", "ev_w_out",
        "ev_cmp_pos_k", "ev_cmp_w1_k", "ev_cmp_w2_k", "ev_cmp_pos_v", "ev_cmp_w1_v", "ev_cmp_w2_v", "ev_lam_q1",
        "ev_lam_k1", "ev_lam_q2", "ev_lam_k2", "ev_subln", "od_w_in", "od_w_out", "positions_2", "norm_g_2", "w_in_2",
        "gdn_conv_2", "gdn_a_log_2", "gdn_dt_bias_2", "gdn_norm_g_2", "mla_q_norm_g_2", "mla_w_uq_2",
        "mla_kv_norm_g_2", "mla_w_ukv_2", "rwkv_mu_2", "rwkv_w0_2", "rwkv_w2_2", "rwkv_a0_2", "rwkv_a2_2",
        "rwkv_k_k_2", "rwkv_k_a_2", "rwkv_r_k_2", "rwkv_ln_g_2", "rwkv_ln_b_2", "w_out_2", "final_norm_g_2"]


class Counts:

    def __init__(self, nc, ctx, known):
        self.nc, self.ctx, self.known = nc, ctx, known
        self.sems, self.value, self.table = {}, {}, {}

    def sem(self, name):
        if name not in self.sems:
            self.sems[name] = self.ctx.enter_context(self.nc.semaphore(name))
            self.value[name] = 0
        return self.sems[name]

    def up(self, name, *key, by=1):
        s = self.sem(name)
        self.value[name] += by
        assert (name,) + key not in self.table, (name, key)
        self.table[(name,) + key] = self.last = self.value[name]
        return s, by

    def at(self, name, *key):
        s = self.sem(name)
        return s, (self.known[(name,) + key] if self.known else 1)


def view(t, off, *dims, p0=0, np_=P):
    w = t.shape[1]
    return bass.AP(t, p0 * w + off, [[w, np_]] + [list(x) for x in dims])


def program(nc, a, out, known=None):
    ctx = ExitStack()
    with ctx:
        C = Counts(nc, ctx, known)
        up, at = C.up, C.at

        def sb(name, n, dt=F32):
            return ctx.enter_context(nc.sbuf_tensor(name, [P, n], dt))

        scratch = nc.dram_tensor("bias_by_distance" + ("" if known else "_dry"), [16, P * 384], F32, kind="Internal")
        ps = ctx.enter_context(nc.psum_tensor("banks", [P, 8 * 512], F32))
        slabs = sb("weight_slabs", SLOTS * SLAB)
        x = sb("x_res", T * D)
        hn = sb("hn", T * D)
        hnT = sb("hnT", KC * S)
        cst = sb("consts", C_N)
        cols = sb("columns", 2 * P)
        rows = sb("row_params", 2680)
        mlaw = sb("mla_weights", 1920)
        rww = sb("rwkv_lora", 512)
        cmpw = sb("cmp_w2", 128)
        sm = sb("small", 1024)
        R = sb("region", R_N)
        posi = sb("positions", T, I32)

        CN_MIX, CN_MLP, CN_G2 = 0, 16, 32
        CL = 48
        K_MU, K_W0, K_A0, K_KK, K_KA, K_RK, K_QN, K_QN_TAIL, K_KVN = \
            (0, 14), (28, 4), (36, 4), (44, 2), (48, 2), (52, 2), (56, 1), (58, 1), (60, 1)
        CB_CONV, CB_POS = P, P + 90
        R_SUB, R_GN, R_LNG, R_LNB, R_FIN, R_AL, R_DT, R_LAM = 0, 128, 256, 768, 1280, 2304, 2328, 2352

        def cc(c, n=1):
            return cst[:, c:c + n]

        IDENT = cst[:, C_ID:C_ID + P]

        plan = []

        def cols_slab(key, w, c0, n):
            plan.append((key, [(view(slabs, 0, (n, KC), (1, n)), w[:, c0:c0 + n].rearrange("(k p) n -> p k n", p=P))]))

        def rows_slab(key, w, r0):
            plan.append((key, [(view(slabs, 0, (D, 4), (1, D)), w[r0:r0 + 512, :].rearrange("(k p) n -> p k n", p=P))]))

        for n, (c0, w) in enumerate(((0, 512), (512, 512), (1024, 280), (1304, 512), (1816, 512), (2328, 512))):
            if n == 3:
                plan.append((("cmp",), [(view(slabs, 2048 * i, (P, 16), (1, P)),
                                         a[nm][0].rearrange("(k p) n -> p k n", p=P)) for i, nm in enumerate(("ev_cmp_w1_k", "ev_cmp_w1_v"))]))
            cols_slab(("in", 0, n), a["ev_w_in"][0], c0, w)
        for L in range(4):
            if L == 1:
                for n in range(6):
                    cols_slab(("in", 1, n), a["od_w_in"][0], 512 * n, 512)
            if L >= 2:
                for n, c0, w in ((2, 1024, 512), (3, 1536, 512), (4, 2048, 504), (5, 2552, 512), (6, 3064, 384), (0, 0, 512), (1, 512, 512)):
                    cols_slab(("in", L, n), a["w_in_2"][L - 2], c0, w)
            wo = (a["ev_w_out"][0], a["od_w_out"][0], a["w_out_2"][0], a["w_out_2"][1])[L]
            for n in range(2):
                cols_slab(("out", L, n), wo, 512 * n, 512)
            if L < 2:
                for n in range(8):
                    cols_slab(("w1", L, n), a["mlp_w1"][L], 512 * n, 512)
                for n in range(8):
                    rows_slab(("w2", L, n), a["mlp_w2"][L], 512 * n)
        slot_of = {key: n % SLOTS for n, (key, _) in enumerate(plan)}

        jobs = {"short": [], "long": []}
        bank_of = known.get("bank_of", {}) if known else {}
        reader = known.get("reader", {}) if known else {}
        freed_by = known.get("freed_by", {}) if known else {}
        new_bank, new_reader, new_freed = {}, {}, {}

        def bank(key):
            return bank_of.get(key, 0) * 512

        block = ctx.enter_context(nc.Block())

        @block.sync
        def _(sp):
            for i, (dst, src) in enumerate((
                    (view(x, 0, (D, T), (1, D)), a["x"][0].rearrange("(t p) d -> p t d", p=P)),
                    (cst[:, :], a["const_masks"]),
                    (view(R, TBL, (1, 16), np_=32), a["bias_table"]),
                    (view(R, OH, (1, 768), np_=32), a["const_buckets"]))):
                sp.dma_start(dst, src).then_inc(*up("constants_in", i, by=16))
            for n, (key, parts) in enumerate(plan):
                slot = n % SLOTS
                if n == 1:
                    sp.wait_ge(*at("column_params_in", "s", 1, 106))
                if n >= SLOTS:
                    sp.wait_ge(*at(*freed_by.get(plan[n - SLOTS][0], ("bank_full",))))
                for i, (dst, src) in enumerate(parts):
                    dst = bass.AP(slabs, dst.offset + slot * SLAB, dst.ap)
                    sp.dma_start(dst, src).then_inc(*up(f"slab_in_slot{slot}", *key, i, by=16))
            for t in range(T):
                sp.wait_ge(*at("result_ready", t))
                sp.dma_start(out[0, t * P:(t + 1) * P, :], view(hn, t * D, (1, D))).then_inc(*up("result_stored", t, by=16))
            for t in range(T):
                sp.wait_ge(*at("result_stored", t))

        @block.tensor
        def _(pe):
            closed = []

            def open_(key, ring="short"):
                size, base = (6, 0) if ring == "short" else (2, 6)
                lst = jobs[ring]
                n = len(lst)
                lst.append(key)
                if n >= size:
                    old = lst[n - size]
                    pe.wait_ge(*at(reader.get(old, "bank_read_by_vector"), *old))
                new_bank[key] = base + n % size
                return (base + n % size) * 512

            def close(ins, key):
                ins.then_inc(*up("bank_full", *key))
                closed.append(key)

            def slab(key, i=0):
                pe.wait_ge(*at(f"slab_in_slot{slot_of[key]}", *key, i))
                return slot_of[key] * SLAB

            def used(key):
                new_freed[key] = ("bank_full",) + closed[-1]

            mm = nc.tensor.matmul

            def transposes(key, srcs, rd, evs=()):
                for e in evs:
                    pe.wait_ge(*e)
                b = open_(key)
                for i, s in enumerate(srcs):
                    k, m = s.shape[0], s.shape[1]
                    ins = nc.tensor.transpose(view(ps, b + i * P, (1, k), np_=m), s, cst[0:k, C_ID:C_ID + k])
                close(ins, key)

            def proj_T(skey, key, c0s, width, wait=()):
                o = slab(skey)
                for e in wait:
                    pe.wait_ge(*e)
                b = open_(key)
                for i, c0 in enumerate(c0s):
                    for k in range(KC):
                        ins = mm(view(ps, b + i * S, (1, S)), view(slabs, o + k * width + c0, (1, P)),
                                 view(hnT, k * S, (1, S)), start=k == 0, stop=k == KC - 1)
                close(ins, key)

            def proj_N(skey, key, c0, n, width, t):
                o = slab(skey)
                b = open_(key)
                for k in range(KC):
                    ins = mm(view(ps, b, (1, n)), view(hnT, k * S + t * P, (1, P)),
                             view(slabs, o + k * width + c0, (1, n)), start=k == 0, stop=k == KC - 1)
                close(ins, key)

            def normed_T(L, which):
                for t in range(T):
                    for q in range(2):
                        transposes(("hnT", which, L, t, q),
                                   [view(hn, t * D + (4 * q + i) * P, (1, P)) for i in range(4)], "v",
                                   [at("hn_ready", which, L, t)])
                pe.wait_ge(*at("bank_read_by_vector", "hnT", which, L, T - 1, 1))

            def mlp(L):
                normed_T(L, "mlp")
                for n in range(8):
                    for m in range(2):
                        proj_T(("w1", L, n), ("h", L, n, m), (256 * m, 256 * m + P), 512)
                    used(("w1", L, n))
                bs = [open_(("y", L, i)) for i in range(4)]
                for n in range(8):
                    o = slab(("w2", L, n))
                    pe.wait_ge(*at("hidden_ready", L, n, 1))
                    for k in range(4):
                        for i in range(4):
                            t, half = i // 2, i % 2
                            kk = 4 * n + k
                            ins = mm(view(ps, bs[i], (1, 512)), view(R, HT + kk * S + t * P, (1, P)),
                                     view(slabs, o + k * D + half * 512, (1, 512)), start=kk == 0, stop=kk == 31)
                            if n == 7 and k == 3:
                                close(ins, ("y", L, i))
                    if n < 7:
                        ins.then_inc(*up("w2_slab_used", L, n))
                        new_freed[("w2", L, n)] = ("w2_slab_used", L, n)
                    else:
                        used(("w2", L, n))

            def out_proj(L):
                for t in range(T):
                    for q in range(2):
                        transposes(("mixT", L, t, q),
                                   [view(R, MIX(L) + t * D + (4 * q + i) * P, (1, P)) for i in range(4)], "v",
                                   [at("mix_ready", L, t)])
                pe.wait_ge(*at("bank_read_by_scalar", "mixT", L, T - 1, 1))
                for n in range(2):
                    for t in range(T):
                        proj_N(("out", L, n), ("o", L, n, t), 0, 512, 512, t)
                    used(("out", L, n))

            def attention(name, H, scores, values, nblk, vw, between=None):
                per = 512 // vw
                for i in range(H + 2):
                    if i < H:
                        scores(i)
                    if between:
                        between(i)
                    if 0 <= i - 1 < H:
                        h = i - 1
                        key = ("PT", name, h)
                        pe.wait_ge(*at("diff_probs_ready" if name == "diff" else "probs_ready", name, h))
                        b = open_(key)
                        for j in range(nblk):
                            ins = nc.tensor.transpose(view(ps, b + j * P, (1, P)), view(R, PB(h, name) + j * P, (1, P)), IDENT)
                        close(ins, key)
                    if 0 <= i - 2 < H:
                        h = i - 2
                        if h % per == 0:
                            ob = [open_(("O", name, h // per, t), "long") for t in range(T)]
                        pe.wait_ge(*at("bank_read_by_scalar", "PT", name, h))
                        c = (h % per) * vw
                        blocks = ((0, 0, 0), (1, 1, 0), (2, 1, 1)) if nblk == 3 else ((0, 0, 0), (1, 0, 1), (2, 1, 0), (3, 1, 1))
                        for j, t, k in blocks:
                            last_k = k == (t if nblk == 3 else 1)
                            ins = mm(view(ps, ob[t] + c, (1, vw)), view(R, PTB(h, name) + j * P, (1, P)), values(h, k),
                                     start=k == 0, stop=last_k)
                            if last_k and (h % per == per - 1 or h == H - 1):
                                close(ins, ("O", name, h // per, t))

            def causal_scores(name, q_of, k_of):
                def f(h, key=None):
                    key = key or ("S", name, h)
                    b = open_(key)
                    q, k = q_of(h), k_of(h)
                    mm(view(ps, b, (1, P)), q(0, P), k(0, P), start=True, stop=True)
                    close(mm(view(ps, b + P, (1, S)), q(P, P), k(0, S), start=True, stop=True), key)
                return f

            def tview(base, tile, half):
                return lambda o, n: view(R, base + tile * S + o, (1, n), p0=64 * half, np_=64)

            pe.wait_ge(*at("column_params_in", "s", 1, 106))
            pe.wait_ge(*at("constants_in", 3))
            transposes(("cols",), [view(R, STG, (1, P)), view(R, STG + P, (1, P))], "v")
            b = open_(("bias",))
            close(mm(view(ps, b, (1, 384), np_=16), view(R, TBL, (1, 16), np_=32), view(R, OH, (1, 384), np_=32),
                     start=True, stop=True), ("bias",))

            normed_T(0, "mix")
            for m in range(2):
                proj_T(("in", 0, 0), ("q", m), (256 * m, 256 * m + P), 512)
            used(("in", 0, 0))
            proj_T(("in", 0, 1), ("kcvc",), (0, P), 512)
            proj_T(("in", 0, 1), ("ks",), (256,), 512)
            for t in range(T):
                proj_N(("in", 0, 1), ("vs", t), 384, P, 512, t)
            used(("in", 0, 1))
            proj_T(("in", 0, 2), ("kw",), (0,), 280)
            for t in range(T):
                proj_N(("in", 0, 2), ("vwg", t), 128, 152, 280, t)
            used(("in", 0, 2))
            pe.wait_ge(*at("cmp_blocks_ready", 1))
            for i in range(2):
                o = slab(("cmp",), 1)
                b = open_(("hid", i))
                for jj in range(16):
                    ins = mm(view(ps, b, (1, 30)), view(slabs, o + 2048 * i + jj * P, (1, P)),
                             view(R, BLK + i * 480 + jj * 15, (240, 2), (1, 15)), start=jj == 0, stop=jj == 15)
                close(ins, ("hid", i))
            used(("cmp",))
            pe.wait_ge(*at("cmp_hidden_ready", 1))
            b = open_(("cmpkv",))
            pe.wait_ge(*at("row_params_in", "all"))
            mm(view(ps, b, (1, 30), np_=64), view(cmpw, 0, (1, 64)), view(R, HID, (1, 30)), start=True, stop=True)
            for g in range(2):
                ins = mm(view(ps, b + 64 + 64 * g, (1, 64), np_=15), view(R, HID + 30 + 15 * g, (1, 15)),
                         view(cmpw, 64, (1, 64)), start=True, stop=True)
            close(ins, ("cmpkv",))
            pe.wait_ge(*at("kdup_ready", 0))
            def diff_projection(i):
                if i in (1, 2):
                    proj_T(("in", 0, 3), ("dq", i - 1), (256 * (i - 1), 256 * (i - 1) + P), 512)
                if i in (3, 4):
                    proj_T(("in", 0, 4), ("dk", i - 3), (256 * (i - 3), 256 * (i - 3) + P), 512)
                if i in (5, 6):
                    proj_N(("in", 0, 5), ("dv", i - 5), 0, 512, 512, i - 5)
                if i in (2, 4, 6):
                    used(("in", 0, 2 + i // 2))
            for nm, kb, vb in (("sel", KD, VS), ("win", KD + 512, VW)):
                attention(nm, 8, causal_scores(nm, lambda h: tview(QT, h // 2, h % 2),
                                               lambda h, kb=kb: tview(kb, h // 4, h % 2)),
                          lambda h, k, vb=vb: view(R, vb + k * P + (h // 4) * 64, (1, 64)), 3, 64, diff_projection if nm == "sel" else None)
            pe.wait_ge(*at("cmp_kv_ready", 0))
            for par in range(2):
                b = open_(("Sc", par))
                for t in range(T):
                    for hh in range(4):
                        h = 2 * hh + par
                        ins = mm(view(ps, b + (t * 4 + hh) * 16, (1, 15)),
                                 view(R, QT + (h // 2) * S + t * P, (1, P), p0=64 * par, np_=64),
                                 view(R, KCT + (h // 4) * 15, (1, 15), p0=64 * par, np_=64), start=True, stop=True)
                close(ins, ("Sc", par))
            pe.wait_ge(*at("cmp_probs_ready", 0))
            transposes(("PTc",), [view(R, PC + t * P, (1, P)) for t in range(T)], "a")
            pe.wait_ge(*at("bank_read_by_scalar", "PTc"))
            pe.wait_ge(*at("vbd_ready", 0, 7))
            for t in range(T):
                b = open_(("Oc", t))
                close(mm(view(ps, b, (1, 512)), view(R, PCT + t * P, (1, P)), view(R, VBD, (1, 512)), start=True, stop=True),
                      ("Oc", t))
            dsc = causal_scores("diff", lambda c: tview(DQ, c // 2, c % 2), lambda c: tview(DK, c // 2, c % 2))

            def diff_scores(h):
                dsc(2 * h, ("S", "diff", h, 0))
                dsc(2 * h + 1, ("S", "diff", h, 1))
            attention("diff", 4, diff_scores, lambda h, k: view(R, DV + k * 512 + h * P, (1, P)), 3, P)
            out_proj(0)
            mlp(0)

            normed_T(1, "mix")
            for n in range(4):
                for m in range(2):
                    proj_T(("in", 1, n), ("mqk", n, m), (256 * m, 256 * m + P), 512)
                used(("in", 1, n))
            for n in range(2):
                for t in range(T):
                    proj_N(("in", 1, 4 + n), ("mv", n, t), 0, 512, 512, t)
                used(("in", 1, 4 + n))
            pe.wait_ge(*at("bank_read_by_scalar", "mv", 1, 1))
            attention("moba", 16, causal_scores("moba", lambda h: tview(MQ, h // 2, h % 2),
                                                lambda h: tview(MQ, 8 + h // 2, h % 2)),
                      lambda h, k: view(R, MV + k * D + h * 64, (1, 64)), 3, 64)
            out_proj(1)
            mlp(1)

            def invert(tag, d, ngroups, LTv, st):
                for g in range(ngroups):
                    key = ("X0", tag, g)
                    transposes(key, [view(R, XT(st) + (4 * g + i) * P, (1, P)) for i in range(4)], "a",
                               [at("inverse_seed_ready", tag, g)])
                def retranspose(n, g):
                    transposes(("XT", tag, n, g), [view(R, XX(st) + (4 * g + i) * P, (1, P)) for i in range(4)], "a",
                               [at("bank_read_by_vector", "Z", tag, n, g)])

                for n, m in enumerate(LEVELS):
                    e = 0 if d == 0 else m
                    np2 = P // (2 * m)
                    for g in range(ngroups):
                        pe.wait_ge(*(at("bank_read_by_scalar", "X0", tag, g) if n == 0 else at("bank_read_by_vector", "Z", tag, n - 1, g)))
                        b = open_(("Y", tag, n, g))
                        for i in range(4):
                            ins = mm(view(ps, b + i * 64, (1, 64)), LTv(4 * g + i),
                                     view(R, XX(st) + (4 * g + i) * P + e, (2 * m, np2), (1, m)), start=True, stop=True)
                        close(ins, ("Y", tag, n, g))
                    if n > 0:
                        for g in range(ngroups):
                            retranspose(n - 1, g)
                    for g in range(ngroups):
                        pe.wait_ge(*at("bank_read_by_vector", "Y", tag, n, g))
                        if n > 0:
                            pe.wait_ge(*at("bank_read_by_scalar", "XT", tag, n - 1, g))
                        b = open_(("Z", tag, n, g))
                        for i in range(4):
                            ins = mm(view(ps, b + i * 64, (1, 64)), view(R, XT(st) + (4 * g + i) * P, (1, P)),
                                     view(R, YY(st) + g * 256 + i * 64, (1, 64)), start=True, stop=True)
                        close(ins, ("Z", tag, n, g))
                for g in range(ngroups):
                    retranspose(len(LEVELS) - 1, g)
                for g in range(ngroups):
                    pe.wait_ge(*at("bank_read_by_scalar", "XT", tag, len(LEVELS) - 1, g))

            for L in (2, 3):
                normed_T(L, "mix")
                for n in range(2):
                    for m in range(2):
                        proj_T(("in", L, 2 + n), ("gqkv", L, n, m), (256 * m, 256 * m + P), 512)
                    used(("in", L, 2 + n))
                proj_T(("in", L, 4), ("gqkv", L, 2, 0), (0,), 504)
                for t in range(T):
                    proj_N(("in", L, 4), ("low", L, t), 128, 376, 504, t)
                used(("in", L, 4))
                for m in range(2):
                    proj_T(("in", L, 5), ("rw", L, m), (256 * m, 256 * m + P), 512)
                used(("in", L, 5))
                proj_T(("in", L, 6), ("rw", L, 2), (0, P), 384)
                proj_T(("in", L, 6), ("rw", L, 3), (256,), 384)
                used(("in", L, 6))

                for t in range(T):
                    transposes(("cT", L, t), [view(R, CQN + t * 320, (1, P)), view(R, CQN + t * 320 + P, (1, 64)),
                                              view(R, CQN + t * 320 + 192, (1, P))], "v", [at("latents_ready", L)])
                for n in range(2):
                    for t in range(T):
                        proj_N(("in", L, n), ("gate", L, n, t), 0, 512, 512, t)
                    used(("in", L, n))
                pe.wait_ge(*at("latents_T_ready", L, 1))
                pe.wait_ge(*at("mla_weights_in", L))
                for t in range(T):
                    for hf in range(2):
                        b = open_(("uq", L, t, hf))
                        mm(view(ps, b, (1, 288)), view(R, CT + t * P, (1, P)), view(mlaw, hf * 288, (1, 288)), start=True, stop=False)
                        close(mm(view(ps, b, (1, 288)), view(R, CT + 256 + t * P, (1, P), np_=64),
                                 view(mlaw, 576 + hf * 288, (1, 288), np_=64), start=False, stop=True), ("uq", L, t, hf))
                    for hf in range(2):
                        b = open_(("ukv", L, t, hf))
                        close(mm(view(ps, b, (1, 384)), view(R, CT + 512 + t * P, (1, P)), view(mlaw, 1152 + hf * 384, (1, 384)),
                                 start=True, stop=True), ("ukv", L, t, hf))
                for h in range(6):
                    transposes(("qkT", L, h), [view(R, QN + t * 576 + h * 96, (1, 96)) for t in range(T)]
                               + [view(R, KN + t * 576 + h * 96, (1, 96)) for t in range(T)], "a", [at("rope_ready", L)])
                pe.wait_ge(*at("bank_read_by_scalar", "qkT", L, 5))

                def mla_scores(h, L=L):
                    b = open_(("S", "mla", L, h))
                    for t in range(T):
                        ins = mm(view(ps, b + t * S, (1, S)), view(R, QKT + h * 512 + t * P, (1, P), np_=96),
                                 view(R, QKT + h * 512 + S, (1, S), np_=96), start=True, stop=True)
                    close(ins, ("S", "mla", L, h))
                attention(("mla", L), 6, mla_scores, lambda h, k: view(R, KV + k * 768 + h * P + 64, (1, 64)), 4, 64)

                pe.wait_ge(*at("shifted_ready", L))
                pe.wait_ge(*at("lora_weights_in", L))
                for e in range(2):
                    for w in range(2):
                        b = open_(("lora", L, e, w))
                        for ct in range(2):
                            ins = mm(view(ps, b + ct * S, (1, S)), view(rww, e * 256 + ct * P, (1, P), p0=64 * w, np_=64),
                                     view(hn, RF + 6 * S, (1, S), p0=64 * w, np_=64), start=True, stop=True)
                        close(ins, ("lora", L, e, w))
                for t in range(T):
                    for w in range(3):
                        transposes(("gn", L, t, w), [view(R, GC + (3 * w + i) * S + t * P, (1, P)) for i in range(3)], "a",
                                   [at("conv_ready", L)])
                for m in range(3):
                    transposes(("kq", L, m), [view(R, GN + t * 1152 + w * 384 + m * P, (1, P)) for w in (1, 0) for t in range(T)],
                               "a", [at("qk_normed", L)])
                pe.wait_ge(*at("decay_ready", L))
                b = open_(("cum", L))
                for t in range(T):
                    for d in range(2):
                        mm(view(ps, b + t * 24 + d * 6, (1, 6)), cc(C_TRI + d * P, P), view(sm, GG + t * 12 + d * 6, (1, 6)),
                           start=True, stop=True)
                    ins = mm(view(ps, b + t * 24 + 12, (1, 12)), cc(C_ONE, P), view(sm, GG + t * 12, (1, 12)), start=True, stop=True)
                close(ins, ("cum", L))
                pe.wait_ge(*at("bank_read_by_scalar", "kq", L, 2))
                for d in range(2):
                    tag = ("g", L, d)
                    for g in range(3):
                        b = open_(("E", tag, g))
                        for i in range(4):
                            c, h = divmod(4 * g + i, 6)
                            ins = mm(view(ps, b + i * P, (1, P)), view(sm, GG + c * 12 + d * 6 + h, (0, P)), cc(C_TRI + d * P, P),
                                     start=True, stop=True)
                        close(ins, ("E", tag, g))
                        for i2 in range(2):
                            b = open_(("G", tag, g, i2))
                            for i in range(2):
                                c, h = divmod(4 * g + 2 * i + i2, 6)
                                m, hf = h // 2, h % 2
                                ins = mm(view(ps, b + i * 256, (1, 256)),
                                         view(R, KQ + m * 512 + c * P, (1, P), p0=64 * hf, np_=64),
                                         view(R, KQ + m * 512 + c * P, (256, 2), (1, P), p0=64 * hf, np_=64), start=True, stop=True)
                            close(ins, ("G", tag, g, i2))
                    invert(tag, d, 3, lambda s: view(R, GLT + s * P, (1, P)), "g")
                    for n, c in enumerate((0, 1) if d == 0 else (1, 0)):
                        if n == 1:
                            for w in range(2):
                                b = open_(("KS", tag, w))
                                for m in range(3):
                                    ins = mm(view(ps, b + m * P, (1, P)), view(R, KQ + m * 512 + w * 256 + c * P, (1, P)),
                                             view(hnT, GS + m * P, (1, P)), start=True, stop=True)
                                close(ins, ("KS", tag, w))
                            pe.wait_ge(*at("delta_rhs_ready", tag))
                        b = open_(("U", tag, n))
                        for h in range(6):
                            rhs = view(R, GN + c * 1152 + 768 + h * 64, (1, 64)) if n == 0 else view(R, GR + h * 64, (1, 64))
                            ins = mm(view(ps, b + h * 64, (1, 64)), view(R, XT("g") + (c * 6 + h) * P, (1, P)), rhs, start=True, stop=True)
                        close(ins, ("U", tag, n))
                        pe.wait_ge(*at("bank_read_by_vector", "U", tag, n))
                        b = open_(("PU", tag, n))
                        for h in range(6):
                            ins = mm(view(ps, b + h * 64, (1, 64)), view(R, GPT + (c * 6 + h) * P, (1, P)), view(R, GU + h * 64, (1, 64)),
                                     start=True, stop=True)
                        close(ins, ("PU", tag, n))
                        if n == 0:
                            pe.wait_ge(*at("kd_ready", tag))
                            b = open_(("GS", tag))
                            for h in range(6):
                                ins = mm(view(ps, b + (h // 2) * 64, (1, 64), p0=64 * (h % 2), np_=64),
                                         view(R, GKD + h * 64, (1, 64)), view(R, GU + h * 64, (1, 64)), start=True, stop=True)
                            close(ins, ("GS", tag))
                            pe.wait_ge(*at("bank_read_by_scalar", "GS", tag))

                    if d == 0:
                        pe.wait_ge(*at("kk_squares_ready", L))
                        b = open_(("kkss", L))
                        close(mm(view(ps, b, (1, 512)), cc(C_BLK, P), view(R, RKK2, (1, 512)), start=True, stop=True), ("kkss", L))
                        transposes(("vn", L), [view(hn, RF + (4 + ct) * S + c * P, (1, P)) for c in range(2) for ct in range(2)], "a")

                pe.wait_ge(*at("bonus_terms_ready", L))
                b = open_(("bonus", L))
                for t in range(T):
                    for ct in range(2):
                        ins = mm(view(ps, b + t * 4 + ct * 2, (1, 2)), view(R, RPR + ct * S + t * P, (1, P)),
                                 view(cst, C_BLK, (64, 2)), start=True, stop=True)
                close(ins, ("bonus", L))
                for d in range(2):
                    tag = ("r", L, d)
                    c1 = d
                    pe.wait_ge(*at("rwkv_factors_ready", L, d))
                    transposes(("BKn", tag), [view(R, RBK + d * 1024 + ct * 512 + w * 256 + c1 * P, (1, P)) for w in range(2) for ct in range(2)], "a")
                    for s in range(8):
                        c, h = divmod(s, 4)
                        ct, hf = h // 2, h % 2
                        b = open_(("M4", tag, s))
                        for w in range(2):
                            ins = mm(view(ps, b + w * 256, (1, 256)),
                                     view(R, RBK + d * 1024 + ct * 512 + w * 256 + c * P, (1, P), p0=64 * hf, np_=64),
                                     view(R, RAR + d * 1024 + ct * 512 + c * P, (256, 2), (1, P), p0=64 * hf, np_=64), start=True, stop=True)
                        close(ins, ("M4", tag, s))
                    invert(tag, d, 2, lambda s: view(R, RM4 + s * 512, (1, P)), "r")
                    for n, c in enumerate((0, 1) if d == 0 else (1, 0)):
                        def from_state(b, h, w):
                            mm(view(ps, b + h * 64, (1, P)), view(R, RAR + d * 1024 + (h // 2) * 512 + w * 256 + c * P, (1, P)),
                               view(hnT, RT0 + (h // 2) * P, (1, P)), start=True, stop=False)

                        def m4(h, w):
                            return view(R, RM4 + (c * 4 + h) * 512 + w * P, (1, P))

                        def vn(h):
                            return view(R, RVN + c * 256 + h * 64, (1, 64))
                        if n == 0:
                            pe.wait_ge(*at("bank_read_by_scalar", "vn", L))
                            pe.wait_ge(*at("bank_read_by_scalar", "BKn", tag))
                        b = open_(("r", tag, n))
                        for h in range(4):
                            o = view(ps, b + h * 64, (1, 64))
                            if n == 1 and h % 2 == 0:
                                from_state(b, h, 0)
                            ins = mm(o, m4(h, 2), vn(h), start=n == 0, stop=n == 0 or h % 2 == 1)
                        close(ins, ("r", tag, n))
                        pe.wait_ge(*at("bank_read_by_scalar", "r", tag, n))
                        b = open_(("Ur", tag, n))
                        for h in range(4):
                            ins = mm(view(ps, b + h * 64, (1, 64)), view(R, XT("r") + (c * 4 + h) * P, (1, P)),
                                     view(R, RRH + h * 64, (1, 64)), start=True, stop=True)
                        close(ins, ("Ur", tag, n))
                        pe.wait_ge(*at("bank_read_by_scalar", "Ur", tag, n))
                        b = open_(("Yr", tag, n))
                        for h in range(4):
                            o = view(ps, b + h * 64, (1, 64))
                            if n == 1 and h % 2 == 0:
                                from_state(b, h, 1)
                            mm(o, m4(h, 1), view(R, RU + h * 64, (1, 64)), start=n == 0, stop=False)
                            ins = mm(o, m4(h, 3), vn(h), start=False, stop=n == 0 or h % 2 == 1)
                        close(ins, ("Yr", tag, n))
                        if n == 0:
                            b = open_(("T0", tag))
                            for h in range(4):
                                o = view(ps, b + (h // 2) * 64, (1, 64), p0=64 * (h % 2), np_=64)
                                mm(o, view(R, RBN + h * 64, (1, 64)), view(R, RU + h * 64, (1, 64)), start=True, stop=False)
                                ins = mm(o, view(R, RBN + 256 + h * 64, (1, 64)), vn(h), start=False, stop=True)
                            close(ins, ("T0", tag))
                            pe.wait_ge(*at("bank_read_by_vector", "T0", tag))
                out_proj(L)

        def full(eng, *key):
            eng.wait_ge(*at("bank_full", *key))
            return bank(key)

        def read(engname, *key):
            new_reader[key] = "bank_read_by_" + engname
            return up("bank_read_by_" + engname, *key)

        @block.gpsimd
        def _(pool):
            def load(dst, src, *key, slow=False):
                pool.dma_start(dst, src, allow_slow_non_contiguous=slow).then_inc(*up(*key, by=16))

            def brow(o, src, name="row_params_in"):
                n = 1
                for s_ in src.shape:
                    n *= s_
                load(view(rows, o, (1, n)), bass.AP(src.tensor, src.offset, [[0, P], [1, n]]), name, o)
            for i, nm in enumerate(("ev_lam_q1", "ev_lam_k1", "ev_lam_q2", "ev_lam_k2")):
                brow(R_LAM + 64 * i, a[nm], "lambda_rows_in")
            brow(R_SUB, a["ev_subln"])
            brow(R_GN, a["gdn_norm_g_2"])
            brow(R_LNG, a["rwkv_ln_g_2"])
            brow(R_LNB, a["rwkv_ln_b_2"])
            brow(R_FIN, a["norm_final"])
            brow(R_AL, a["gdn_a_log_2"])
            brow(R_DT, a["gdn_dt_bias_2"])
            load(view(cmpw, 0, (1, 64)), a["ev_cmp_w2_k"][0], "row_params_in", "w2k")
            load(view(cmpw, 64, (1, 64)), a["ev_cmp_w2_v"][0], "row_params_in", "w2v")
            load(bass.AP(posi, 0, [[T, P], [1, T]]), a["positions_2"].rearrange("b (t p) -> p (b t)", p=P), "row_params_in", "all", slow=True)


        @block.scalar
        def _(act):
            def step(ins):
                s, _ = up("scalar_step", C.value.get("scalar_step", 0))
                ins.then_inc(s, 1)
                act.wait_ge(s, C.value["scalar_step"])

            def say(ins, ev):
                ins.then_inc(*ev)
                act.wait_ge(ev[0], C.last)

            A = nc.scalar.activation

            def copy_out(dst, *key, dims=None, n=512, np_=P, scale=1.0):
                b = full(act, *key)
                say(A(dst, view(ps, b, *(dims or ((1, n),)), np_=np_), ACT.Copy, scale=scale), read("scalar", *key))

            def rstd(o, n, scale, eps):
                v = view(sm, o, (1, n))
                step(A(v, v, ACT.Ln, scale=scale, bias=cc(C_EPS + eps)))
                step(A(v, v, ACT.Exp, scale=-0.5))

            def norm(L, which):
                if (which, L) in (("mix", 0), ("mix", 1), ("end", 2), ("mix", 2)):
                    for t in range(T):
                        if L > 0:
                            act.wait_ge(*at("x_updated", which, L, t, 1))
                        step(A(view(hn, t * D, (1, D)), view(x, t * D, (1, D)), ACT.Square, accum_out=view(sm, SS + t, (1, 1))))
                    rstd(SS, T, 1.0 / D, 0)
                    for t in range(T):
                        say(A(view(hn, t * D, (1, D)), view(x, t * D, (1, D)), ACT.Copy, scale=view(sm, SS + t, (1, 1))),
                            up("hn_ready", which, L, t))
                    return
                for t in range(T):
                    act.wait_ge(*at("x_updated", which, L, t, 1))
                    step(A(view(hn, t * D, (1, D)), view(x, t * D, (1, D)), ACT.Square, accum_out=view(sm, SS + t, (1, 1))))
                    rstd(SS + t, 1, 1.0 / D, 0)
                    say(A(view(hn, t * D, (1, D)), view(x, t * D, (1, D)), ACT.Copy, scale=view(sm, SS + t, (1, 1))),
                        up("hn_ready", which, L, t))

            def mlp(L):
                norm(L, "mlp")
                for n in range(8):
                    for m in range(2):
                        act.wait_ge(*at("relu_ready", L, n, m))
                        say(A(view(R, HT + (4 * n + 2 * m) * S, (1, 512)), view(R, RT(m), (1, 512)), ACT.Square),
                            up("hidden_ready", L, n, m))

            def mix_T(L):
                for t in range(T):
                    for q in range(2):
                        copy_out(view(hnT, 4 * q * S + t * P, (S, 4), (1, P)), "mixT", L, t, q, dims=((P, 4), (1, P)))

            def softmax_exp(name, H, shape, width=384, maps=1, between=None):
                for i in range(H + 1):
                    if i < H:
                        for mp in range(maps):
                            act.wait_ge(*at("logits_ready", name, i, mp))
                            b = bank(("S", "mla", name[1], i)) if isinstance(name, tuple) else 0
                            for j, (o, n, t) in enumerate(shape):
                                dst = view(R, PB(i, name) + mp * 384 + o, (1, n))
                                src = view(ps, b + o, (1, n)) if isinstance(name, tuple) else dst
                                ins = A(dst, src, ACT.Exp, scale=1.0 if name[0] == "mla" else 0.125, bias=view(sm, MX(i, mp) + t, (1, 1)), accum_out=view(sm, SU(name, i, mp) + t, (1, 1)))
                                if j == len(shape) - 1:
                                    if name[0] == "mla":
                                        say(ins, read("scalar", "S", "mla", name[1], i))
                                    elif maps == 2:
                                        say(ins, up("diff_exp_ready", i, mp))
                                if not (j == len(shape) - 1) or (maps == 1 and name[0] != "mla"):
                                    if j == len(shape) - 1:
                                        say(ins, up("probs_ready", name, i))
                                    else:
                                        step(ins)
                            if name[0] == "mla":
                                act.sem_inc(up("probs_ready", name, i)[0], 1)
                    if i >= 1:
                        h = i - 1
                        copy_out(view(R, PTB(h, name), (1, width)), "PT", name, h, n=width)
                        if between:
                            between(h)

            CAUSAL = ((0, P, 0), (P, S, 1))

            def load(dst, src, *key, slow=False):
                act.dma_start(dst, src, allow_slow_non_contiguous=slow).then_inc(*up(*key, by=16))
            act.wait_ge(*at("stage_cleared", 0))

            def rload(r0, src, tile=0, w=P):
                load(view(R, STG + tile * P, (1, w), p0=r0, np_=src.shape[0]), src, "column_params_in", "s", tile, r0)
            for nm, r0 in (("norm_mix", CN_MIX), ("norm_mlp", CN_MLP), ("norm_g_2", CN_G2)):
                rload(r0, a[nm].rearrange("l (k p) -> (l k) p", p=P))
            for (c0, _), src in ((K_MU, a["rwkv_mu_2"].rearrange("l e (k p) -> (l e k) p", p=P)),
                                 (K_W0, a["rwkv_w0_2"].rearrange("l e (k p) -> (l e k) p", p=P)),
                                 (K_A0, a["rwkv_a0_2"].rearrange("l e (k p) -> (l e k) p", p=P)),
                                 (K_KK, a["rwkv_k_k_2"].rearrange("l (k p) -> (l k) p", p=P)),
                                 (K_KA, a["rwkv_k_a_2"].rearrange("l (k p) -> (l k) p", p=P)),
                                 (K_RK, a["rwkv_r_k_2"].rearrange("l (k a) d -> (l k) (a d)", a=2)),
                                 (K_QN, a["mla_q_norm_g_2"][:, 0:P]),
                                 (K_KVN, a["mla_kv_norm_g_2"])):
                rload(CL + c0, src)
            rload(CL + K_QN_TAIL[0], a["mla_q_norm_g_2"][:, P:192], w=64)
            rload(0, a["gdn_conv_2"].rearrange("l j (m p) -> (l j m) p", p=P), tile=1)
            for i, nm in enumerate(("ev_cmp_pos_k", "ev_cmp_pos_v")):
                rload(90 + 16 * i, a[nm][0].rearrange("(j e) d -> j (e d)", e=2), tile=1)

            def layer_weights(l):
                load(view(mlaw, 0, (1, 576)), a["mla_w_uq_2"][l, 0:P, :], "mla_weights_in", "a", l)
                load(view(mlaw, 576, (1, 576), np_=64), a["mla_w_uq_2"][l, P:192, :], "mla_weights_in", "b", l)
                load(view(mlaw, 1152, (1, 768)), a["mla_w_ukv_2"][l], "mla_weights_in", l + 2)
                load(view(rww, 0, (256, 2), (1, 256), np_=64), a["rwkv_w2_2"][l].rearrange("e d c -> d e c"), "lora_weights_in", "a", l)
                load(view(rww, 0, (256, 2), (1, 256), p0=64, np_=64), a["rwkv_a2_2"][l].rearrange("e d c -> d e c"), "lora_weights_in", l + 2)
            act.wait_ge(*at("constants_in", 3))
            norm(0, "mix")
            layer_weights(0)
            act.wait_ge(*at("bias_rows_ready", 0))
            act.dma_start(scratch.ap().rearrange("h (q x) -> h q x", q=P), view(R, FR, (0, P), (1, 384), np_=16))\
                .then_inc(*up("bias_rows_stored", 0, by=16))
            act.wait_ge(*at("bias_rows_stored", 0))
            for h in range(16):
                act.dma_start(view(R, BT + h * S, (1, S)), bass.AP(scratch, h * P * 384 + 127, [[383, P], [1, S]]))\
                    .then_inc(*up("bias_tiles_in", h, by=16))

            for m in range(2):
                copy_out(view(R, QT + m * 512, (1, 512)), "q", m)
            copy_out(view(R, KCVC, (1, 512)), "kcvc")
            copy_out(view(R, KST, (1, S)), "ks", n=S)
            for t in range(T):
                copy_out(view(R, VS + t * P, (1, P)), "vs", t, n=P)
            copy_out(view(R, KST + S, (1, S)), "kw", n=S)
            for kind in range(2):
                for g in range(2):
                    for half in range(2):
                        ins = A(view(R, KD + kind * 512 + g * S, (1, S), p0=64 * half, np_=64),
                                view(R, KST + kind * S, (1, S), p0=64 * g, np_=64), ACT.Copy)
                        if (kind, g, half) == (1, 1, 1):
                            say(ins, up("kdup_ready", 0))
                        else:
                            step(ins)
            for t in range(T):
                b = full(act, "vwg", t)
                step(A(view(R, VW + t * P, (1, P)), view(ps, b, (1, P)), ACT.Copy))
                say(A(view(R, GT + t * 24, (1, 24)), view(ps, b + P, (1, 24)), ACT.Exp, scale=-1.0), read("scalar", "vwg", t))
            for i in range(2):
                act.wait_ge(*at("gelu_arg_ready", i))
                say(A(view(R, GE + 60 + 30 * i, (1, 30)), view(R, GE + 60 + 30 * i, (1, 30)), ACT.Exp, scale=2 * math.sqrt(2 / math.pi)),
                    up("gelu_exp_ready", i))
            act.wait_ge(*at("lam_sums_ready", 0))
            say(A(view(sm, LM, (1, 2)), view(sm, LM, (1, 2)), ACT.Exp), up("lam_exp_ready", 0))
            b = full(act, "cmpkv")
            for half in range(2):
                step(A(view(R, KCT, (1, 30), p0=64 * half, np_=64), view(ps, b, (1, 30), np_=64), ACT.Copy))
            say(A(view(R, VCN, (1, 128), np_=15), view(ps, b + 64, (1, 128), np_=15), ACT.Copy), read("scalar", "cmpkv"))
            act.sem_inc(up("cmp_kv_ready", 0)[0], 1)
            act.wait_ge(*at("vbd_cleared", 0))
            for h in range(8):
                act.dma_start(view(R, VBD + h * 64, (1, 64), p0=16 * h, np_=15), view(R, VCN + (h // 4) * 64, (1, 64), np_=15))\
                    .then_inc(*up("vbd_ready", 0, h, by=16))
            def diff_copies(h):
                if h < 4:
                    copy_out(view(R, (DQ, DK)[h // 2] + (h % 2) * 512, (1, 512)), ("dq", "dk")[h // 2], h % 2)
                elif h < 6:
                    copy_out(view(R, DV + (h - 4) * 512, (1, 512)), "dv", h - 4)
            softmax_exp("sel", 8, CAUSAL, between=diff_copies)
            softmax_exp("win", 8, CAUSAL)
            act.wait_ge(*at("cmp_logits_ready", 0))
            say(A(view(R, PC, (1, 256)), view(R, PC, (1, 256)), ACT.Exp), up("cmp_exp_ready", 0))
            copy_out(view(R, PCT, (1, 256)), "PTc", n=256)
            for h in range(5):
                if h < 4:
                    for mp in range(2):
                        act.wait_ge(*at("logits_ready", "diff", h, mp))
                        for o, n, t in CAUSAL:
                            v = view(R, PB(h) + mp * 384 + o, (1, n))
                            ins = A(v, v, ACT.Exp, scale=0.125, bias=view(sm, MX(h, mp) + t, (1, 1)), accum_out=view(sm, SU("diff", h, mp) + t, (1, 1)))
                            if t == 0:
                                step(ins)
                            else:
                                say(ins, up("diff_exp_ready", h, mp))
                if h >= 1:
                    copy_out(view(R, PTB(h - 1), (1, 384)), "PT", "diff", h - 1, n=384)
            act.wait_ge(*at("subln_ss_ready", 0))
            rstd(SB, 8, 1.0 / 128, 0)
            act.sem_inc(up("subln_rstd_ready", 0)[0], 1)
            mix_T(0)
            mlp(0)

            norm(1, "mix")
            for n in range(4):
                for m in range(2):
                    copy_out(view(R, MQ + (4 * n + 2 * m) * S, (1, 512)), "mqk", n, m)
            for n in range(2):
                for t in range(T):
                    copy_out(view(R, MV + t * D + 512 * n, (1, 512)), "mv", n, t)
            softmax_exp("moba", 16, CAUSAL)
            mix_T(1)
            mlp(1)

            norm(2, "end")

            for L in (2, 3):
                norm(L, "mix")
                if L == 2:
                    load(view(rows, R_FIN, (1, D)), bass.AP(a["final_norm_g_2"].tensor, a["final_norm_g_2"].offset, [[0, P], [1, D]]),
                 "final_gain_in", 0)
                for n, m in ((0, 0), (0, 1), (1, 0), (1, 1), (2, 0)):
                    k = 1 if n == 2 else 2
                    copy_out(view(R, GP + (4 * n + 2 * m) * 260 + 2, (260, k), (1, S)), "gqkv", L, n, m, dims=((S, k), (1, S)))
                for t in range(T):
                    copy_out(view(R, LOW + t * 376, (1, 376)), "low", L, t, n=376)
                for m in range(4):
                    k = 1 if m == 3 else 2
                    copy_out(view(R, RP + 2 * m * 258 + 1, (258, k), (1, S)), "rw", L, m, dims=((S, k), (1, S)))
                act.sem_inc(up("low_ready", L)[0], 1)
                for t in range(T):
                    for w, (o, n) in enumerate(((24, 192), (216, 128))):
                        step(A(view(R, CQN + t * 320, (1, n)), view(R, LOW + t * 376 + o, (1, n)), ACT.Square,
                               accum_out=view(sm, SS + 2 * w + t, (1, 1))))
                for o, n in ((SS, 192), (SS + 2, 128)):
                    step(A(view(sm, o, (1, 2)), view(sm, o, (1, 2)), ACT.Ln, scale=1.0 / n, bias=cc(C_EPS)))
                step(A(view(sm, SS, (1, 4)), view(sm, SS, (1, 4)), ACT.Exp, scale=-0.5))
                for t in range(T):
                    for w, (o, n, q) in enumerate(((24, 192, 0), (216, 128, 192))):
                        ins = A(view(R, CQN + t * 320 + q, (1, n)), view(R, LOW + t * 376 + o, (1, n)), ACT.Copy,
                                scale=view(sm, SS + 2 * w + t, (1, 1)))
                        if t == 1 and w == 1:
                            say(ins, up("latents_ready", L))
                        else:
                            step(ins)
                act.wait_ge(*at("conv_sum_ready", L))
                say(A(view(R, GP, (1, 2304)), view(R, GC, (1, 2304)), ACT.Exp, scale=-1.0), up("silu_exp_ready", L))
                for n in range(2):
                    for t in range(T):
                        b = full(act, "gate", L, n, t)
                        o = GATE + t * D + 512 * n
                        step(A(view(R, MIXB + t * D + 512 * n, (1, 512)), view(ps, b, (1, 512)), ACT.Exp, scale=-1.0))
                        say(A(view(R, o, (1, 512)), view(ps, b, (1, 512)), ACT.Copy), read("scalar", "gate", L, n, t))
                act.wait_ge(*at("tanh_arg_ready", L))
                say(A(view(hn, RF + 6 * S, (1, S), np_=64), view(hn, RF + 6 * S, (1, S), np_=64), ACT.Exp, scale=2.0), up("tanh_exp_ready", L))
                if L == 2:
                    act.wait_ge(*at("angles_ready", 0))
                    say(A(view(sm, TRG, (1, 64)), view(sm, TRG, (1, 64)), ACT.Sin), up("trig_ready", 0))
                for t in range(T):
                    for hf in range(2):
                        copy_out(view(R, QN + t * 576 + hf * 288, (1, 288)), "uq", L, t, hf, n=288, scale=96 ** -0.5)
                    for hf in range(2):
                        copy_out(view(R, KV + t * 768 + hf * 384, (1, 384)), "ukv", L, t, hf, n=384)
                for t in range(T):
                    ins = A(view(R, KN + t * 576, (96, 6), (1, 64)), view(R, KV + t * 768, (P, 6), (1, 64)), ACT.Copy)
                    if t == 0:
                        step(ins)
                    else:
                        say(ins, up("uprojected", L))
                for h in range(6):
                    copy_out(view(R, QKT + h * 512, (1, 512), np_=96), "qkT", L, h, np_=96)
                softmax_exp(("mla", L), 6, ((0, S, 0), (S, S, 1)), width=512)

                for e in range(2):
                    for w, (dst, k) in enumerate(((RSW, K_W0), (RSA, K_A0))):
                        b = full(act, "lora", L, e, w)
                        for ct in range(2):
                            ins = A(view(R, dst + e * 512 + ct * S, (1, S)), view(ps, b + ct * S, (1, S)), ACT.Exp, scale=-1.0,
                                    bias=view(sm, NB + (0 if w == 0 else 4) + 2 * e + ct, (1, 1)))
                            if ct == 0:
                                step(ins)
                            else:
                                say(ins, read("scalar", "lora", L, e, w))
                for t in range(T):
                    for w in range(3):
                        copy_out(view(R, GN + t * 1152 + w * 384, (1, 384)), "gn", L, t, w, n=384)
                step(A(view(R, GP, (768, 2), (1, 768)), view(R, GN, (1152, 2), (1, 768)), ACT.Square))
                act.sem_inc(up("qk_squares_ready", L)[0], 1)
                act.wait_ge(*at("qk_ss_ready", L))
                rstd(SS, 24, 1.0, 0)
                act.sem_inc(up("qk_rstd_ready", L)[0], 1)
                act.wait_ge(*at("dt_ready", L))
                step(A(view(sm, GAB, (1, 24)), view(sm, GAB, (1, 24)), ACT.Exp))
                step(A(view(sm, GAB, (1, 24)), view(sm, GAB, (1, 24)), ACT.Ln, bias=cc(C_EPS + 2)))
                step(A(view(sm, GBT, (12, 2), (1, 12)), view(R, LOW + 12, (376, 2), (1, 12)), ACT.Exp, scale=-1.0))
                act.wait_ge(*at("row_params_in", "all"))
                say(A(view(sm, GAL, (1, 12)), view(rows, R_AL + 12 * (L - 2), (1, 12)), ACT.Exp), up("softplus_ready", L))
                for m in range(3):
                    copy_out(view(R, KQ + m * 512, (1, 512)), "kq", L, m)
                act.wait_ge(*at("cum_ready", L))
                step(A(view(sm, GGA, (12, 2), (1, 12)), view(sm, GCU, (24, 2), (1, 12)), ACT.Exp))
                say(A(view(sm, GKF, (12, 2), (1, 12)), view(sm, GKF, (12, 2), (1, 12)), ACT.Exp), up("decay_exp_ready", L))
                for d in range(2):
                    tag = ("g", L, d)
                    for g in range(3):
                        act.wait_ge(*at("exponent_ready", tag, g))
                        say(A(view(R, GE_(g), (1, 512)), view(R, GE_(g), (1, 512)), ACT.Exp), up("decay_matrix_ready", tag, g))
                    for g in range(3):
                        copy_out(view(R, XX("g") + g * 512, (1, 512)), "X0", tag, g)
                    for n in range(len(LEVELS)):
                        for g in range(3):
                            copy_out(view(R, XT("g") + g * 512, (1, 512)), "XT", tag, n, g)
                    if d == 1:
                        act.wait_ge(*at("rwkv_cum_ready", L))
                        step(A(view(R, REP, (1, 1024)), view(R, RCM, (1, 1024)), ACT.Exp))
                        step(A(view(R, RCL, (1, 1024)), view(R, RCL, (1, 1024)), ACT.Exp))
                        step(A(view(sm, RE, (1, 4)), view(sm, RE, (1, 4)), ACT.Exp))
                        say(A(view(R, RCM, (1, 1024)), view(R, RCM, (1, 1024)), ACT.Exp, scale=-1.0), up("rwkv_exp_ready", L))
                    b = full(act, "GS", tag)
                    step(A(view(hnT, GS, (P, 3), (1, 64), np_=64), view(ps, b, (64, 3), (1, 64), np_=64), ACT.Copy))
                    say(A(view(hnT, GS + 64, (P, 3), (1, 64), p0=64, np_=64), view(ps, b, (64, 3), (1, 64), p0=64, np_=64), ACT.Copy),
                        read("scalar", "GS", tag))
                    if d == 0:
                        b = full(act, "kkss", L)
                        step(A(view(R, RKK2, (1, 512)), view(ps, b, (1, 512)), ACT.Ln, bias=cc(C_EPS)))
                        say(A(view(R, RKK2, (1, 512)), view(R, RKK2, (1, 512)), ACT.Exp, scale=-0.5), read("scalar", "kkss", L))
                        copy_out(view(R, RVN, (1, 512)), "vn", L)
                act.wait_ge(*at("gdn_ss_ready", L))
                rstd(SS, 12, 1.0 / 64, 0)
                act.sem_inc(up("gdn_rstd_ready", L)[0], 1)

                for d in range(2):
                    tag = ("r", L, d)
                    copy_out(view(R, RBN, (1, 512)), "BKn", tag)
                    for g in range(2):
                        copy_out(view(R, XX("r") + g * 512, (1, 512)), "X0", tag, g)
                    for n in range(len(LEVELS)):
                        for g in range(2):
                            copy_out(view(R, XT("r") + g * 512, (1, 512)), "XT", tag, n, g)
                    for n in range(2):
                        copy_out(view(R, RRH, (1, 256)), "r", tag, n, n=256, scale=-1.0)
                        copy_out(view(R, RU, (1, 256)), "Ur", tag, n, n=256)
                act.wait_ge(*at("rwkv_var_ready", L))
                rstd(SS, 8, 1.0 / 64, 1)
                act.sem_inc(up("rwkv_rstd_ready", L)[0], 1)
                if L == 2:
                    layer_weights(1)
                mix_T(L)
            norm(4, "fin")

        @block.vector
        def _(dve):
            V = nc.vector

            def step(ins):
                s, _ = up("vector_step", C.value.get("vector_step", 0))
                ins.then_inc(s, 1)
                dve.wait_ge(s, C.value["vector_step"])

            def go(ins):
                ins.then_inc(up("vector_step", C.value.get("vector_step", 0))[0], 1)

            def settle():
                dve.wait_ge(C.sem("vector_step"), C.value["vector_step"])

            def say(ins, ev):
                ins.then_inc(*ev)
                dve.wait_ge(ev[0], C.last)

            def tt(o, p_, q, op):
                step(V.tensor_tensor(o, p_, q, op))

            def ts(o, i, s1, s2, op0, op1=None):
                step(V.tensor_scalar(o, i, s1, s2, op0, op1) if op1 is not None else V.tensor_scalar(o, i, s1, None, op0))

            def recip(o, i):
                step(V.reciprocal(o, i))

            def signal(*key):
                dve.sem_inc(up(*key)[0], 1)

            def normed_T(L, which):
                base = {"mix": (CN_MIX, CN_MIX + 8, CN_G2, CN_G2 + 8)[L] if L < 4 else 0, "mlp": CN_MLP + 8 * L}[which]
                for t in range(T):
                    for q in range(2):
                        key = ("hnT", which, L, t, q)
                        b = full(dve, *key)
                        say(V.tensor_tensor(view(hnT, 4 * q * S + t * P, (S, 4), (1, P)), view(ps, b, (P, 4), (1, P)),
                                            view(cols, base + 4 * q, (1, 4), (0, P)), MUL), read("vector", *key))

            def residual(kind, L, nxt, nL):
                for t in range(T):
                    for half in range(2):
                        key = (kind, L, half, t) if kind == "o" else (kind, L, 2 * t + half)
                        b = full(dve, *key)
                        v = view(x, t * D + 512 * half, (1, 512))
                        say(V.tensor_tensor(v, view(ps, b, (1, 512)), v, ADD), read("vector", *key))
                        signal("x_updated", nxt, nL, t, half)

            def mlp(L):
                normed_T(L, "mlp")
                for n in range(8):
                    for m in range(2):
                        b = full(dve, "h", L, n, m)
                        if n > 0:
                            dve.wait_ge(*at("hidden_ready", L, n - 1, m))
                        say(V.tensor_scalar(view(R, RT(m), (1, 512)), view(ps, b, (1, 512)), 0.0, None, MAX), read("vector", "h", L, n, m))
                        signal("relu_ready", L, n, m)
                residual("y", L, "mix" if L == 0 else "end", L + 1)

            def logits(name, h, mp, key, bh):
                b = full(dve, *key)
                v = [view(R, PB(h) + mp * 384 + o, (1, n)) for o, n in ((0, P), (P, S))]
                go(V.tensor_tensor(v[0], view(ps, b, (1, P)), view(R, BT + bh * S + P, (1, P)), ADD))
                say(V.tensor_tensor(v[1], view(ps, b + P, (1, S)), view(R, BT + bh * S, (1, S)), ADD), read("vector", *key))
                for t in range(T):
                    go(V.tensor_reduce(view(sm, MX(h, mp) + t, (1, 1)), v[t], AX.X, MAX))
                settle()
                ts(view(sm, MX(h, mp), (1, 2)), view(sm, MX(h, mp), (1, 2)), -0.125, None, MUL)
                signal("logits_ready", name, h, mp)

            def head_out(name, H, dst, coef, first, per=8, vw=64, groups=None):
                for gq in groups or range((H + per - 1) // per):
                    n = min(per, H - gq * per)
                    for t in range(T):
                        b = full(dve, "O", name, gq, t)
                        o = dst(t) + gq * per * vw
                        src = view(ps, b, (vw, n), (1, vw))
                        cf = coef(t, gq * per, n)
                        if first:
                            say(V.tensor_tensor(view(R, o, (vw, n), (1, vw)), src, cf, MUL), read("vector", "O", name, gq, t))
                        else:
                            say(V.tensor_tensor(view(hn, 0, (vw, n), (1, vw)), src, cf, MUL), read("vector", "O", name, gq, t))
                            tt(view(R, o, (vw, n), (1, vw)), view(R, o, (vw, n), (1, vw)), view(hn, 0, (vw, n), (1, vw)), ADD)

            step(V.memset(view(R, STG, (1, 2 * P)), 0.0))
            signal("stage_cleared", 0)
            dve.wait_ge(*at("constants_in", 3))
            b = full(dve, "cols")
            say(V.tensor_copy(cols[:, :], view(ps, b, (1, 2 * P))), read("vector", "cols"))
            b = full(dve, "bias")
            say(V.scalar_tensor_tensor(view(R, FR, (1, 384), np_=16), view(ps, b, (1, 384), np_=16), 8.0,
                                       view(R, OH + 384, (1, 384), np_=16), MUL, ADD), read("vector", "bias"))
            signal("bias_rows_ready", 0)
            dve.wait_ge(*at("lambda_rows_in", R_LAM + 192))
            for i in range(2):
                tt(view(R, GE, (1, 64)), view(rows, R_LAM + 128 * i, (1, 64)), view(rows, R_LAM + 128 * i + 64, (1, 64)), MUL)
                step(V.tensor_reduce(view(sm, LM + i, (1, 1)), view(R, GE, (1, 64)), AX.X, ADD))
            signal("lam_sums_ready", 0)
            normed_T(0, "mix")
            dve.wait_ge(*at("bank_read_by_scalar", "kcvc"))
            for i in range(2):
                for g in range(2):
                    for par in range(2):
                        tt(view(R, BLK + i * 480 + g * 240, (15, 16), (1, 15), p0=64 * par, np_=64),
                           view(R, KCVC + i * S + par, (2, 16), (16, 15), p0=64 * g, np_=64),
                           view(cols, CB_POS + 16 * i, (1, 16), (0, 15), p0=64 * par, np_=64), ADD)
            signal("cmp_blocks_ready", 1)
            dve.wait_ge(*at("bank_read_by_scalar", "vwg", 1))
            ts(view(R, GT, (1, 48)), view(R, GT, (1, 48)), 1.0, None, ADD)
            recip(view(R, GT, (1, 48)), view(R, GT, (1, 48)))
            for i in range(2):
                h_, u_ = view(R, GE + 30 * i, (1, 30)), view(R, GE + 60 + 30 * i, (1, 30))
                b = full(dve, "hid", i)
                say(V.tensor_copy(h_, view(ps, b, (1, 30))), read("vector", "hid", i))
                tt(u_, h_, h_, MUL)
                ts(u_, u_, 0.044715, 1.0, MUL, ADD)
                tt(u_, u_, h_, MUL)
                ts(u_, u_, 20.0, None, MIN)
                signal("gelu_arg_ready", i)
            for i in range(2):
                h_, u_ = view(R, GE + 30 * i, (1, 30)), view(R, GE + 60 + 30 * i, (1, 30))
                dve.wait_ge(*at("gelu_exp_ready", i))
                ts(u_, u_, 1.0, None, ADD)
                recip(u_, u_)
                ts(u_, u_, -1.0, 1.0, MUL, ADD)
                tt(view(R, HID + 30 * i, (1, 30)), u_, h_, MUL)
            signal("cmp_hidden_ready", 1)
            dve.wait_ge(*at("lam_exp_ready", 0))
            tt(view(sm, LM, (1, 1)), view(sm, LM + 1, (1, 1)), view(sm, LM, (1, 1)), SUB)
            ts(view(sm, LM, (1, 1)), view(sm, LM, (1, 1)), -LAM_INIT, None, ADD)
            step(V.memset(view(R, VBD, (1, 512)), 0.0))
            signal("vbd_cleared", 0)
            dve.wait_ge(*at("bias_tiles_in", 15))

            def softmax(name, H, bh, between=None):
                for h in range(H):
                    if between and h == 11:
                        between()
                    if h >= 3:
                        dve.wait_ge(*at("bank_full", "PT", name, h - 3))
                    logits(name, h, 0, ("S", name, h), bh(h))

            for gi, nm in ((1, "sel"), (2, "win")):
                softmax(nm, 8, lambda h: h)
                dve.wait_ge(*at("probs_ready", nm, 7))
                su = view(sm, SU(nm, 0, 0), (2, 8), (1, 2))
                recip(su, su)
                tt(su, su, view(R, GT + gi * 8, (1, 8), (24, 2)), MUL)
                head_out(nm, 8, lambda t: MIX(0) + t * D,
                         lambda t, h0, n, nm=nm: view(sm, SU(nm, 0, 0) + t, (2, n), (0, 64)), nm == "sel")
            for par in range(2):
                b = full(dve, "Sc", par)
                for t in range(T):
                    nv, k0 = (15, 31) if t == 1 else (7, 159)
                    pc = PC + t * P + par * 16
                    if par == 0:
                        step(V.memset(view(R, PC + t * P, (1, P)), 8 * NEG))
                    ins = V.tensor_tensor(view(R, pc, (32, 4), (1, nv)), view(ps, b + t * 64, (16, 4), (1, nv)),
                                          view(R, BT + par * S + k0, (2 * S, 4), (16, nv)), ADD)
                    if t == 0:
                        step(ins)
                    else:
                        say(ins, read("vector", "Sc", par))
            allp = view(R, PC, (16, 16), (1, 16))
            mx = view(sm, CM, (1, 16))
            step(V.tensor_reduce(mx, allp, AX.X, MAX))
            tt(allp, allp, view(sm, CM, (1, 16), (0, 16)), SUB)
            ts(view(R, PC, (1, 256)), view(R, PC, (1, 256)), 0.125, None, MUL)
            signal("cmp_logits_ready", 0)
            dve.wait_ge(*at("cmp_exp_ready", 0))
            step(V.memset(view(R, PC + 15, (16, 16)), 0.0))
            signal("cmp_probs_ready", 0)
            step(V.tensor_reduce(mx, allp, AX.X, ADD))
            recip(mx, mx)
            for t in range(T):
                tt(view(sm, CM + 8 * t, (1, 8)), view(sm, CM + 8 * t, (1, 8)), view(R, GT + 24 * t, (1, 8)), MUL)
                ts(view(sm, CM + 8 * t, (1, 8)), view(sm, CM + 8 * t, (1, 8)), cc(C_ROWOK + t), None, MUL)
                b = full(dve, "Oc", t)
                say(V.tensor_tensor(view(hn, 0, (64, 8), (1, 64)), view(ps, b, (64, 8), (1, 64)),
                                    view(sm, CM + 8 * t, (1, 8), (0, 64)), MUL), read("vector", "Oc", t))
                tt(view(R, MIX(0) + t * D, (1, 512)), view(R, MIX(0) + t * D, (1, 512)), view(hn, 0, (1, 512)), ADD)
            for i in range(5):
                if i < 4:
                    if i >= 3:
                        dve.wait_ge(*at("bank_full", "PT", "diff", i - 3))
                    for mp in range(2):
                        logits("diff", i, mp, ("S", "diff", i, mp), 8 + i)
                if i >= 1:
                    h = i - 1
                    dve.wait_ge(*at("diff_exp_ready", h, 1))
                    c0, c1 = SU("diff", h, 0), SU("diff", h, 1)
                    recip(view(sm, c0, (1, 2)), view(sm, c0, (1, 2)))
                    recip(view(sm, c1, (1, 2)), view(sm, c1, (1, 2)))
                    ts(view(sm, c1, (1, 2)), view(sm, c1, (1, 2)), view(sm, LM, (1, 1)), None, MUL)
                    for o, n, t in ((0, P, 0), (P, S, 1)):
                        p0_, p1_ = view(R, PB(h) + o, (1, n)), view(R, PB(h) + 384 + o, (1, n))
                        ts(p1_, p1_, view(sm, c1 + t, (1, 1)), None, MUL)
                        step(V.scalar_tensor_tensor(p0_, p0_, view(sm, c0 + t, (1, 1)), p1_, MUL, ADD))
                    signal("diff_probs_ready", "diff", h)
            for t in range(T):
                b = full(dve, "O", "diff", 0, t)
                say(V.tensor_copy(view(R, MIX(0) + t * D + 512, (1, 512)), view(ps, b, (1, 512))), read("vector", "O", "diff", 0, t))
                v = view(R, MIX(0) + t * D + 512, (1, 512))
                tt(view(hn, 0, (1, 512)), v, v, MUL)
                step(V.tensor_reduce(view(sm, SB + 4 * t, (1, 4)), view(hn, 0, (P, 4), (1, P)), AX.X, ADD))
            signal("subln_ss_ready", 0)
            dve.wait_ge(*at("subln_rstd_ready", 0))
            dve.wait_ge(*at("row_params_in", "all"))
            for t in range(T):
                v = view(R, MIX(0) + t * D + 512, (P, 4), (1, P))
                tt(v, v, view(sm, SB + 4 * t, (1, 4), (0, P)), MUL)
                ts(v, v, 1.0 - LAM_INIT, None, MUL)
                tt(v, v, view(rows, R_SUB, (0, 4), (1, P)), MUL)
                signal("mix_ready", 0, t)
            residual("o", 0, "mlp", 0)
            mlp(0)

            normed_T(1, "mix")
            def moba_out(g):
                dve.wait_ge(*at("probs_ready", "moba", 8 * g + 7))
                su = view(sm, SU("moba", 8 * g, 0), (1, 16))
                recip(su, su)
                head_out("moba", 16, lambda t: MIX(1) + t * D,
                         lambda t, h0, n: view(sm, SU("moba", 0, 0) + 2 * h0 + t, (2, n), (0, 64)), True, groups=(g,))
            softmax("moba", 16, lambda h: h, lambda: moba_out(0))
            moba_out(1)
            for t in range(T):
                signal("mix_ready", 1, t)
            residual("o", 1, "mlp", 1)
            mlp(1)
            for t in range(T):
                dve.wait_ge(*at("hn_ready", "end", 2, t))
                tt(view(x, t * D, (1, D)), view(hn, t * D, (1, D)), view(rows, R_FIN, (1, D)), MUL)
                signal("x_updated", "mix", 2, t, 1)

            step(V.tensor_copy(view(sm, PF, (1, 2)), bass.AP(posi, 0, [[T, P], [1, T]])))
            for t in range(T):
                for w, ph in enumerate((0.25, 0.0)):
                    v = view(sm, TRG + w * 32 + t * 16, (1, 16))
                    k_ = view(sm, TRK, (1, 16))
                    ts(v, cc(C_FRQ, 16), view(sm, PF + t, (1, 1)), None, MUL)
                    ts(k_, v, 1.0 / (2 * math.pi), ph, MUL, ADD)
                    ts(k_, k_, 12582912.0, None, ADD)
                    ts(k_, k_, -12582912.0, None, ADD)
                    step(V.scalar_tensor_tensor(v, k_, -6.28125, v, MUL, ADD))
                    step(V.scalar_tensor_tensor(v, k_, -(2 * math.pi - 6.28125), v, MUL, ADD))
                    ts(v, v, ph * 2 * math.pi, 3.1415925, ADD, MIN)
                    ts(v, v, -3.1415925, None, MAX)
            signal("angles_ready", 0)

            def invert(tag, d, ngroups, LTs, st, between=None):
                lt, stp = LTs
                for g in range(ngroups):
                    v = view(R, XT(st) + g * 512, (P, 4), (1, P))
                    tt(v, view(R, lt + 4 * g * stp, (stp, 4), (1, P)), view(cst, C_M1 + d * P, (0, 4), (1, P)), MUL)
                    tt(v, view(cst, C_ID, (0, 4), (1, P)), v, SUB)
                    signal("inverse_seed_ready", tag, g)
                for n, m in enumerate(LEVELS):
                    e = 0 if d == 0 else m
                    np2 = P // (2 * m)
                    packed = ((64, 4), (m, np2), (1, m))
                    for g in range(ngroups):
                        key = ("Y", tag, n, g)
                        b = full(dve, *key)
                        say(V.tensor_tensor(view(R, YY(st) + g * 256, *packed), view(ps, b, *packed),
                                            view(cst, C_LV + (d * len(LEVELS) + n) * P + e, (0, 4), (2 * m, np2), (1, m)), MUL),
                            read("vector", *key))
                    if between:
                        between(n)
                    for g in range(ngroups):
                        key = ("Z", tag, n, g)
                        b = full(dve, *key)
                        v = view(R, XX(st) + g * 512 + e, (2 * m, 4 * np2), (1, m))
                        say(V.tensor_tensor(v, v, view(ps, b, (m, 4 * np2), (1, m)), SUB), read("vector", *key))

            for L in (2, 3):

                def col(k, i=0, n=1, p0=0, np_=P):
                    return view(cols, CL + k[0] + k[1] * (L - 2) + i, (1, n), p0=p0, np_=np_)
                if L == 3:
                    dve.wait_ge(*at("x_updated", "mix", L, 1, 1))
                step(V.memset(view(R, GP, (260, 9), (1, 2)), 0.0))
                step(V.memset(view(R, GP + 258, (260, 9), (1, 2)), 0.0))
                step(V.memset(view(R, RP, (257, 2), (258, 7)), 0.0))
                normed_T(L, "mix")
                dve.wait_ge(*at("bank_read_by_scalar", "gqkv", L, 2, 0))
                for j in range(5):
                    for m in range(9):
                        w = view(cols, CB_CONV + 45 * (L - 2) + 9 * j + m, (1, 1))
                        o = view(R, GC + m * S, (1, S))
                        tap = view(R, GP + m * 260 + j, (1, S))
                        if j == 0:
                            go(V.tensor_scalar(o, tap, w, None, MUL))
                        else:
                            go(V.scalar_tensor_tensor(o, tap, w, o, MUL, ADD))
                    settle()
                signal("conv_sum_ready", L)
                for t in range(T):
                    b = full(dve, "cT", L, t)
                    ts(view(R, CT + t * P, (1, P)), view(ps, b, (1, P)), col(K_QN), None, MUL)
                    ts(view(R, CT + 256 + t * P, (1, P), np_=64), view(ps, b + P, (1, P), np_=64), col(K_QN_TAIL, np_=64), None, MUL)
                    say(V.tensor_scalar(view(R, CT + 512 + t * P, (1, P)), view(ps, b + 2 * P, (1, P)), col(K_KVN), None, MUL),
                        read("vector", "cT", L, t))
                    signal("latents_T_ready", L, t)
                dve.wait_ge(*at("silu_exp_ready", L))
                e_ = view(R, GP, (1, 2304))
                ts(e_, e_, 1.0, None, ADD)
                recip(e_, e_)
                tt(view(R, GC, (1, 2304)), view(R, GC, (1, 2304)), e_, MUL)
                signal("conv_ready", L)
                dve.wait_ge(*at("bank_read_by_scalar", "rw", L, 3))
                step(V.tensor_tensor(view(sm, MU, (1, 7)), col(K_MU, 0, 7), col(K_MU, 7, 7), ADD))
                ts(view(sm, MU, (1, 7)), view(sm, MU, (1, 7)), -1.0, 1.0, MUL, ADD)
                for j, (off, k) in enumerate(((1, None), (0, 0), (2, 7))):
                    for m in range(7):
                        o = view(hn, RF + m * S, (1, S))
                        tap = view(R, RP + m * 258 + off, (1, S))
                        if j == 0:
                            go(V.tensor_scalar(o, tap, view(sm, MU + m, (1, 1)), None, MUL))
                        else:
                            go(V.scalar_tensor_tensor(o, tap, col(K_MU, k + m), o, MUL, ADD))
                    settle()
                w6 = view(hn, RF + 6 * S, (1, S), np_=64)
                ts(w6, w6, 20.0, None, MIN)
                signal("tanh_arg_ready", L)
                ts(view(sm, NB, (1, 4)), col(K_W0, n=4), -1.0, None, MUL)
                ts(view(sm, NB + 4, (1, 4)), col(K_A0, n=4), -1.0, None, MUL)
                dve.wait_ge(*at("tanh_exp_ready", L))
                ts(w6, w6, 1.0, None, ADD)
                recip(w6, w6)
                ts(w6, w6, -2.0, 1.0, MUL, ADD)
                signal("shifted_ready", L)
                dve.wait_ge(*at("uprojected", L))
                dve.wait_ge(*at("trig_ready", 0))
                for t in range(T):
                    cs, sn = TRG + t * 16, TRG + 32 + t * 16
                    for o, hs, H_ in ((QN + t * 576 + 64, 96, 6), (LOW + t * 376 + 344, 96, 1)):
                        x1, x2 = view(R, o, (hs, H_), (1, 16)), view(R, o + 16, (hs, H_), (1, 16))
                        tc = [view(R, RTM + 96 * i, (16, H_), (1, 16)) for i in range(4)]
                        c_, s_ = view(sm, cs, (0, H_), (1, 16)), view(sm, sn, (0, H_), (1, 16))
                        go(V.tensor_tensor(tc[0], x1, c_, MUL))
                        go(V.tensor_tensor(tc[1], x2, s_, MUL))
                        go(V.tensor_tensor(tc[2], x2, c_, MUL))
                        go(V.tensor_tensor(tc[3], x1, s_, MUL))
                        settle()
                        go(V.tensor_tensor(x1, tc[0], tc[1], SUB))
                        go(V.tensor_tensor(x2, tc[2], tc[3], ADD))
                        settle()
                    step(V.tensor_copy(view(R, KN + t * 576 + 64, (96, 6), (1, 32)), view(R, LOW + t * 376 + 344, (0, 6), (1, 32))))
                signal("rope_ready", L)
                dve.wait_ge(*at("bank_read_by_scalar", "gate", L, 1, 1))
                name = ("mla", L)
                for h in range(6):
                    b = full(dve, "S", "mla", L, h)
                    step(V.tensor_reduce(view(sm, MX(h, 0), (1, 2)), view(ps, b, (S, 2), (1, S)), AX.X, MAX))
                    ts(view(sm, MX(h, 0), (1, 2)), view(sm, MX(h, 0), (1, 2)), -1.0, None, MUL)
                    if h >= 3:
                        dve.wait_ge(*at("bank_full", "PT", name, h - 3))
                    signal("logits_ready", name, h, 0)
                    n = min(384, 2048 - 384 * h)
                    e_, g_ = view(R, MIXB + 384 * h, (1, n)), view(R, GATE + 384 * h, (1, n))
                    ts(e_, e_, 1.0, None, ADD)
                    recip(e_, e_)
                    tt(g_, g_, e_, MUL)
                dve.wait_ge(*at("probs_ready", name, 5))
                su = view(sm, SU(name, 0, 0), (1, 12))
                recip(su, su)
                head_out(name, 6, lambda t: MIXB + t * D + 384, lambda t, h0, n: view(sm, SU(name, 0, 0) + t, (2, n), (0, 64)), True)

                dtv = view(sm, GSP, (12, 2), (1, 12))
                tt(dtv, view(R, LOW, (376, 2), (1, 12)), view(rows, R_DT + 12 * (L - 2), (0, 2), (1, 12)), ADD)
                neg = view(sm, GAB, (1, 24))
                ts(neg, view(sm, GSP, (1, 24)), -1.0, None, MUL)
                tt(neg, neg, view(sm, GSP, (1, 24)), MIN)
                ts(view(sm, GSP, (1, 24)), view(sm, GSP, (1, 24)), 0.0, None, MAX)
                signal("dt_ready", L)
                dve.wait_ge(*at("qk_squares_ready", L))
                step(V.tensor_reduce(view(sm, SS, (1, 24)), view(R, GP, (64, 24), (1, 64)), AX.X, ADD))
                signal("qk_ss_ready", L)
                dve.wait_ge(*at("qk_rstd_ready", L))
                ts(view(sm, SS, (12, 2), (1, 6)), view(sm, SS, (12, 2), (1, 6)), 0.125, None, MUL)
                for t in range(T):
                    v = view(R, GN + t * 1152, (64, 12), (1, 64))
                    tt(v, v, view(sm, SS + 12 * t, (1, 12), (0, 64)), MUL)
                signal("qk_normed", L)
                dve.wait_ge(*at("softplus_ready", L))
                tt(view(sm, GSP, (1, 24)), view(sm, GSP, (1, 24)), neg, ADD)
                ts(view(sm, GBT, (1, 24)), view(sm, GBT, (1, 24)), 1.0, None, ADD)
                recip(view(sm, GBT, (1, 24)), view(sm, GBT, (1, 24)))
                tt(view(sm, GG, (12, 2), (1, 12)), dtv, view(sm, GAL, (0, 2), (1, 12)), MUL)
                ts(view(sm, GG, (1, 24)), view(sm, GG, (1, 24)), -1.0, None, MUL)
                signal("decay_ready", L)
                b = full(dve, "cum", L)
                say(V.tensor_copy(view(sm, GCU, (1, 48)), view(ps, b, (1, 48))), read("vector", "cum", L))
                tt(view(sm, GKF, (12, 2), (1, 12)), view(sm, GCU + 12, (24, 2), (1, 12)), view(sm, GCU, (24, 2), (1, 12)), SUB)
                signal("cum_ready", L)
                dve.wait_ge(*at("decay_exp_ready", L))
                def rwkv_prepare(n):
                    if n == 0:
                        kx = view(R, RKX, (1, 512))
                        for ct in range(2):
                            ts(view(R, RKX + ct * S, (1, S)), view(hn, RF + (2 + ct) * S, (1, S)), col(K_KK, ct), None, MUL)
                        tt(view(R, RKK2, (1, 512)), kx, kx, MUL)
                        signal("kk_squares_ready", L)
                    if n in (1, 2):
                        v = view(R, (RSW, RSA)[n - 1], (1, 1024))
                        ts(v, v, 1.0, None, ADD)
                        recip(v, v)
                    if n == 3:
                        v = view(R, RSW, (1, 1024))
                        ts(v, v, -math.exp(-0.5), None, MUL)
                        ts(view(sm, NB + 8, (1, 2)), col(K_KA, n=2), -1.0, 1.0, MUL, ADD)
                        for d in range(2):
                            for ct in range(2):
                                o = view(R, RKM + d * 512 + ct * S, (1, S))
                                ts(o, view(R, RSA + d * 512 + ct * S, (1, S)), col(K_KA, ct), view(sm, NB + 8 + ct, (1, 1)), MUL, ADD)
                            tt(view(R, RKM + d * 512, (1, 512)), view(R, RKM + d * 512, (1, 512)), view(hn, RF + 2 * S, (1, 512)), MUL)
                    if n in (4, 5):
                        d = n - 4
                        for ct in range(2):
                            for c in range(2):
                                q0 = d * 512 + ct * S + c * P
                                first, stp = (0, 1) if d == 0 else (P - 1, -1)
                                step(V.tensor_tensor_scan(view(R, RCM + q0 + first, (stp, P)), view(cst, C_ONE, (1, P)),
                                                          view(R, RSW + q0 + first, (stp, P)), 0.0, MUL, ADD))
                                q = d * 4 + ct * 2 + c
                                mid, end = (63, P - 1) if d == 0 else (64, 0)
                                ts(view(sm, RMD + q, (1, 1)), view(R, RCM + q0 + mid, (1, 1)), 1.0, None, MUL)
                                ts(view(sm, REN + q, (1, 1)), view(R, RCM + q0 + end, (1, 1)), 1.0, None, MUL)
                                ts(view(R, RCM + q0, (1, P)), view(R, RCM + q0, (1, P)), view(sm, RMD + q, (1, 1)), None, SUB)
                            q = d * 4 + ct * 2
                            tt(view(sm, RE + d * 2 + ct, (1, 1)), view(sm, REN + q + d, (1, 1)), view(sm, RMD + q + d, (1, 1)), SUB)
                            tt(view(sm, RE + d * 2 + ct, (1, 1)), view(sm, RE + d * 2 + ct, (1, 1)), view(sm, RMD + q + 1 - d, (1, 1)), ADD)

                def rwkv_bonus(n):
                    if n == 0:
                        kx = view(R, RKX, (1, 512))
                        dve.wait_ge(*at("bank_read_by_scalar", "kkss", L))
                        tt(kx, kx, view(R, RKK2, (1, 512)), MUL)
                        pr = view(R, RPR, (1, 512))
                        tt(pr, view(R, RKM, (1, 512)), view(R, RKM + 512, (1, 512)), ADD)
                        tt(pr, pr, view(hn, RF, (1, 512)), MUL)
                        for ct in range(2):
                            v = view(R, RPR + ct * S, (1, S))
                            ts(v, v, col(K_RK, ct), 0.5, MUL, MUL)
                        signal("bonus_terms_ready", L)
                        tt(view(R, RCL, (1, 1024)), view(R, RCM, (1, 1024)), view(R, RSW, (1, 1024)), SUB)
                        signal("rwkv_cum_ready", L)

                for d in range(2):
                    tag = ("g", L, d)
                    for g in range(3):
                        b = full(dve, "E", tag, g)
                        for i in range(4):
                            c, h = divmod(4 * g + i, 6)
                            ins = V.scalar_tensor_tensor(view(R, GE_(g) + i * P, (1, P)), view(ps, b + i * P, (1, P)),
                                                         view(sm, GCU + c * 24 + d * 6 + h, (1, 1)), cc(C_NEG + d * P, P), SUB, ADD)
                            if i < 3:
                                go(ins)
                            else:
                                say(ins, read("vector", "E", tag, g))
                        signal("exponent_ready", tag, g)
                        dve.wait_ge(*at("decay_matrix_ready", tag, g))
                        for i2 in range(2):
                            b = full(dve, "G", tag, g, i2)
                            for i in range(2):
                                s = 4 * g + 2 * i + i2
                                c, h = divmod(s, 6)
                                ev = view(R, GE_(g) + (2 * i + i2) * P, (1, P))
                                go(V.scalar_tensor_tensor(view(R, GLT + s * P, (1, P)), view(ps, b + i * 256, (1, P)),
                                                            view(sm, GBT + c * 12 + d * 6 + h, (1, 1)), ev, MUL, MUL))
                                ins = V.tensor_tensor(view(R, GPT + s * P, (1, P)), view(ps, b + i * 256 + P, (1, P)), ev, MUL)
                                if i == 0:
                                    go(ins)
                                else:
                                    say(ins, read("vector", "G", tag, g, i2))
                    c1 = d
                    kd = view(R, GKD, (64, 6), (1, 64))
                    tt(kd, view(R, GN + c1 * 1152 + 384, (64, 6), (1, 64)), view(sm, GKF + c1 * 12 + d * 6, (1, 6), (0, 64)), MUL)
                    if d == 0:
                        step(V.memset(view(hnT, GS, (1, 640)), 0.0))
                    signal("kd_ready", tag)
                    dve.wait_ge(*at("bank_read_by_scalar", "lora", L, 1, 1))
                    invert(tag, d, 3, (GLT, P), "g", rwkv_prepare if d == 0 else rwkv_bonus)
                    for n, c in enumerate((0, 1) if d == 0 else (1, 0)):
                        gam = view(sm, GGA + c * 12 + d * 6, (1, 6), (0, 64))
                        tmp = view(R, GR, (64, 6), (1, 64))
                        if n == 1:
                            b = full(dve, "KS", tag, 0)
                            say(V.tensor_tensor(tmp, view(ps, b, (64, 6), (1, 64)), gam, MUL), read("vector", "KS", tag, 0))
                            tt(view(R, GR, (1, 384)), view(R, GN + c * 1152 + 768, (1, 384)), view(R, GR, (1, 384)), SUB)
                            signal("delta_rhs_ready", tag)
                        b = full(dve, "U", tag, n)
                        say(V.tensor_tensor(view(R, GU, (64, 6), (1, 64)), view(ps, b, (64, 6), (1, 64)),
                                            view(sm, GBT + c * 12 + d * 6, (1, 6), (0, 64)), MUL), read("vector", "U", tag, n))
                        o = view(R, GO + c * 384, (1, 384))
                        if n == 1:
                            b = full(dve, "KS", tag, 1)
                            say(V.tensor_tensor(tmp, view(ps, b, (64, 6), (1, 64)), gam, MUL), read("vector", "KS", tag, 1))
                            if d == 0:
                                step(V.tensor_copy(o, view(R, GR, (1, 384))))
                            else:
                                tt(o, o, view(R, GR, (1, 384)), ADD)
                        b = full(dve, "PU", tag, n)
                        if d == 0 and n == 0:
                            say(V.tensor_copy(o, view(ps, b, (1, 384))), read("vector", "PU", tag, n))
                        else:
                            say(V.tensor_tensor(o, view(ps, b, (1, 384)), o, ADD), read("vector", "PU", tag, n))
                v = view(R, GO, (1, 768))
                tt(view(R, GR, (1, 768)), v, v, MUL)
                step(V.tensor_reduce(view(sm, SS, (1, 12)), view(R, GR, (64, 12), (1, 64)), AX.X, ADD))
                signal("gdn_ss_ready", L)
                dve.wait_ge(*at("rwkv_exp_ready", L))

                def rwkv_factors(d, ct):
                    o = d * 512 + ct * S
                    q = d * 1024 + ct * 512
                    kk = view(R, RKX + ct * S, (1, S))
                    go(V.tensor_tensor(view(R, RAR + q, (1, S)), kk, view(R, RCL + o, (1, S)), MUL))
                    go(V.tensor_tensor(view(R, RAR + q + 256, (1, S)), view(hn, RF + ct * S, (1, S)), view(R, REP + o, (1, S)), MUL))
                    go(V.tensor_tensor(view(R, RBK + q, (1, S)), kk, view(R, RSA + o, (1, S)), MUL))
                    tt(view(R, RBK + q + 256, (1, S)), view(R, RKM + o, (1, S)), view(R, RCM + o, (1, S)), MUL)
                    tt(view(R, RBK + q, (1, S)), view(R, RBK + q, (1, S)), view(R, RCM + o, (1, S)), MUL)
                rwkv_factors(0, 0)
                dve.wait_ge(*at("gdn_rstd_ready", L))
                tt(view(R, GO, (64, 12), (1, 64)), view(R, GO, (64, 12), (1, 64)), view(sm, SS, (1, 12), (0, 64)), MUL)
                for t in range(T):
                    tt(view(R, MIXB + t * D, (64, 6), (1, 64)), view(R, GO + t * 384, (64, 6), (1, 64)),
                       view(rows, R_GN + 64 * (L - 2), (0, 6), (1, 64)), MUL)
                rwkv_factors(0, 1)
                signal("rwkv_factors_ready", L, 0)
                for ct in range(2):
                    rwkv_factors(1, ct)
                signal("rwkv_factors_ready", L, 1)
                b = full(dve, "bonus", L)
                say(V.tensor_copy(view(sm, BN, (1, 8)), view(ps, b, (1, 8))), read("vector", "bonus", L))
                for d in range(2):
                    tag = ("r", L, d)
                    for s in range(8):
                        b = full(dve, "M4", tag, s)
                        say(V.tensor_tensor(view(R, RM4 + s * 512, (256, 2), (1, 256)), view(ps, b, (256, 2), (1, 256)),
                                            view(cst, C_SI + 2 * d * P, (0, 2), (1, 256)), MUL), read("vector", "M4", tag, s))
                        if s == 3 and d == 0:
                            for t in range(T):
                                v = view(R, MIXB + t * D, (1, 768))
                                go(V.tensor_tensor(v, v, view(R, GATE + t * D, (1, 768)), MUL))
                    invert(tag, d, 2, (RM4, 512), "r")
                    for n, c in enumerate((0, 1) if d == 0 else (1, 0)):
                        o = view(R, RY + c * 256, (1, 256))
                        b = full(dve, "Yr", tag, n)
                        if d == 0:
                            say(V.tensor_copy(o, view(ps, b, (1, 256))), read("vector", "Yr", tag, n))
                        else:
                            say(V.tensor_tensor(o, view(ps, b, (1, 256)), o, ADD), read("vector", "Yr", tag, n))
                        if n == 0:
                            b = full(dve, "T0", tag)
                            for hf in range(2):
                                half = dict(p0=64 * hf, np_=64)
                                ins = V.tensor_tensor(view(hnT, RT0 + 64 * hf, (P, 2), (1, 64), **half), view(ps, b, (64, 2), (1, 64), **half),
                                                      view(sm, RE + 2 * d, (1, 2), (0, 64), **half), MUL)
                                if hf == 0:
                                    step(ins)
                                else:
                                    say(ins, read("vector", "T0", tag))
                y8 = view(R, RY, (64, 8), (1, 64))
                step(V.tensor_reduce(view(sm, YM, (1, 8)), y8, AX.X, ADD))
                ts(view(sm, YM, (1, 8)), view(sm, YM, (1, 8)), 1.0 / 64, None, MUL)
                tt(y8, y8, view(sm, YM, (1, 8), (0, 64)), SUB)
                tt(view(R, RYY, (1, 512)), view(R, RY, (1, 512)), view(R, RY, (1, 512)), MUL)
                step(V.tensor_reduce(view(sm, SS, (1, 8)), view(R, RYY, (64, 8), (1, 64)), AX.X, ADD))
                signal("rwkv_var_ready", L)
                tt(view(R, RVN, (64, 8), (1, 64)), view(R, RVN, (64, 8), (1, 64)), view(sm, BN, (1, 8), (0, 64)), MUL)
                tt(view(R, RVN, (256, 2), (1, 256)), view(R, RVN, (256, 2), (1, 256)),
                   view(rows, R_LNB + 256 * (L - 2), (0, 2), (1, 256)), ADD)
                dve.wait_ge(*at("rwkv_rstd_ready", L))
                tt(y8, y8, view(sm, SS, (1, 8), (0, 64)), MUL)
                for t in range(T):
                    yv = view(R, RY + t * 256, (1, 256))
                    tt(yv, yv, view(rows, R_LNG + 256 * (L - 2), (1, 256)), MUL)
                    tt(yv, yv, view(R, RVN + t * 256, (1, 256)), ADD)
                    tt(view(R, MIXB + t * D + 768, (1, 256)), yv, view(R, GATE + t * D + 768, (1, 256)), MUL)
                    signal("mix_ready", L, t)
                residual("o", L, "mix" if L == 2 else "fin", L + 1)
            for t in range(T):
                dve.wait_ge(*at("hn_ready", "fin", 4, t))
                dve.wait_ge(*at("final_gain_in", 0))
                v = view(hn, t * D, (1, D))
                tt(v, v, view(rows, R_FIN, (1, D)), MUL)
                signal("result_ready", t)

    return dict(C.table, bank_of=new_bank, reader=new_reader, freed_by=new_freed)


def kernel(**inputs):
    import concourse.bacc as _bacc
    from concourse.bass_utils import run_bass_kernel_spmd as _run

    masks, buckets = shape_constants()
    arrays = {}
    for name in _INS:
        arrays[f"in_{name}"] = np.ascontiguousarray(inputs[name])
    arrays["in_const_masks"] = masks
    arrays["in_const_buckets"] = buckets

    def build(known):
        nc = _bacc.Bacc("TRN2", target_bir_lowering=False, num_devices=1)
        a = {n[3:]: nc.dram_tensor(n, v.shape, mybir.dt.from_np(v.dtype), kind="ExternalInput").ap() for n, v in arrays.items()}
        out = nc.dram_tensor("out", (1, S, D), F32, kind="ExternalOutput").ap()
        return nc, program(nc, a, out, known)

    _, known = build(None)
    nc, _ = build(known)
    r = _run(nc, [arrays], core_ids=[0])
    return r.results[0]["out"]
```
